# Optimizing a Trainium2 kernel written in Bass

```python
import jax
import jax.numpy as jnp
from jax import lax
import numpy as np

D_MODEL = 1024
BATCH = 1
SEQ = 1024
DEPTH = 1

LRU_WIDTH = D_MODEL
LRU_BLOCK_W = 256
LRU_BLOCKS = LRU_WIDTH // LRU_BLOCK_W
CONV_W = 4
LRU_C = 8.0
N_HEADS = 8
HEAD_DIM = D_MODEL // N_HEADS
ATTN_WIDTH = N_HEADS * HEAD_DIM
Q_BLOCK = 128
N_GROUPS = 4
EXPERTS_PER_GROUP = 8
N_EXPERTS = N_GROUPS * EXPERTS_PER_GROUP
TOP_K = 2
D_EXPERT = D_MODEL // 2
ROUTE_BLOCK = 128
EPS = 1e-6
IN_WIDTHS = (LRU_WIDTH, LRU_WIDTH, ATTN_WIDTH, ATTN_WIDTH, ATTN_WIDTH, N_HEADS, D_MODEL, D_MODEL)
IN_WIDTH = sum(IN_WIDTHS)

kernel_name = 'hybrid_rglru_fox_hmoe'

def rms_norm(x, g):
    x32 = x.astype(jnp.float32)
    y = x32 * lax.rsqrt(jnp.mean(x32 * x32, axis=-1, keepdims=True) + EPS)
    return (y * g.astype(jnp.float32)).astype(x.dtype)

def causal_depthwise_conv(x, w, b):
    y = lax.conv_general_dilated(
        x, w[:, None, :].astype(x.dtype), window_strides=(1,),
        padding=[(CONV_W - 1, 0)], dimension_numbers=('NWC', 'WIO', 'NWC'),
        feature_group_count=x.shape[-1])
    return y + b.astype(x.dtype)

def _linear_recurrence_combine(e1, e2):
    a1, b1 = e1
    a2, b2 = e2
    return a1 * a2, a2 * b1 + b2

def rg_lru(xc, w_a, b_a, w_x, b_x, lam):
    B, S, C = xc.shape
    xb = xc.reshape(B, S, LRU_BLOCKS, LRU_BLOCK_W)
    r = jax.nn.sigmoid(jnp.einsum('bsnc,ncd->bsnd', xb, w_a).reshape(B, S, C).astype(jnp.float32) + b_a.astype(jnp.float32))
    i = jax.nn.sigmoid(jnp.einsum('bsnc,ncd->bsnd', xb, w_x).reshape(B, S, C).astype(jnp.float32) + b_x.astype(jnp.float32))
    log_a = -LRU_C * r * jax.nn.softplus(-lam.astype(jnp.float32))
    a = jnp.exp(log_a)
    mult = jnp.sqrt(-jnp.expm1(2.0 * log_a))
    b = mult * i * xc.astype(jnp.float32)
    _, h = lax.associative_scan(_linear_recurrence_combine, (a, b), axis=1)
    return h.astype(xc.dtype)

def forgetting_attention(q, k, v, log_f):
    B, S, H, Dh = q.shape
    scale = Dh ** -0.5
    c = jnp.cumsum(log_f, axis=1).transpose(0, 2, 1)
    outs = []
    for qb in range(S // Q_BLOCK):
        lo = qb * Q_BLOCK
        hi = lo + Q_BLOCK
        s = jnp.einsum('bqhd,bkhd->bhqk', q[:, lo:hi], k[:, :hi], preferred_element_type=jnp.float32) * scale
        s = s + c[:, :, lo:hi, None] - c[:, :, None, :hi]
        causal = jnp.arange(hi)[None, :] <= (lo + jnp.arange(Q_BLOCK))[:, None]
        s = jnp.where(causal, s, -jnp.inf)
        p = jax.nn.softmax(s, axis=-1)
        outs.append(jnp.einsum('bhqk,bkhd->bqhd', p.astype(v.dtype), v[:, :hi]))
    return jnp.concatenate(outs, axis=1).reshape(B, S, H * Dh)

def parallel_mixer(u, w_in, conv_w, conv_b, w_rg_a, b_rg_a, w_rg_x, b_rg_x, lam, b_forget,
                   w_lru_out, w_attn_out, w_out):
    B, S, _ = u.shape
    z = u @ w_in
    split_points = np.cumsum(IN_WIDTHS)[:-1].tolist()
    xr, gr, q, k, v, fl, m_lru, m_attn = jnp.split(z, split_points, axis=-1)
    h = rg_lru(causal_depthwise_conv(xr, conv_w, conv_b), w_rg_a, b_rg_a, w_rg_x, b_rg_x, lam)
    y_lru = (h * jax.nn.gelu(gr)) @ w_lru_out
    log_f = jax.nn.log_sigmoid(fl.astype(jnp.float32) + b_forget.astype(jnp.float32))
    o = forgetting_attention(q.reshape(B, S, N_HEADS, HEAD_DIM), k.reshape(B, S, N_HEADS, HEAD_DIM),
                             v.reshape(B, S, N_HEADS, HEAD_DIM), log_f)
    y_attn = o @ w_attn_out
    merged = jax.nn.sigmoid(m_lru) * y_lru + jax.nn.sigmoid(m_attn) * y_attn
    return merged @ w_out

def hierarchical_moe(xn, w_rg, b_rg, w_re, b_re, w1, w3, w2):
    B, S, D = xn.shape
    T = B * S
    xt = xn.reshape(T, D)
    g_logits = (xt @ w_rg).astype(jnp.float32) + b_rg.astype(jnp.float32)
    g_prob = jax.nn.softmax(g_logits, axis=-1)
    _, g_sel = lax.top_k(g_logits, 1)
    p_group = jnp.take_along_axis(g_prob, g_sel, axis=1)
    e_logits = ((xt @ w_re).astype(jnp.float32) + b_re.astype(jnp.float32)).reshape(T, N_GROUPS, EXPERTS_PER_GROUP)
    e_in_group = jnp.take_along_axis(e_logits, g_sel[:, :, None], axis=1)[:, 0]
    top_v, top_i = lax.top_k(e_in_group, TOP_K)
    comb_w = p_group * jax.nn.softmax(top_v, axis=-1)
    expert = g_sel * EXPERTS_PER_GROUP + top_i
    N = T * TOP_K
    flat_e = expert.reshape(N)
    flat_w = comb_w.reshape(N)
    flat_t = jnp.arange(N) // TOP_K
    order = jnp.argsort(flat_e, stable=True)
    sorted_e = flat_e[order]
    counts = jnp.bincount(flat_e, length=N_EXPERTS)
    padded = ((counts + ROUTE_BLOCK - 1) // ROUTE_BLOCK) * ROUTE_BLOCK
    pad_end = jnp.cumsum(padded)
    pad_start = pad_end - padded
    seg_start = jnp.cumsum(counts) - counts
    dest = pad_start[sorted_e] + jnp.arange(N) - seg_start[sorted_e]
    n_blocks = (N + N_EXPERTS * (ROUTE_BLOCK - 1) + ROUTE_BLOCK - 1) // ROUTE_BLOCK
    P = n_blocks * ROUTE_BLOCK
    slot_tok = jnp.full((P,), T, dtype=jnp.int32).at[dest].set(flat_t[order].astype(jnp.int32))
    slot_w = jnp.zeros((P,), xn.dtype).at[dest].set(flat_w[order].astype(xn.dtype))
    blk_expert = jnp.minimum(jnp.searchsorted(pad_end, jnp.arange(n_blocks) * ROUTE_BLOCK, side='right'), N_EXPERTS - 1)
    x_pad = jnp.concatenate([xt, jnp.zeros((1, D), xt.dtype)], axis=0)

    def expert_block(args):
        tok, e = args
        xb = x_pad[tok]
        hb = jax.nn.silu(xb @ w1[e]) * (xb @ w3[e])
        return hb @ w2[e]

    y = lax.map(expert_block, (slot_tok.reshape(n_blocks, ROUTE_BLOCK), blk_expert)).reshape(P, D)
    out = jnp.zeros((T + 1, D), xn.dtype).at[slot_tok].add(y * slot_w[:, None])[:T]
    return out.reshape(B, S, D)

def setup_inputs(seed: int = 0) -> dict:
    key = jax.random.key(seed)
    ks = jax.random.split(key, 23)
    f32 = jnp.float32

    def nrm(k, shape, fan_in):
        return jax.random.normal(k, shape, f32) * (fan_in ** -0.5)

    u = jax.random.uniform(ks[9], (DEPTH, LRU_WIDTH), f32, minval=0.9, maxval=0.999)
    a0 = u ** (1.0 / LRU_C)
    return {
        'x': jax.random.normal(ks[0], (BATCH, SEQ, D_MODEL), f32),
        'g_mix': 1.0 + 0.05 * jax.random.normal(ks[1], (DEPTH, D_MODEL), f32),
        'w_in': nrm(ks[2], (DEPTH, D_MODEL, IN_WIDTH), D_MODEL),
        'conv_w': nrm(ks[3], (DEPTH, CONV_W, LRU_WIDTH), CONV_W),
        'conv_b': 0.02 * jax.random.normal(ks[4], (DEPTH, LRU_WIDTH), f32),
        'w_rg_a': nrm(ks[5], (DEPTH, LRU_BLOCKS, LRU_BLOCK_W, LRU_BLOCK_W), LRU_BLOCK_W),
        'b_rg_a': 0.02 * jax.random.normal(ks[6], (DEPTH, LRU_WIDTH), f32),
        'w_rg_x': nrm(ks[7], (DEPTH, LRU_BLOCKS, LRU_BLOCK_W, LRU_BLOCK_W), LRU_BLOCK_W),
        'b_rg_x': 0.02 * jax.random.normal(ks[8], (DEPTH, LRU_WIDTH), f32),
        'lru_lambda': jnp.log(a0) - jnp.log1p(-a0),
        'b_forget': 2.0 + 0.1 * jax.random.normal(ks[10], (DEPTH, N_HEADS), f32),
        'w_lru_out': nrm(ks[11], (DEPTH, LRU_WIDTH, D_MODEL), LRU_WIDTH),
        'w_attn_out': nrm(ks[12], (DEPTH, ATTN_WIDTH, D_MODEL), ATTN_WIDTH),
        'w_out': nrm(ks[13], (DEPTH, D_MODEL, D_MODEL), D_MODEL),
        'g_ffn': 1.0 + 0.05 * jax.random.normal(ks[14], (DEPTH, D_MODEL), f32),
        'w_route_group': nrm(ks[15], (DEPTH, D_MODEL, N_GROUPS), D_MODEL),
        'b_route_group': 0.01 * jax.random.normal(ks[16], (DEPTH, N_GROUPS), f32),
        'w_route_expert': nrm(ks[17], (DEPTH, D_MODEL, N_EXPERTS), D_MODEL),
        'b_route_expert': 0.01 * jax.random.normal(ks[18], (DEPTH, N_EXPERTS), f32),
        'w_exp_gate': nrm(ks[19], (DEPTH, N_EXPERTS, D_MODEL, D_EXPERT), D_MODEL),
        'w_exp_up': nrm(ks[20], (DEPTH, N_EXPERTS, D_MODEL, D_EXPERT), D_MODEL),
        'w_exp_down': nrm(ks[21], (DEPTH, N_EXPERTS, D_EXPERT, D_MODEL), D_EXPERT),
        'g_final': 1.0 + 0.05 * jax.random.normal(ks[22], (D_MODEL,), f32),
    }

def reference(x, g_mix, w_in, conv_w, conv_b, w_rg_a, b_rg_a, w_rg_x, b_rg_x, lru_lambda, b_forget,
              w_lru_out, w_attn_out, w_out, g_ffn, w_route_group, b_route_group, w_route_expert,
              b_route_expert, w_exp_gate, w_exp_up, w_exp_down, g_final):
    for l in range(DEPTH):
        u = rms_norm(x, g_mix[l])
        x = x + parallel_mixer(u, w_in[l], conv_w[l], conv_b[l], w_rg_a[l], b_rg_a[l], w_rg_x[l], b_rg_x[l],
                               lru_lambda[l], b_forget[l], w_lru_out[l], w_attn_out[l], w_out[l])
        v = rms_norm(x, g_ffn[l])
        x = x + hierarchical_moe(v, w_route_group[l], b_route_group[l], w_route_expert[l], b_route_expert[l],
                                 w_exp_gate[l], w_exp_up[l], w_exp_down[l])
    return rms_norm(x, g_final)


_drawn_inputs = setup_inputs


def setup_inputs(seed=0):
    import zlib

    import numpy as np

    out = dict(_drawn_inputs(seed))
    spreads = {}
    factors = {'b_rg_a': 24.215,
     'b_rg_x': 7.984,
     'b_forget': 120.216,
     'b_route_group': 5.589,
     'b_route_expert': 3.73}
    for name, (base, spread) in spreads.items():
        noise = np.random.default_rng([zlib.crc32(name.encode()), seed]).standard_normal(out[name].shape)
        drawn = base * np.exp(spread * noise) if base else spread * noise
        out[name] = jnp.asarray(drawn.astype(out[name].dtype))
    for name, factor in factors.items():
        out[name] = (out[name] * factor).astype(out[name].dtype)
    return out
```

```python
import concourse.bass as bass
from concourse import mybir

F32 = mybir.dt.float32
F32R = mybir.dt.float32r
I32 = mybir.dt.int32
U32 = mybir.dt.uint32
ALU = mybir.AluOpType
ACT = mybir.ActivationFunctionType
AX = mybir.AxisListType

P = 128
D = 1024
T = 1024
KD = D // P
NT = T // P
HALF = 512
NH = 8
HD = D // NH
WB = 256
CONV_W = 4
LRU_C = 8.0
EPS = 1e-6
NG = 4
EG = 8
NE = NG * EG
FE = 512
XR, GR, QC, KC, VC, FL, ML, MA = 0, D, 2 * D, 3 * D, 4 * D, 5 * D, 5 * D + NH, 6 * D + NH
NEG = -3.0e38
PW, PB, PBA, PBX, PS, NPRM = 0, 4, 5, 6, 7, 8
BLK = 128
MAXX = 2 * T // BLK
SLOTS = (NE + MAXX) * BLK


class Map:

    def __init__(self, nc, start, end):
        self.nc, self.at, self.end = nc, start, end

    def put(self, name, shape, dt=F32):
        size = 4
        for n in shape[1:]:
            size *= n
        place = self.nc.alloc_sbuf_tensor_at(name, shape, dt, offset=self.at)
        self.at += (size + 31) // 32 * 32
        assert self.at <= self.end, (name, self.at, self.end)
        return place


class Steps:

    def __init__(self, engine, sem, start=0):
        self.engine, self.sem, self.start, self.n = engine, sem, start, 0

    def did(self, instruction):
        instruction.then_inc(self.sem, 1)
        self.n += 1
        self.engine.wait_ge(self.sem, self.start + self.n)


class Kernel:
    def __init__(self, nc, ins, out):
        self.nc, self.out = nc, out
        self.x, self.g_mix, self.w_in = ins["x"][0], ins["g_mix"][0], ins["w_in"][0]
        self.ins = ins
        dram = lambda name, shape, dt=F32: nc.dram_tensor(name, shape, dt).ap()
        self.qk_d = dram("qk_d", (NH, P, 4, T))
        self.v_d = dram("v_d", (NH // 2, 2, P, NT, WB))
        self.sig_d = dram("sig_d", (2, KD, P, T))
        self.c_d = dram("c_d", (NH, T))
        self.o_d = dram("o_d", (NH, P, T))
        self.xn_d = dram("xn_d", (T, D))
        self.slots_d = dram("slots_d", (SLOTS + BLK, 1), I32)
        self.y_d = dram("y_d", (SLOTS, D))
        self.stage_sems = []
        low, high = (nc.SBUF_PARTITION_SIZE_BYTES - nc.sbuf_bytes_remaining + 31) // 32 * 32, nc.sbuf_usable_end
        fixed = Map(nc, low, high)
        self.ident = fixed.put("ident", [P, P])
        self.ones = fixed.put("ones", [P, P])
        self.zeros_at = fixed.at
        self.zeros = fixed.put("zeros", [P, P])
        self.tri = fixed.put("tri", [P, P])
        self.stri = fixed.put("stri", [P, P])
        self.gm = fixed.put("gm", [P, KD])
        self.prm = fixed.put("prm", [P, KD, NPRM])
        self.f_log = fixed.put("f_log", [P, NT, NH])
        self.c_tok = fixed.put("c_tok", [P, NT, NH])
        self.wgt = fixed.put("wgt", [P, 2, NT])
        self.dest = fixed.put("dest", [P, 2, NT], I32)
        self.blocks = fixed.put("blocks", [1, 32], I32)
        mixer = Map(nc, fixed.at, high)
        self.w_raw = [mixer.put(f"w_raw{s}", [P, KD, WB]) for s in range(2)]
        self.w_h = [mixer.put(f"w_h{s}", [P, KD, WB], F32R) for s in range(2)]
        self.w_l = [mixer.put(f"w_l{s}", [P, KD, WB], F32R) for s in range(2)]
        self.act_start, self.high, self.fixed_end = mixer.at, high, fixed.at
        self.uh = mixer.put("uh", [P, KD, T], F32R)
        self.ul = mixer.put("ul", [P, KD, T], F32R)
        self.mix = mixer.put("mix", [P, KD, T])
        self.work_start = mixer.at
        self.w_loaded = [self.sem(f"w_loaded{s}") for s in range(2)]
        self.w_hi = [self.sem(f"w_hi{s}") for s in range(2)]
        self.w_lo = [self.sem(f"w_lo{s}") for s in range(2)]
        self.w_first = [self.sem(f"w_first{s}") for s in range(2)]
        self.w_used = [self.sem(f"w_used{s}") for s in range(2)]
        self.pairs = 0
        self.e_in = [self.sem(f"e_in{r}") for r in range(6)]
        self.e_hi, self.e_lo, self.e_used = ([self.sem(f"e_{n}{s}") for s in range(3)] for n in ("hi", "lo", "used"))
        self.ps = [nc.alloc_psum_tensor(f"ps{t}", [P, 2 * HALF], F32) for t in range(4)]

    def sem(self, name):
        self.stage_sems.append(self.nc.alloc_semaphore(name))
        return self.stage_sems[-1]

    def stage(self, write, *args):
        self.stage_sems = []
        write(*args)
        self.nc.clear_and_free_semaphores(self.stage_sems)
        self.nc.all_engine_barrier(sem_only=True)

    def work(self):
        return Map(self.nc, self.work_start, self.high)

    def load_block(self, eng, s, p, src):
        eng.wait_ge(self.w_lo[s], p)
        eng.dma_start(self.w_raw[s][:, :, :], src).then_inc(self.w_loaded[s], 16)

    def split_hi(self, act, s, p):
        act.wait_ge(self.w_loaded[s], 16 * (p + 1))
        act.wait_ge(self.w_used[s], p)
        act.activation(self.w_h[s][:, :, :], self.w_raw[s][:, :, :], ACT.Copy).then_inc(self.w_hi[s], 1)

    def split_lo(self, dve, s, p):
        dve.wait_ge(self.w_hi[s], p + 1)
        dve.tensor_tensor(self.w_l[s][:, :, :], self.w_raw[s][:, :, :], self.w_h[s][:, :, :].bitcast(F32),
                          ALU.subtract).then_inc(self.w_lo[s], 1)

    def w_block(self, w, col):
        return w.rearrange("(k p) n -> p k n", p=P)[:, :, bass.ds(col, WB)]

    def product(self, pe, ps, s, c):
        wh, wl = (w[s][:, :, c * P:(c + 1) * P] for w in (self.w_h, self.w_l))
        for k in range(KD):
            for w, u, first, last in ((wh, self.uh, k == 0, False), (wh, self.ul, False, False),
                                      (wl, self.uh, False, k == KD - 1)):
                for h in range(2):
                    mm = pe.matmul(ps[:, h * HALF:(h + 1) * HALF], w[:, k, :], u[:, k, h * HALF:(h + 1) * HALF],
                                   start=first, stop=last)
        return mm

    def product_rows(self, pe, ps, s, tile):
        rows = slice(tile * P, (tile + 1) * P)
        for k in range(KD):
            for u, w, first, last in ((self.uh, self.w_h, k == 0, False), (self.uh, self.w_l, False, False),
                                      (self.ul, self.w_h, False, k == KD - 1)):
                mm = pe.matmul(ps, u[:, k, rows], w[s][:, k, :], start=first, stop=last)
        return mm

    def norm_in(self):
        nc, k_ = self.nc, self
        work = self.work()
        square = work.put("na_square", [P, D])
        total = work.put("na_total", [P, NT])
        mean = work.put("na_mean", [P, NT])
        rstd = work.put("na_rstd", [P, NT])
        power = work.put("na_power", [P, NT])
        rows = work.put("na_rows", [P, P])
        e, w1, dw, ln, eq = (work.put(f"na_{n}", [P, KD]) for n in ("e", "w1", "dw", "ln", "eq"))
        x_loaded = [self.sem(f"na_x{t}") for t in range(NT)]
        prm_loaded, prm_mm, prm_turned = self.sem("na_prm"), self.sem("na_prm_mm"), self.sem("na_prm_turned")
        consts = self.sem("na_consts")
        squared, averaged, powered, scaled = (self.sem(f"na_{n}") for n in ("squared", "averaged", "powered", "scaled"))
        turned, high, low = self.sem("na_turned"), self.sem("na_high"), self.sem("na_low")
        sp_exp, sp_one, sp_ln, own = (self.sem(f"na_{n}") for n in ("sp_exp", "sp_one", "sp_ln", "own"))
        xt = self.mix
        ins = self.ins
        vectors = [ins["conv_w"][0, j] for j in range(CONV_W)] + \
                  [ins[n][0] for n in ("conv_b", "b_rg_a", "b_rg_x", "lru_lambda", "g_mix")]
        turn = k_.ps[3][:, HALF:HALF + P]
        turn_v = turn.rearrange("p (v k) -> p k v", k=KD)

        with nc.Block() as block:
            @block.sync
            def _(sp):
                for t in range(NT):
                    sp.dma_start(xt[:, t, :], k_.x[t * P:(t + 1) * P, :]).then_inc(x_loaded[t], 16)
                for s, col in enumerate((XR, GR)):
                    k_.load_block(sp, s, 0, k_.w_block(k_.w_in, col))

            @block.scalar
            def _(act):
                act.wait_ge(consts, 3)
                for v, src in enumerate(vectors):
                    act.dma_start(rows[v * KD:(v + 1) * KD, :], src.rearrange("(k p) -> k p", p=P))\
                        .then_inc(prm_loaded, 16)
                for t in range(NT):
                    act.wait_ge(x_loaded[t], 16)
                    act.activation(square[:, :], xt[:, t, :], ACT.Square,
                                   accum_out=total[:, t:t + 1]).then_inc(squared, 1)
                    act.wait_ge(squared, t + 1)
                act.wait_ge(prm_turned, 2)
                act.activation(e[:, :], k_.prm[:, :, PS], ACT.Exp, scale=-1.0).then_inc(sp_exp, 1)
                act.wait_ge(sp_one, 1)
                act.activation(ln[:, :], w1[:, :], ACT.Ln).then_inc(sp_ln, 1)
                k_.split_hi(act, 0, 0)
                k_.split_hi(act, 1, 0)
                for h in range(2):
                    for k in range(KD):
                        act.wait_ge(turned, h * KD + k + 1)
                        act.activation(k_.uh[:, k, h * HALF:(h + 1) * HALF], k_.ps[k % 4][:, 0:HALF], ACT.Copy,
                                       scale=k_.gm[:, k:k + 1]).then_inc(high, 1)

            @block.gpsimd
            def _(pool):
                pool.memset(power[:, :], -0.5).then_inc(consts, 1)
                pool.memset(k_.ones[:, :], 1.0).then_inc(consts, 1)
                pool.memset(rows[:, :], 0.0).then_inc(consts, 1)
                pool.wait_ge(consts, 3)
                pool.affine_select(out=k_.ident[:, :], in_=k_.ones[:, :], compare_op=ALU.is_equal, fill=0.0,
                                   base=0, pattern=[[-1, P]], channel_multiplier=1).then_inc(consts, 1)
                pool.affine_select(out=k_.tri[:, :], in_=k_.ones[:, :], compare_op=ALU.is_ge, fill=0.0,
                                   base=0, pattern=[[1, P]], channel_multiplier=-1).then_inc(consts, 1)
                pool.affine_select(out=k_.stri[:, :], in_=k_.ones[:, :], compare_op=ALU.is_gt, fill=0.0,
                                   base=0, pattern=[[1, P]], channel_multiplier=-1).then_inc(consts, 1)
                pool.wait_ge(averaged, 1)
                pool.tensor_tensor(rstd[:, :], mean[:, :], power[:, :], ALU.pow).then_inc(powered, 1)

            @block.tensor
            def _(pe):
                pe.wait_ge(consts, 6)
                pe.wait_ge(prm_loaded, 16 * len(vectors))
                pe.transpose(turn, rows[:, :], k_.ident[:, :]).then_inc(prm_mm, 1)
                for h in range(2):
                    pe.wait_ge(scaled, 4 * h + 4)
                    for k in range(KD):
                        n = h * KD + k
                        if n >= 4:
                            pe.wait_ge(low, n - 3)
                        for t in range(4):
                            mm = pe.transpose(k_.ps[k % 4][:, t * P:(t + 1) * P],
                                              xt[:, 4 * h + t, k * P:(k + 1) * P], k_.ident[:, :])
                        mm.then_inc(turned, 1)

            @block.vector
            def _(dve):
                steps = Steps(dve, own)
                dve.wait_ge(prm_mm, 1)
                dve.tensor_copy(k_.prm[:, :, :], turn_v[:, :, 0:NPRM]).then_inc(prm_turned, 1)
                dve.tensor_copy(k_.gm[:, :], turn[:, NPRM * KD:(NPRM + 1) * KD]).then_inc(prm_turned, 1)
                dve.wait_ge(sp_exp, 1)
                dve.tensor_scalar(w1[:, :], e[:, :], 1.0, None, ALU.add).then_inc(sp_one, 1)
                dve.wait_ge(sp_one, 1)
                steps.did(dve.tensor_scalar(dw[:, :], w1[:, :], -1.0, None, ALU.add))
                steps.did(dve.tensor_scalar(eq[:, :], dw[:, :], 0.0, None, ALU.is_equal))
                steps.did(dve.tensor_tensor(dw[:, :], dw[:, :], eq[:, :], ALU.add))
                steps.did(dve.reciprocal(dw[:, :], dw[:, :]))
                dve.wait_ge(sp_ln, 1)
                steps.did(dve.tensor_tensor(eq[:, :], eq[:, :], ln[:, :], ALU.add))
                steps.did(dve.tensor_tensor(eq[:, :], eq[:, :], dw[:, :], ALU.mult))
                steps.did(dve.tensor_tensor(eq[:, :], eq[:, :], e[:, :], ALU.mult))
                dve.tensor_scalar(k_.prm[:, :, PS], eq[:, :], LRU_C / 2, None, ALU.mult).then_inc(own, 1)
                dve.wait_ge(squared, NT)
                dve.tensor_scalar(mean[:, :], total[:, :], 1.0 / D, EPS, ALU.mult, ALU.add).then_inc(averaged, 1)
                k_.split_lo(dve, 0, 0)
                k_.split_lo(dve, 1, 0)
                dve.wait_ge(powered, 1)
                for t in range(NT):
                    dve.tensor_scalar(xt[:, t, :], xt[:, t, :], rstd[:, t:t + 1], None, ALU.mult).then_inc(scaled, 1)
                for h in range(2):
                    for k in range(KD):
                        dve.wait_ge(high, h * KD + k + 1)
                        dve.scalar_tensor_tensor(out=k_.ul[:, k, h * HALF:(h + 1) * HALF],
                                                 in0=k_.ps[k % 4][:, 0:HALF], scalar=k_.gm[:, k:k + 1],
                                                 in1=k_.uh[:, k, h * HALF:(h + 1) * HALF].bitcast(F32),
                                                 op0=ALU.mult, op1=ALU.subtract).then_inc(low, 1)

    def lru(self):
        nc, k_ = self.nc, self
        n_pairs = D // WB
        p0, self.pairs = self.pairs, self.pairs + n_pairs
        work = self.work()
        rg_raw = work.put("rg_raw", [P, 2, 2, WB])
        rg_h = work.put("rg_h", [P, 2, 2, WB], F32R)
        rg_l = work.put("rg_l", [P, 2, 2, WB], F32R)
        cur = work.put("lru_prm", [P, 2, NPRM])
        pad = CONV_W - 1
        xr = work.put("lru_xr", [P, 2, T + 8])
        xc = work.put("lru_xc", [P, 2, T])
        xc_h = work.put("lru_xch", [P, 2, T], F32R)
        xc_l = work.put("lru_xcl", [P, 2, T], F32R)
        root_at = work.at - 2 * (2 * T * 4)
        rt_sb = Map(nc, root_at, work.at).put("lru_rt", [P, 2, T])
        t_sb = work.put("lru_t", [P, 2, T])
        i_sb = xr[:, :, pad:pad + T]
        gl = work.put("lru_gl", [P, 2, T])
        sem = self.sem
        rg_loaded, rg_hi, rg_lo, rg_used = (sem(f"rg_{n}") for n in ("loaded", "hi", "lo", "used"))
        xr_out = [sem(f"lru_xr_out{c}") for c in range(2)]
        gr_out = [sem(f"lru_gr_out{c}") for c in range(2)]
        conv, xch_done, xcl_done = (sem(f"lru_{n}") for n in ("conv", "xch", "xcl"))
        gate_mm = [sem(f"lru_gate_mm{g}") for g in range(2)]
        gate_out = [sem(f"lru_gate_out{g}") for g in range(2)]
        t_done, root, mixed, own = (sem(f"lru_{n}") for n in ("t", "root", "mixed", "own"))
        w_a, w_x = (self.ins[n][0].rearrange("b (c p) n -> b p c n", p=P) for n in ("w_rg_a", "w_rg_x"))
        zeroed, cleared, filled = sem("lru_zeroed"), sem("lru_cleared"), sem("lru_filled")
        zeros = self.zeros

        with nc.Block() as block:
            @block.sync
            def _(sp):
                def gates(i):
                    sp.wait_ge(rg_lo, i)
                    for g, w in enumerate((w_a, w_x)):
                        sp.dma_start(rg_raw[:, g, :, :], w[i]).then_inc(rg_loaded, 16)
                gates(0)
                with sp.Fori(1, n_pairs) as i:
                    for s, col in enumerate((XR, GR)):
                        k_.load_block(sp, s, p0 + i, k_.w_block(k_.w_in, col + WB * i))
                    gates(i)
                for s, col in enumerate((QC, KC)):
                    k_.load_block(sp, s, p0 + n_pairs, k_.w_block(k_.w_in, col))

            @block.gpsimd
            def _(pool):
                pool.memset(xr[:, :, 0:pad], 0.0).then_inc(zeroed, 1)
                pool.memset(zeros[:, :], 0.0).then_inc(cleared, 1)
                pool.wait_ge(cleared, 1)
                with pool.Fori(0, MAXX) as j:
                    pool.dma_start(k_.y_d[bass.ds(NE * BLK + BLK * j, BLK), :].rearrange("p (a n) -> p a n", n=P),
                                   zeros[:, :].unsqueeze(1).to_broadcast([P, D // P, P])).then_inc(filled, 16)
                pool.wait_ge(filled, 16 * MAXX)

            @block.tensor
            def _(pe):
                with pe.Fori(0, n_pairs) as i:
                    for s, out in ((0, gr_out), (1, xr_out)):
                        pe.wait_ge(k_.w_lo[s], p0 + i + 1)
                        for c in range(2):
                            pe.wait_ge(out[c], i + s)
                            k_.product(pe, k_.ps[c], s, c).then_inc((k_.w_first, k_.w_used)[c][s], 1)
                    pe.wait_ge(rg_lo, i + 1)
                    pe.wait_ge(xcl_done, 2 * i + 2)
                    for m in range(2):
                        for g in range(2):
                            pe.wait_ge(gate_out[g], 2 * i + m)
                            for kk in range(2):
                                for w, u, first, last in ((rg_h, xc_h, kk == 0, False), (rg_h, xc_l, False, False),
                                                          (rg_l, xc_h, False, kk == 1)):
                                    for h in range(2):
                                        mm = pe.matmul(k_.ps[2 + g][:, h * HALF:(h + 1) * HALF],
                                                       w[:, g, kk, m * P:(m + 1) * P],
                                                       u[:, kk, h * HALF:(h + 1) * HALF], start=first, stop=last)
                            mm.then_inc(gate_mm[g], 1)

            @block.scalar
            def _(act):
                with act.Fori(0, n_pairs) as i:
                    act.wait_ge(mixed, 2 * i)
                    for c in range(2):
                        act.wait_ge((k_.w_first, k_.w_used)[c][0], p0 + i + 1)
                        act.activation(xr[:, c, pad:pad + T], k_.ps[c][:, :], ACT.Copy).then_inc(xr_out[c], 1)
                    act.wait_ge(rg_loaded, 32 * (i + 1))
                    act.wait_ge(gate_mm[1], 2 * i)
                    act.activation(rg_h[:, :, :, :], rg_raw[:, :, :, :], ACT.Copy).then_inc(rg_hi, 1)
                    k_.split_hi(act, 0, p0 + i + 1)
                    for c in range(2):
                        act.wait_ge(conv, 2 * i + c + 1)
                        act.activation(xc_h[:, c, :], xc[:, c, :], ACT.Copy).then_inc(xch_done, 1)
                    for c in range(2):
                        act.wait_ge((k_.w_first, k_.w_used)[c][1], p0 + i + 1)
                        act.activation(gl[:, c, :], k_.ps[c][:, :], ACT.Gelu_apprx_tanh).then_inc(gr_out[c], 1)
                    k_.split_hi(act, 1, p0 + i + 1)
                    for m in range(2):
                        act.wait_ge(gate_mm[0], 2 * i + m + 1)
                        act.activation(t_sb[:, m, :], k_.ps[2][:, :], ACT.Sigmoid, bias=cur[:, m, PBA:PBA + 1])\
                            .then_inc(gate_out[0], 1)
                        act.wait_ge(gate_mm[1], 2 * i + m + 1)
                        act.activation(i_sb[:, m, :], k_.ps[3][:, :], ACT.Sigmoid, bias=cur[:, m, PBX:PBX + 1])\
                            .then_inc(gate_out[1], 1)
                        act.wait_ge(gate_out[0], 2 * i + m + 1)
                        act.activation(t_sb[:, m, :], t_sb[:, m, :], ACT.Tanh, scale=cur[:, m, PS:PS + 1])\
                            .then_inc(t_done, 1)
                    act.wait_ge(t_done, 2 * i + 2)
                    act.activation(rt_sb[:, :, :], t_sb[:, :, :], ACT.Sqrt).then_inc(root, 1)

            @block.vector
            def _(dve):
                PER = 21
                dve.wait_ge(zeroed, 1)
                with dve.Fori(0, n_pairs) as i:
                    steps = Steps(dve, own, i * PER)
                    dve.wait_ge(t_done, 2 * i)
                    steps.did(dve.tensor_scalar(cur[:, :, :], k_.prm[:, bass.ds(2 * i, 2), :], 1.0, None, ALU.mult))
                    for c in range(2):
                        dve.wait_ge(xr_out[c], i + 1)
                        w = lambda j: cur[:, c, PW + j:PW + j + 1]
                        steps.did(dve.tensor_scalar(xc[:, c, :], xr[:, c, 0:T], w(0), cur[:, c, PB:PB + 1],
                                                    ALU.mult, ALU.add))
                        for j in range(1, CONV_W):
                            op = dve.scalar_tensor_tensor(out=xc[:, c, :], in0=xr[:, c, j:j + T], scalar=w(j),
                                                          in1=xc[:, c, :], op0=ALU.mult, op1=ALU.add)
                            if j < CONV_W - 1:
                                steps.did(op)
                        op.then_inc(conv, 1)
                    dve.wait_ge(rg_hi, i + 1)
                    dve.tensor_tensor(rg_l[:, :, :, :], rg_raw[:, :, :, :], rg_h[:, :, :, :].bitcast(F32),
                                      ALU.subtract).then_inc(rg_lo, 1)
                    for c in range(2):
                        dve.wait_ge(xch_done, 2 * i + c + 1)
                        dve.tensor_tensor(xc_l[:, c, :], xc[:, c, :], xc_h[:, c, :].bitcast(F32),
                                          ALU.subtract).then_inc(xcl_done, 1)
                    k_.split_lo(dve, 0, p0 + i + 1)
                    k_.split_lo(dve, 1, p0 + i + 1)
                    dve.wait_ge(root, i + 1)
                    for m in range(2):
                        t = t_sb[:, m, :]
                        rt = rt_sb[:, m, :]
                        steps.did(dve.tensor_scalar(t, t, 1.0, None, ALU.add))
                        steps.did(dve.reciprocal(t, t))
                        steps.did(dve.tensor_tensor(i_sb[:, m, :], i_sb[:, m, :], xc[:, m, :], ALU.mult))
                        steps.did(dve.scalar_tensor_tensor(out=rt, in0=rt, scalar=2.0, in1=t, op0=ALU.mult, op1=ALU.mult))
                        steps.did(dve.tensor_tensor(i_sb[:, m, :], i_sb[:, m, :], rt, ALU.mult))
                        steps.did(dve.tensor_scalar(t, t, 2.0, -1.0, ALU.mult, ALU.add))
                        steps.did(dve.tensor_tensor_scan(rt, t, i_sb[:, m, :], 0.0, ALU.mult, ALU.add))
                        dve.wait_ge(gr_out[m], i + 1)
                        dve.tensor_tensor(k_.mix[:, bass.ds(2 * i + m, 1), :].rearrange("p a t -> p (a t)"),
                                          rt, gl[:, m, :], ALU.mult).then_inc(mixed, 1)
                    assert steps.n == PER

    def qk(self):
        nc, k_ = self.nc, self
        n_pairs = D // WB
        p0, self.pairs = self.pairs, self.pairs + n_pairs
        work = self.work()
        st = [[work.put(f"qk_{s}{c}", [P, 2, T], F32R) for c in range(2)] for s in range(2)]
        named = lambda what: [[self.sem(f"qk_{what}{s}{c}") for c in range(2)] for s in range(2)]
        hi, lo, stored = named("hi"), named("lo"), named("stored")
        both = [(s, c) for s in range(2) for c in range(2)]

        with nc.Block() as block:
            @block.sync
            def _(sp):
                def store(i):
                    for s, c in both:
                        sp.wait_ge(lo[s][c], i + 1)
                        sp.dma_start(k_.qk_d[2 * i + c][:, 2 * s:2 * s + 2, :], st[s][c][:, :, :].bitcast(F32))\
                            .then_inc(stored[s][c], 16)
                with sp.Fori(0, n_pairs - 1) as i:
                    for s, col in enumerate((QC, KC)):
                        k_.load_block(sp, s, p0 + i + 1, k_.w_block(k_.w_in, col + WB + WB * i))
                    store(i)
                for s in range(2):
                    k_.load_block(sp, s, p0 + n_pairs, k_.w_block(k_.w_in, VC + WB * s))
                store(n_pairs - 1)
                for s, c in both:
                    sp.wait_ge(stored[s][c], 16 * n_pairs)

            @block.tensor
            def _(pe):
                with pe.Fori(0, n_pairs) as i:
                    for s, c in both:
                        if c == 0:
                            pe.wait_ge(k_.w_lo[s], p0 + i + 1)
                        pe.wait_ge(lo[s][c], i)
                        k_.product(pe, k_.ps[2 * s + c], s, c).then_inc((k_.w_first, k_.w_used)[c][s], 1)

            @block.scalar
            def _(act):
                with act.Fori(0, n_pairs) as i:
                    for s, c in both:
                        act.wait_ge((k_.w_first, k_.w_used)[c][s], p0 + i + 1)
                        act.wait_ge(stored[s][c], 16 * i)
                        act.activation(st[s][c][:, 0, :], k_.ps[2 * s + c][:, :], ACT.Copy,
                                       scale=(HD ** -0.5, 1.0)[s]).then_inc(hi[s][c], 1)
                        if c == 1:
                            k_.split_hi(act, s, p0 + i + 1)

            @block.vector
            def _(dve):
                with dve.Fori(0, n_pairs) as i:
                    for s, c in both:
                        dve.wait_ge(hi[s][c], i + 1)
                        dve.scalar_tensor_tensor(out=st[s][c][:, 1, :], in0=k_.ps[2 * s + c][:, :],
                                                 scalar=(HD ** -0.5, 1.0)[s], in1=st[s][c][:, 0, :].bitcast(F32),
                                                 op0=ALU.mult, op1=ALU.subtract).then_inc(lo[s][c], 1)
                        if c == 1:
                            k_.split_lo(dve, s, p0 + i + 1)

    def value(self):
        nc, k_ = self.nc, self
        n_pairs = D // WB // 2
        p0, self.pairs = self.pairs, self.pairs + n_pairs
        work = self.work()
        st = [[work.put(f"v_{s}{part}", [P, NT, WB], F32R) for part in range(2)] for s in range(2)]
        f_raw = work.put("f_raw", [P, KD, NH])
        f_h = work.put("f_h", [P, KD, NH], F32R)
        f_l = work.put("f_l", [P, KD, NH], F32R)
        b_f = work.put("b_f", [P, NH])
        v_mm = [self.sem(f"v_mm{s}") for s in range(2)]
        hi, lo = ([self.sem(f"v_{n}{t}") for t in range(4)] for n in ("hi", "lo"))
        stored = [self.sem(f"v_stored{s}") for s in range(2)]
        f_loaded, f_hi, f_lo, f_mm, f_out = (self.sem(f"f_{n}") for n in ("loaded", "hi", "lo", "mm", "out"))
        steps_of_slot = [(s, t) for s in range(2) for t in range(NT)]

        with nc.Block() as block:
            @block.sync
            def _(sp):
                sp.dma_start(f_raw[:, :, :], k_.w_in.rearrange("(k p) n -> p k n", p=P)[:, :, FL:FL + NH])\
                    .then_inc(f_loaded, 16)
                sp.dma_start(b_f[:, :], k_.ins["b_forget"][0].partition_broadcast(P)).then_inc(f_loaded, 16)

                def store(i):
                    for s in range(2):
                        for t in range(4):
                            sp.wait_ge(lo[t], 4 * i + 2 * s + 2)
                        for part in range(2):
                            sp.dma_start(k_.v_d[2 * i + s, part], st[s][part][:, :, :].bitcast(F32)).then_inc(stored[s], 16)
                with sp.Fori(0, n_pairs - 1) as i:
                    for s in range(2):
                        k_.load_block(sp, s, p0 + i + 1, k_.w_block(k_.w_in, VC + WB * (2 + s) + 2 * WB * i))
                    store(i)
                for s, col in enumerate((ML, MA)):
                    k_.load_block(sp, s, p0 + n_pairs, k_.w_block(k_.w_in, col))
                store(n_pairs - 1)
                for s in range(2):
                    sp.wait_ge(stored[s], 32 * n_pairs)

            @block.tensor
            def _(pe):
                with pe.Fori(0, n_pairs) as i:
                    for s, t in steps_of_slot:
                        if t == 0:
                            pe.wait_ge(k_.w_lo[s], p0 + i + 1)
                        pe.wait_ge(lo[t % 4], 4 * i + 2 * s + t // 4)
                        mm = k_.product_rows(pe, k_.ps[t % 4][:, 0:WB], s, t)
                        mm.then_inc(k_.w_first[s] if t == 0 else k_.w_used[s] if t == NT - 1 else v_mm[s], 1)
                pe.wait_ge(f_lo, 1)
                pe.wait_ge(lo[0], 4 * n_pairs)
                for t in range(NT):
                    rows = slice(t * P, (t + 1) * P)
                    for k in range(KD):
                        for u, w, first, last in ((k_.uh, f_h, k == 0, False), (k_.uh, f_l, False, False),
                                                  (k_.ul, f_h, False, k == KD - 1)):
                            mm = pe.matmul(k_.ps[0][:, t * NH:(t + 1) * NH], u[:, k, rows], w[:, k, :],
                                           start=first, stop=last)
                mm.then_inc(f_mm, 1)

            @block.scalar
            def _(act):
                act.wait_ge(f_loaded, 32)
                act.activation(f_h[:, :, :], f_raw[:, :, :], ACT.Copy).then_inc(f_hi, 1)
                with act.Fori(0, n_pairs) as i:
                    for s, t in steps_of_slot:
                        if t == 0:
                            act.wait_ge(stored[s], 32 * i)
                        if t in (0, NT - 1):
                            act.wait_ge((k_.w_first if t == 0 else k_.w_used)[s], p0 + i + 1)
                        else:
                            act.wait_ge(v_mm[s], (NT - 2) * i + t)
                        act.activation(st[s][0][:, t, :], k_.ps[t % 4][:, 0:WB], ACT.Copy).then_inc(hi[t % 4], 1)
                        if t == NT - 1:
                            k_.split_hi(act, s, p0 + i + 1)

            @block.vector
            def _(dve):
                dve.wait_ge(f_hi, 1)
                dve.tensor_tensor(f_l[:, :, :], f_raw[:, :, :], f_h[:, :, :].bitcast(F32), ALU.subtract).then_inc(f_lo, 1)
                with dve.Fori(0, n_pairs) as i:
                    for s, t in steps_of_slot:
                        dve.wait_ge(hi[t % 4], 4 * i + 2 * s + t // 4 + 1)
                        dve.tensor_tensor(st[s][1][:, t, :], k_.ps[t % 4][:, 0:WB],
                                          st[s][0][:, t, :].bitcast(F32), ALU.subtract).then_inc(lo[t % 4], 1)
                        if t == NT - 1:
                            k_.split_lo(dve, s, p0 + i + 1)
                dve.wait_ge(f_mm, 1)
                dve.tensor_tensor(k_.f_log[:, :, :], k_.ps[0][:, 0:NT * NH].rearrange("p (t h) -> p t h", h=NH),
                                  b_f[:, :].unsqueeze(1).to_broadcast([P, NT, NH]), ALU.add).then_inc(f_out, 1)

    def merge_gates(self):
        nc, k_ = self.nc, self
        n_pairs = D // WB
        p0, self.pairs = self.pairs, self.pairs + n_pairs
        work = self.work()
        st = [[work.put(f"m_{s}{c}", [P, T]) for c in range(2)] for s in range(2)]
        flat = lambda name: work.put(name, [P, NT * NH])
        size, e, w1, dw, eq, ln, neg = (flat(f"d_{n}") for n in ("size", "e", "w1", "dw", "eq", "ln", "neg"))
        c_row = work.put("c_row", [NH, T])
        named = lambda what: [[self.sem(f"m_{what}{s}{c}") for c in range(2)] for s in range(2)]
        out, stored = named("out"), named("stored")
        sized, d_exp, one, d_ln, own, summed_mm, c_out, turned, row_out, row_stored = (
            self.sem(f"d_{n}") for n in ("sized", "exp", "one", "ln", "own", "mm", "c_out", "turned", "row", "stored"))
        both = [(s, c) for s in range(2) for c in range(2)]
        f = k_.f_log[:, :, :].rearrange("p t h -> p (t h)")

        with nc.Block() as block:
            @block.sync
            def _(sp):
                def store(i):
                    for s, c in both:
                        sp.wait_ge(out[s][c], i + 1)
                        sp.dma_start(k_.sig_d[s, 2 * i + c], st[s][c][:, :]).then_inc(stored[s][c], 16)
                with sp.Fori(0, n_pairs - 1) as i:
                    for s, col in enumerate((ML, MA)):
                        k_.load_block(sp, s, p0 + i + 1, k_.w_block(k_.w_in, col + WB + WB * i))
                    store(i)
                for s in range(2):
                    k_.load_block(sp, s, p0 + n_pairs, k_.w_block(k_.ins["w_lru_out"][0], WB * s))
                store(n_pairs - 1)
                sp.wait_ge(row_out, 1)
                sp.dma_start(k_.c_d, c_row[:, :]).then_inc(row_stored, 16)
                sp.wait_ge(row_stored, 16)
                for s, c in both:
                    sp.wait_ge(stored[s][c], 16 * n_pairs)

            @block.tensor
            def _(pe):
                with pe.Fori(0, n_pairs) as i:
                    for s, c in both:
                        if c == 0:
                            pe.wait_ge(k_.w_lo[s], p0 + i + 1)
                        pe.wait_ge(out[s][c], i)
                        k_.product(pe, k_.ps[2 * s + c], s, c).then_inc((k_.w_first, k_.w_used)[c][s], 1)
                pe.wait_ge(own, 9)
                pe.wait_ge(out[0][0], n_pairs)
                for t in range(NT):
                    for j in range(t + 1):
                        mm = pe.matmul(k_.ps[0][:, t * NH:(t + 1) * NH], (k_.tri if j == t else k_.ones)[:, :],
                                       k_.f_log[:, j, :], start=(j == 0), stop=(j == t))
                mm.then_inc(summed_mm, 1)
                pe.wait_ge(c_out, 1)
                pe.wait_ge(out[0][1], n_pairs)
                for t in range(NT):
                    mm = pe.transpose(k_.ps[1][0:NH, t * P:(t + 1) * P], k_.c_tok[:, t, :], k_.ident[:, :])
                mm.then_inc(turned, 1)

            @block.scalar
            def _(act):
                act.wait_ge(sized, 1)
                act.activation(e[:, :], size[:, :], ACT.Exp, scale=-1.0).then_inc(d_exp, 1)
                act.wait_ge(one, 1)
                act.activation(ln[:, :], w1[:, :], ACT.Ln).then_inc(d_ln, 1)
                with act.Fori(0, n_pairs) as i:
                    for s, c in both:
                        act.wait_ge((k_.w_first, k_.w_used)[c][s], p0 + i + 1)
                        act.wait_ge(stored[s][c], 16 * i)
                        act.activation(st[s][c][:, :], k_.ps[2 * s + c][:, :], ACT.Sigmoid).then_inc(out[s][c], 1)
                        if c == 1:
                            k_.split_hi(act, s, p0 + i + 1)

            @block.vector
            def _(dve):
                steps = Steps(dve, own)
                dve.scalar_tensor_tensor(out=size[:, :], in0=f, scalar=-1.0, in1=f, op0=ALU.mult, op1=ALU.max)\
                    .then_inc(sized, 1)
                steps.did(dve.tensor_scalar(neg[:, :], f, 0.0, None, ALU.min))
                dve.wait_ge(d_exp, 1)
                dve.tensor_scalar(w1[:, :], e[:, :], 1.0, None, ALU.add).then_inc(one, 1)
                dve.wait_ge(one, 1)
                steps.did(dve.tensor_scalar(dw[:, :], w1[:, :], -1.0, None, ALU.add))
                steps.did(dve.tensor_scalar(eq[:, :], dw[:, :], 0.0, None, ALU.is_equal))
                steps.did(dve.tensor_tensor(dw[:, :], dw[:, :], eq[:, :], ALU.add))
                steps.did(dve.reciprocal(dw[:, :], dw[:, :]))
                dve.wait_ge(d_ln, 1)
                steps.did(dve.tensor_tensor(eq[:, :], eq[:, :], ln[:, :], ALU.add))
                steps.did(dve.tensor_tensor(eq[:, :], eq[:, :], dw[:, :], ALU.mult))
                steps.did(dve.tensor_tensor(eq[:, :], eq[:, :], e[:, :], ALU.mult))
                steps.did(dve.tensor_tensor(f, neg[:, :], eq[:, :], ALU.subtract))
                with dve.Fori(0, n_pairs) as i:
                    for s in range(2):
                        k_.split_lo(dve, s, p0 + i + 1)
                dve.wait_ge(summed_mm, 1)
                dve.tensor_copy(k_.c_tok[:, :, :].rearrange("p t h -> p (t h)"), k_.ps[0][:, 0:NT * NH]).then_inc(c_out, 1)
                dve.wait_ge(turned, 1)
                dve.tensor_copy(c_row[:, :], k_.ps[1][0:NH, :]).then_inc(row_out, 1)

    def branch_out(self, branch):
        nc, k_ = self.nc, self
        n_pairs = D // WB // 2
        p0, self.pairs = self.pairs, self.pairs + n_pairs
        weights = self.ins["w_lru_out" if branch == 0 else "w_attn_out"][0]
        following = self.ins["w_attn_out" if branch == 0 else "w_out"][0]
        work = self.work()
        tag = "lo" if branch == 0 else "ao"
        sg = [[work.put(f"{tag}_sg{s}{c}", [P, T]) for c in range(2)] for s in range(2)]
        stage = [work.put(f"{tag}_in{r}", [P, T]) for r in range(4)]
        named = lambda what: [[self.sem(f"{tag}_{what}{s}{c}") for c in range(2)] for s in range(2)]
        loaded, gated = named("loaded"), named("gated")
        in_loaded = [self.sem(f"{tag}_in{r}") for r in range(4)]
        in_hi, in_lo, own = (self.sem(f"{tag}_{n}") for n in ("hi", "split", "own"))
        both = [(s, c) for s in range(2) for c in range(2)]
        source = lambda k: k_.mix[:, k, :] if branch == 0 else stage[k % 4][:, :]

        with nc.Block() as block:
            @block.sync
            def _(sp):
                if branch == 1:
                    for k in range(KD):
                        if k >= 4:
                            sp.wait_ge(in_lo, k - 3)
                        sp.dma_start(stage[k % 4][:, :], k_.o_d[k]).then_inc(in_loaded[k % 4], 16)

                def gates(i):
                    for s, c in both:
                        sp.wait_ge(gated[s][c], i)
                        sp.dma_start(sg[s][c][:, :], k_.sig_d[branch, 4 * i + 2 * s + c]).then_inc(loaded[s][c], 16)
                with sp.Fori(0, n_pairs - 1) as i:
                    gates(i)
                    for s in range(2):
                        k_.load_block(sp, s, p0 + i + 1, k_.w_block(weights, WB * (2 + s) + 2 * WB * i))
                gates(n_pairs - 1)
                for s in range(2):
                    k_.load_block(sp, s, p0 + n_pairs, k_.w_block(following, WB * s))

            @block.tensor
            def _(pe):
                for k in range(KD):
                    pe.wait_ge(in_lo, k + 1)
                with pe.Fori(0, n_pairs) as i:
                    for s, c in both:
                        if c == 0:
                            pe.wait_ge(k_.w_lo[s], p0 + i + 1)
                        pe.wait_ge(gated[s][c], i)
                        k_.product(pe, k_.ps[2 * s + c], s, c).then_inc((k_.w_first, k_.w_used)[c][s], 1)

            @block.scalar
            def _(act):
                for k in range(KD):
                    if branch == 1:
                        act.wait_ge(in_loaded[k % 4], 16 * (k // 4 + 1))
                    act.activation(k_.uh[:, k, :], source(k), ACT.Copy).then_inc(in_hi, 1)
                with act.Fori(0, n_pairs) as i:
                    for s in range(2):
                        k_.split_hi(act, s, p0 + i + 1)

            @block.vector
            def _(dve):
                for k in range(KD):
                    dve.wait_ge(in_hi, k + 1)
                    dve.tensor_tensor(k_.ul[:, k, :], source(k), k_.uh[:, k, :].bitcast(F32),
                                      ALU.subtract).then_inc(in_lo, 1)
                with dve.Fori(0, n_pairs) as i:
                    for s, c in both:
                        dve.wait_ge((k_.w_first, k_.w_used)[c][s], p0 + i + 1)
                        dve.wait_ge(loaded[s][c], 16 * (i + 1))
                        mix = k_.mix[:, bass.ds(4 * i + 2 * s + c, 1), :].rearrange("p a t -> p (a t)")
                        if branch == 0:
                            dve.tensor_tensor(mix, k_.ps[2 * s + c][:, :], sg[s][c][:, :], ALU.mult)\
                                .then_inc(gated[s][c], 1)
                        else:
                            dve.tensor_tensor(sg[s][c][:, :], k_.ps[2 * s + c][:, :], sg[s][c][:, :], ALU.mult)\
                                .then_inc(own, 1)
                            dve.wait_ge(own, 4 * i + 2 * s + c + 1)
                            dve.tensor_tensor(mix, mix, sg[s][c][:, :], ALU.add).then_inc(gated[s][c], 1)
                        if c == 1:
                            k_.split_lo(dve, s, p0 + i + 1)

    def attention(self):
        nc, k_ = self.nc, self
        upper = Map(nc, self.act_start, self.work_start - 4 * KD * T)
        qk = [upper.put(f"at_qk{c}", [P, 4, T], F32R) for c in range(2)]
        v = [upper.put(f"at_v{c}", [P, 2, NT, HD], F32R) for c in range(2)]
        c_all = [upper.put(f"at_c{c}", [P, T]) for c in range(2)]
        o_sb = [upper.put(f"at_o{g}", [P, HALF]) for g in range(2)]
        bias = upper.put("at_bias", [P, T])
        work = self.work()
        pt_h = [work.put(f"at_pth{g}", [P, 4 + 4 * g, HALF], F32R) for g in range(2)]
        pt_l = [work.put(f"at_ptl{g}", [P, 4 + 4 * g, HALF], F32R) for g in range(2)]
        SB = 3
        sb = [work.put(f"at_s{b}", [P, T]) for b in range(SB)]
        later = Map(nc, k_.zeros_at, k_.zeros_at + 4 * P).put("at_later", [P, P])
        c_q = work.put("at_cq", [P, 2, NT])
        small = work.put("at_small", [P, 2, 4])
        sem = self.sem
        qk_in, v_in, c_in, cq_done, stored = ([sem(f"at_{n}{c}") for c in range(2)]
                                              for n in ("qk", "vin", "cin", "cq", "stored"))
        names = ("later", "biased", "masked", "s_mm", "maxed", "negated", "exped", "inverted", "scaled",
                 "t_mm", "hi", "lo", "pv_mm", "o_out")
        later_made, biased, masked, s_mm, maxed, negated, exped, inverted, scaled, t_mm, hi, lo, pv_mm, o_out = (
            sem("at_" + n) for n in names)
        turns, tiles = NH // 2, 2 * NT
        parts = [(n, kb, min(4, n % NT + 1 - kb)) for n in range(tiles) for kb in range(0, n % NT + 1, 4)]
        of_tile = [[st for st, part in enumerate(parts) if part[0] == n] for n in range(tiles)]
        turned = lambda st: k_.ps[2][:, st % 2 * HALF:st % 2 * HALF + parts[st][2] * P]

        def piece(pt, st):
            n, kb, m = parts[st]
            return pt[n % NT // 4][:, kb:kb + m, n % 4 * P:n % 4 * P + P]

        with nc.Block() as block:
            @block.sync
            def _(sp):
                def load(i, c):
                    sp.wait_ge(pv_mm, 4 * i)
                    sp.dma_start(qk[c][:, :, :].bitcast(F32), k_.qk_d[2 * i + c]).then_inc(qk_in[c], 16)
                    sp.dma_start(c_all[c][:, :], k_.c_d[2 * i + c].partition_broadcast(P)).then_inc(c_in[c], 16)
                    for part in range(2):
                        sp.dma_start(v[c][:, part, :, :].bitcast(F32),
                                     k_.v_d[i, part, :, :, c * HD:(c + 1) * HD]).then_inc(v_in[c], 16)
                with sp.Fori(0, turns) as i:
                    for c in range(2):
                        load(i, c)
                    for group in range(4):
                        c, g = group // 2, group % 2
                        sp.wait_ge(o_out, 4 * i + group + 1)
                        sp.dma_start(k_.o_d[2 * i + c][:, g * HALF:(g + 1) * HALF], o_sb[g][:, :]).then_inc(stored[g], 16)
                for g in range(2):
                    sp.wait_ge(stored[g], 32 * turns)

            @block.gpsimd
            def _(pool):
                pool.memset(later[:, :], 0.0).then_inc(later_made, 1)
                pool.wait_ge(later_made, 1)
                pool.affine_select(out=later[:, :], in_=later[:, :], compare_op=ALU.is_ge, fill=NEG, base=0,
                                   pattern=[[-1, P]], channel_multiplier=1).then_inc(later_made, 1)
                pool.wait_ge(later_made, 2)
                with pool.Fori(0, turns) as i:
                    for n in range(tiles):
                        c, qb = n // NT, n % NT
                        keys = (qb + 1) * P
                        if qb == 0:
                            pool.wait_ge(cq_done[c], i + 1)
                            pool.wait_ge(c_in[c], 16 * (i + 1))
                        pool.wait_ge(maxed, tiles * i + n)
                        pool.tensor_tensor(bias[:, 0:keys], c_q[:, c, qb:qb + 1].to_broadcast([P, keys]),
                                           c_all[c][:, 0:keys], ALU.subtract).then_inc(biased, 1)
                        pool.wait_ge(biased, tiles * i + n + 1)
                        pool.tensor_tensor(bias[:, keys - P:keys], bias[:, keys - P:keys], later[:, :], ALU.add)\
                            .then_inc(masked, 1)

            @block.tensor
            def _(pe):
                def scores(i, n):
                    c, qb = n // NT, n % NT
                    keys = (qb + 1) * P
                    if qb == 0:
                        pe.wait_ge(qk_in[c], 16 * (i + 1))
                    pe.wait_ge(maxed, tiles * i + max(n - 1, 0))
                    q_h, q_l = (qk[c][:, part, qb * P:(qb + 1) * P] for part in range(2))
                    for at in range(0, keys, HALF):
                        end = min(at + HALF, keys)
                        for q, part, first, last in ((q_h, 2, True, False), (q_h, 3, False, False), (q_l, 2, False, True)):
                            mm = pe.matmul(k_.ps[n % 2][:, at:end], q, qk[c][:, part, at:end], start=first, stop=last)
                    mm.then_inc(s_mm, 1)

                def turn(i, n):
                    pe.wait_ge(scaled, tiles * i + n + 1)
                    for st in of_tile[n]:
                        _, kb, m = parts[st]
                        pe.wait_ge(lo, len(parts) * i + max(st - 1, 0))
                        for j in range(m):
                            mm = pe.transpose(turned(st)[:, j * P:(j + 1) * P], sb[n % SB][:, (kb + j) * P:(kb + j + 1) * P],
                                              k_.ident[:, :])
                        mm.then_inc(t_mm, 1)

                def values(i, group):
                    c, g = group // 2, group % 2
                    if g == 0:
                        pe.wait_ge(v_in[c], 32 * (i + 1))
                    pe.wait_ge(lo, len(parts) * i + of_tile[4 * group + 3][-1] + 1)
                    pe.wait_ge(o_out, 4 * i + max(group - 1, 0))
                    blocks = 4 * g + 4
                    for kb in range(blocks):
                        q0 = max(0, kb - 4 * g) * P
                        for part, pt, first, last in ((0, pt_h, kb == 0, False), (0, pt_l, False, False),
                                                      (1, pt_h, False, kb == blocks - 1)):
                            mm = pe.matmul(k_.ps[3][:, g * HALF + q0:(g + 1) * HALF], v[c][:, part, kb, :],
                                           pt[g][:, kb, q0:HALF], start=first, stop=last)
                    mm.then_inc(pv_mm, 1)

                with pe.Fori(0, turns) as i:
                    for n in range(tiles + 3):
                        if n < tiles:
                            scores(i, n)
                        if 2 <= n < tiles + 2:
                            turn(i, n - 2)
                        if n >= 6 and n % 4 == 2:
                            values(i, (n - 6) // 4)

            @block.scalar
            def _(act):
                def output(i, group):
                    c, g = group // 2, group % 2
                    act.wait_ge(pv_mm, 4 * i + group + 1)
                    act.wait_ge(stored[g], 16 * (2 * i + c))
                    act.activation(o_sb[g][:, :], k_.ps[3][:, g * HALF:(g + 1) * HALF],
                                   ACT.Copy).then_inc(o_out, 1)

                with act.Fori(0, turns) as i:
                    for n in range(tiles + 3):
                        if n < tiles:
                            keys = (n % NT + 1) * P
                            act.wait_ge(negated, tiles * i + n + 1)
                            act.activation(sb[n % SB][:, 0:keys], sb[n % SB][:, 0:keys], ACT.Exp,
                                           bias=small[:, n % 2, 1:2], accum_out=small[:, n % 2, 2:3]).then_inc(exped, 1)
                        if 2 <= n < tiles + 2:
                            for st in of_tile[n - 2]:
                                group = (n - 2) // 4
                                act.wait_ge(t_mm, len(parts) * i + st + 1)
                                act.wait_ge(pv_mm, 4 * i + max(group - 1, 0))
                                act.activation(piece(pt_h, st), turned(st).rearrange("p (k q) -> p k q", q=P),
                                               ACT.Copy).then_inc(hi, 1)
                        if n >= 6 and n % 4 == 2:
                            output(i, (n - 6) // 4)

            @block.vector
            def _(dve):
                def biased_scores(i, n):
                    dve.wait_ge(s_mm, tiles * i + n + 1)
                    dve.wait_ge(masked, tiles * i + n + 1)

                def take_cq(i, c):
                    dve.tensor_scalar(c_q[:, c, :], k_.c_tok[:, :, bass.ds(2 * i + c, 1)].rearrange("p t h -> p (t h)"),
                                      1.0, None, ALU.mult).then_inc(cq_done[c], 1)

                with dve.Fori(0, turns) as i:
                    dve.wait_ge(masked, tiles * i)
                    take_cq(i, 0)
                    biased_scores(i, 0)
                    take_cq(i, 1)
                    for n in range(tiles + 2):
                        if n < tiles:
                            keys = (n % NT + 1) * P
                            dve.tensor_tensor_reduce(out=sb[n % SB][:, 0:keys], in0=k_.ps[n % 2][:, 0:keys],
                                                     in1=bias[:, 0:keys], scale=1.0, scalar=NEG, op0=ALU.add,
                                                     op1=ALU.max, accum_out=small[:, n % 2, 0:1]).then_inc(maxed, 1)
                            dve.wait_ge(maxed, tiles * i + n + 1)
                            if n == 0:
                                biased_scores(i, 1)
                            dve.tensor_scalar(small[:, n % 2, 1:2], small[:, n % 2, 0:1], -1.0, None, ALU.mult)\
                                .then_inc(negated, 1)
                        if 1 <= n < tiles + 1:
                            b, s3, keys = (n - 1) % 2, (n - 1) % SB, ((n - 1) % NT + 1) * P
                            dve.wait_ge(exped, tiles * i + n)
                            dve.reciprocal(small[:, b, 3:4], small[:, b, 2:3]).then_inc(inverted, 1)
                            dve.wait_ge(inverted, tiles * i + n)
                            if n + 1 < tiles:
                                biased_scores(i, n + 1)
                            dve.tensor_scalar(sb[s3][:, 0:keys], sb[s3][:, 0:keys], small[:, b, 3:4], None, ALU.mult)\
                                .then_inc(scaled, 1)
                        if 2 <= n < tiles + 2:
                            for st in of_tile[n - 2]:
                                dve.wait_ge(hi, len(parts) * i + st + 1)
                                dve.tensor_tensor(piece(pt_l, st), turned(st).rearrange("p (k q) -> p k q", q=P),
                                                  piece(pt_h, st).bitcast(F32), ALU.subtract).then_inc(lo, 1)

    def project(self):
        nc, k_ = self.nc, self
        n_pairs = D // WB // 2
        p0, self.pairs = self.pairs, self.pairs + n_pairs
        work = self.work()
        self.x2 = work.put("x2", [P, NT, D])
        self.x2_end = work.at
        x_in = [self.sem(f"pr_x{t}") for t in range(NT)]
        in_hi, in_lo = self.sem("pr_hi"), self.sem("pr_split")
        mm_done = [self.sem(f"pr_mm{s}") for s in range(2)]
        added = [self.sem(f"pr_add{t}") for t in range(4)]
        weights = self.ins["w_out"][0]

        with nc.Block() as block:
            @block.sync
            def _(sp):
                for t in range(NT):
                    sp.dma_start(k_.x2[:, t, :], k_.x[t * P:(t + 1) * P, :]).then_inc(x_in[t], 16)
                for s in range(2):
                    k_.load_block(sp, s, p0 + 1, k_.w_block(weights, WB * (2 + s)))

            @block.tensor
            def _(pe):
                for k in range(KD):
                    pe.wait_ge(in_lo, k + 1)
                with pe.Fori(0, n_pairs) as i:
                    for s in range(2):
                        for t in range(NT):
                            if t == 0:
                                pe.wait_ge(k_.w_lo[s], p0 + i + 1)
                            pe.wait_ge(added[t % 4], 4 * i + 2 * s + t // 4)
                            mm = k_.product_rows(pe, k_.ps[t % 4][:, 0:WB], s, t)
                            mm.then_inc(k_.w_first[s] if t == 0 else k_.w_used[s] if t == NT - 1 else mm_done[s], 1)

            @block.scalar
            def _(act):
                for k in range(KD):
                    act.activation(k_.uh[:, k, :], k_.mix[:, k, :], ACT.Copy).then_inc(in_hi, 1)
                for s in range(2):
                    k_.split_hi(act, s, p0 + 1)

            @block.vector
            def _(dve):
                for k in range(KD):
                    dve.wait_ge(in_hi, k + 1)
                    dve.tensor_tensor(k_.ul[:, k, :], k_.mix[:, k, :], k_.uh[:, k, :].bitcast(F32),
                                      ALU.subtract).then_inc(in_lo, 1)
                for t in range(NT):
                    dve.wait_ge(x_in[t], 16)

                def turn(i, last):
                    for s in range(2):
                        for t in range(NT):
                            if t in (0, NT - 1):
                                dve.wait_ge((k_.w_first if t == 0 else k_.w_used)[s], p0 + i + 1)
                            else:
                                dve.wait_ge(mm_done[s], (NT - 2) * i + t)
                            part = k_.x2[:, t, bass.ds(WB * (2 * i + s), WB)]
                            dve.tensor_tensor(part, part, k_.ps[t % 4][:, 0:WB], ALU.add).then_inc(added[t % 4], 1)
                        if not last:
                            k_.split_lo(dve, s, p0 + i + 1)
                turn(0, False)
                turn(1, True)

    def route(self):
        nc, k_, ins = self.nc, self, self.ins
        low = Map(nc, self.fixed_end, self.act_start)
        self.e_raw = [low.put(f"e_raw{r}", [P, 4, HALF]) for r in range(6)]
        work = Map(nc, self.act_start, self.work_start)
        put, sem = work.put, self.sem
        NL = NG + NE
        g_b, b_r, w_r = put("rt_g", [P, D]), put("rt_b", [P, NL]), put("rt_w", [P, KD, NL])
        xn = [put(f"rt_xn{b}", [P, D]) for b in range(2)]
        xt = [put(f"rt_xt{b}", [P, KD, P]) for b in range(2)]
        square, zeros = put("rt_square", [P, D]), put("rt_zeros", [P, SLOTS // P + 1], I32)
        total, mean, rstd, power = (put(f"rt_{n}", [P, NT]) for n in ("total", "mean", "rstd", "power"))
        logits = put("rt_logits", [P, NT, NL])
        i_exp, e_base = put("rt_iexp", [P, NT, NE]), put("rt_ebase", [P, NT, NE])
        i_grp, grp, g_eq = (put(f"rt_{n}", [P, NT, NG]) for n in ("igrp", "grp", "geq"))
        m_exp, eq, oh1, oh2, prod = (put(f"rt_{n}", [P, NT, NE]) for n in ("mexp", "eq", "oh1", "oh2", "prod"))
        gmax, gsum, gsel, m1, m2, sel, ex, inv, dst = (
            put(f"rt_{n}", [P, NT]) for n in ("gmax", "gsum", "gsel", "m1", "m2", "sel", "ex", "inv", "dst"))
        tok = put("rt_tok", [P, NT], I32)
        NX = MAXX
        cnt, extra, ends, shift = (put(f"rt_{n}", [P, NE]) for n in ("cnt", "extra", "ends", "shift"))
        limit, over = put("rt_limit", [P, NE, KD - 1]), put("rt_over", [P, NE, KD - 1])
        jj, before, which = put("rt_jj", [1, NX, NE]), put("rt_before", [1, NX, NE]), put("rt_which", [1, NX])

        in_sem, zeroed, filled, consts = sem("rt_in"), sem("rt_zeroed"), sem("rt_filled"), sem("rt_consts")
        squared, averaged, powered, scaled, stored = (
            sem(f"rt_{n}") for n in ("squared", "averaged", "powered", "scaled", "stored0"))
        stored = [stored, sem("rt_stored1")]
        turned, copied, logit_mm, logit_out = (sem(f"rt_{n}") for n in ("turned", "copied", "mm", "logit"))
        own, to_exp, exped, chosen, rank_mm, dest_out, scattered = (
            sem(f"rt_{n}") for n in ("own", "to_exp", "exped", "chosen", "rank", "dest", "scattered"))
        tiles = NT // 2

        with nc.Block() as block:
            @block.sync
            def _(sp):
                sp.dma_start(g_b[:, :], ins["g_ffn"][0].partition_broadcast(P)).then_inc(in_sem, 16)
                sp.dma_start(b_r[:, 0:NG], ins["b_route_group"][0].partition_broadcast(P)).then_inc(in_sem, 16)
                sp.dma_start(b_r[:, NG:NL], ins["b_route_expert"][0].partition_broadcast(P)).then_inc(in_sem, 16)
                rows = lambda w: w[0].rearrange("(k p) n -> p k n", p=P)
                sp.dma_start(w_r[:, :, 0:NG], rows(ins["w_route_group"])).then_inc(in_sem, 16)
                sp.dma_start(w_r[:, :, NG:NL], rows(ins["w_route_expert"])).then_inc(in_sem, 16)
                sp.wait_ge(zeroed, 1)
                sp.dma_start(k_.slots_d.rearrange("(p n) a -> p (n a)", p=P), zeros[:, :]).then_inc(filled, 16)
                for m, e in ((0, 0), (1, 0), (2, 0), (3, 0), (4, 1), (5, 1)):
                    k_.load_piece(sp, (0, m), ("gate", "up", "gate")[m // 2], m % 2, e, True)
                with sp.Fori(0, tiles) as i:
                    for b in range(2):
                        sp.wait_ge(scaled, 2 * i + b + 1)
                        sp.dma_start(k_.xn_d[bass.ds((2 * i + b) * P, P), :], xn[b][:, :]).then_inc(stored[b], 16)
                for b in range(2):
                    sp.wait_ge(stored[b], 16 * tiles)

            @block.gpsimd
            def _(pool):
                pool.memset(zeros[:, :], 0).then_inc(zeroed, 1)
                pool.memset(power[:, :], -0.5).then_inc(consts, 1)
                iota = lambda out, pattern, base, step: pool.iota(
                    out, pattern, base=base, channel_multiplier=step,
                    allow_small_or_imprecise_dtypes=True).then_inc(consts, 1)
                iota(i_grp[:, :, :], [[0, NT], [1, NG]], 100, 0)
                iota(i_exp[:, :, :], [[0, NT], [1, NE]], 100, 0)
                iota(e_base[:, :, :], [[0, NT], [BLK, NE]], 0, 0)
                iota(limit[:, :, :], [[0, NE], [BLK, KD - 1]], BLK, 0)
                iota(jj[:, :, :], [[1, NX], [0, NE]], 0, 0)
                iota(tok[:, :], [[P, NT]], 0, 1)
                pool.wait_ge(averaged, 1)
                pool.wait_ge(consts, 7)
                pool.tensor_tensor(rstd[:, :], mean[:, :], power[:, :], ALU.pow).then_inc(powered, 1)
                pool.wait_ge(filled, 16)
                for s in range(2):
                    pool.wait_ge(dest_out, s + 1)
                    for t in range(NT):
                        pool.indirect_dma_start(
                            out=k_.slots_d, out_offset=bass.IndirectOffsetOnAxis(ap=k_.dest[:, s, t:t + 1], axis=0),
                            in_=tok[:, t:t + 1], in_offset=None).then_inc(scattered, 16)
                pool.wait_ge(scattered, 16 * 2 * NT)

            @block.tensor
            def _(pe):
                pe.wait_ge(in_sem, 16 * 5)

                def logits_of(i, b):
                    pe.wait_ge(copied, 2 * i + b + 1)
                    pe.wait_ge(logit_out, 2 * i)
                    for k in range(KD):
                        mm = pe.matmul(k_.ps[2 + b][:, 0:NL], xt[b][:, k, :], w_r[:, k, :],
                                       start=(k == 0), stop=(k == KD - 1))
                    mm.then_inc(logit_mm, 1)
                with pe.Fori(0, tiles) as i:
                    for b in range(2):
                        pe.wait_ge(scaled, 2 * i + b + 1)
                        pe.wait_ge(copied, 2 * i)
                        for k in range(KD):
                            mm = pe.transpose(k_.ps[b][:, k * P:(k + 1) * P], xn[b][:, k * P:(k + 1) * P], k_.ident[:, :])
                        mm.then_inc(turned, 1)
                    for b in range(2):
                        logits_of(i, b)
                pe.wait_ge(chosen, 1)
                for t in range(NT + 1):
                    for j in range(min(t + 1, NT)):
                        mm = pe.matmul(k_.ps[0][:, t * NE:(t + 1) * NE], (k_.stri if j == t else k_.ones)[:, :],
                                       prod[:, j, :], start=(j == 0), stop=(j == min(t, NT - 1)))
                mm.then_inc(rank_mm, 1)

            @block.scalar
            def _(act):
                for t in range(NT):
                    act.activation(square[:, :], k_.x2[:, t, :], ACT.Square, accum_out=total[:, t:t + 1]).then_inc(squared, 1)
                    act.wait_ge(squared, t + 1)
                with act.Fori(0, tiles) as i:
                    for b in range(2):
                        act.wait_ge(turned, 2 * i + b + 1)
                        act.wait_ge(logit_mm, 2 * i)
                        act.activation(xt[b][:, :, :].rearrange("p k t -> p (k t)"), k_.ps[b][:, :], ACT.Copy)\
                            .then_inc(copied, 1)
                act.wait_ge(to_exp, 1)
                act.activation(grp[:, :, :], grp[:, :, :], ACT.Exp).then_inc(exped, 1)
                act.wait_ge(to_exp, 2)
                act.activation(ex[:, :], ex[:, :], ACT.Exp).then_inc(exped, 1)

            @block.vector
            def _(dve):
                dve.wait_ge(squared, NT)
                dve.tensor_scalar(mean[:, :], total[:, :], 1.0 / D, EPS, ALU.mult, ALU.add).then_inc(averaged, 1)
                dve.wait_ge(powered, 1)
                dve.wait_ge(in_sem, 16 * 5)
                with dve.Fori(0, tiles) as i:
                    for b in range(2):
                        t = 2 * i + b
                        dve.wait_ge(stored[b], 16 * i)
                        dve.wait_ge(turned, 2 * i)
                        dve.scalar_tensor_tensor(out=xn[b][:, :], in0=k_.x2[:, bass.ds(t, 1), :].rearrange("p a n -> p (a n)"),
                                                 scalar=rstd[:, bass.ds(t, 1)], in1=g_b[:, :], op0=ALU.mult,
                                                 op1=ALU.mult).then_inc(scaled, 1)
                    for b in range(2):
                        dve.wait_ge(logit_mm, 2 * i + b + 1)
                        dve.tensor_tensor(logits[:, bass.ds(2 * i + b, 1), :].rearrange("p a n -> p (a n)"),
                                          k_.ps[2 + b][:, 0:NL], b_r[:, :], ALU.add).then_inc(logit_out, 1)
                dve.wait_ge(logit_out, NT)
                dve.wait_ge(consts, 7)
                steps = Steps(dve, own)
                did = steps.did
                tt = lambda out, a, b, op: did(dve.tensor_tensor(out, a, b, op))
                over_last = lambda v, n: v.unsqueeze(2).to_broadcast([P, NT, n])
                gl, el = logits[:, :, 0:NG], logits[:, :, NG:NL]

                def first_match(values, top, numbers, scratch, chosen_one, n):
                    tt(scratch, values, over_last(top, n), ALU.is_equal)
                    did(dve.scalar_tensor_tensor(out=scratch, in0=scratch, scalar=-100.0, in1=numbers,
                                                 op0=ALU.mult, op1=ALU.add))
                    did(dve.tensor_reduce(sel[:, :], scratch, AX.X, ALU.min))
                    did(dve.tensor_scalar(sel[:, :], sel[:, :], 100.0, None, ALU.add))
                    tt(chosen_one, numbers, over_last(sel[:, :], n), ALU.is_equal)

                did(dve.tensor_reduce(gmax[:, :], gl, AX.X, ALU.max))
                dve.tensor_tensor(grp[:, :, :], gl, over_last(gmax[:, :], NG), ALU.subtract).then_inc(to_exp, 1)
                dve.wait_ge(exped, 1)
                did(dve.tensor_reduce(gsum[:, :], grp[:, :, :], AX.X, ALU.add))
                did(dve.reciprocal(gsum[:, :], gsum[:, :]))
                first_match(gl, gmax[:, :], i_grp[:, :, :], g_eq[:, :, :], grp[:, :, :], NG)
                in_group = grp[:, :, :].unsqueeze(3).to_broadcast([P, NT, NG, EG])
                by_group = lambda v: v.rearrange("p t (g e) -> p t g e", g=NG)
                tt(by_group(m_exp[:, :, :]), by_group(el), in_group, ALU.mult)
                did(dve.tensor_scalar(g_eq[:, :, :], grp[:, :, :], -NEG, NEG, ALU.mult, ALU.add))
                tt(by_group(m_exp[:, :, :]), by_group(m_exp[:, :, :]),
                   g_eq[:, :, :].unsqueeze(3).to_broadcast([P, NT, NG, EG]), ALU.add)
                did(dve.tensor_reduce(m1[:, :], m_exp[:, :, :], AX.X, ALU.max))
                first_match(m_exp[:, :, :], m1[:, :], i_exp[:, :, :], eq[:, :, :], oh1[:, :, :], NE)
                did(dve.scalar_tensor_tensor(out=m_exp[:, :, :], in0=oh1[:, :, :], scalar=NEG, in1=m_exp[:, :, :],
                                             op0=ALU.mult, op1=ALU.add))
                did(dve.tensor_reduce(m2[:, :], m_exp[:, :, :], AX.X, ALU.max))
                dve.tensor_tensor(ex[:, :], m2[:, :], m1[:, :], ALU.subtract).then_inc(to_exp, 1)
                first_match(m_exp[:, :, :], m2[:, :], i_exp[:, :, :], eq[:, :, :], oh2[:, :, :], NE)
                dve.tensor_tensor(prod[:, :, :], oh1[:, :, :], oh2[:, :, :], ALU.add).then_inc(chosen, 1)
                dve.wait_ge(exped, 2)
                did(dve.tensor_scalar(inv[:, :], ex[:, :], 1.0, None, ALU.add))
                did(dve.reciprocal(inv[:, :], inv[:, :]))
                tt(k_.wgt[:, 0, :], inv[:, :], gsum[:, :], ALU.mult)
                tt(k_.wgt[:, 1, :], k_.wgt[:, 0, :], ex[:, :], ALU.mult)
                dve.wait_ge(rank_mm, 1)
                did(dve.tensor_copy(cnt[:, :], k_.ps[0][:, NT * NE:(NT + 1) * NE]))
                tt(over[:, :, :], cnt[:, :].unsqueeze(2).to_broadcast([P, NE, KD - 1]), limit[:, :, :], ALU.is_gt)
                did(dve.tensor_reduce(extra[:, :], over[:, :, :], AX.X, ALU.add))
                did(dve.tensor_tensor_scan(ends[:, :], k_.ones[:, 0:NE], extra[:, :], 0.0, ALU.mult, ALU.add))
                tt(shift[:, :], ends[:, :], extra[:, :], ALU.subtract)
                did(dve.tensor_scalar(shift[:, :], shift[:, :], float(BLK), float(BLK * (NE - 1)), ALU.mult, ALU.add))
                tt(shift[:, :], shift[:, :], e_base[:, 0, :], ALU.subtract)
                rank = k_.ps[0][:, 0:NT * NE].rearrange("p (t e) -> p t e", e=NE)
                did(dve.tensor_scalar(eq[:, :, :], rank, float(BLK), None, ALU.is_ge))
                tt(eq[:, :, :], eq[:, :, :], shift[:, :].unsqueeze(1).to_broadcast([P, NT, NE]), ALU.mult)
                tt(e_base[:, :, :], e_base[:, :, :], rank, ALU.add)
                tt(e_base[:, :, :], e_base[:, :, :], eq[:, :, :], ALU.add)
                for s, oh in enumerate((oh1, oh2)):
                    tt(oh[:, :, :], oh[:, :, :], e_base[:, :, :], ALU.mult)
                    did(dve.tensor_reduce(dst[:, :], oh[:, :, :], AX.X, ALU.add))
                    dve.tensor_copy(k_.dest[:, s, :], dst[:, :]).then_inc(dest_out, 1)
                tt(before[:, :, :], ends[0:1, :].unsqueeze(1).to_broadcast([1, NX, NE]), jj[:, :, :], ALU.is_le)
                did(dve.tensor_reduce(which[:, :], before[:, :, :], AX.X, ALU.add))
                did(dve.tensor_scalar(which[:, :], which[:, :], float(NE - 1), None, ALU.min))
                did(dve.tensor_copy(k_.blocks[:, 0:NX], which[:, :]))
                did(dve.tensor_copy(k_.blocks[:, NX:NX + 1], ends[0:1, NE - 1:NE]))

    def load_piece(self, eng, piece, kind, half, e, first=False):
        j, m = piece
        if not first:
            eng.wait_ge(self.e_lo[m % 3], 2 * j + m // 3 - 1)
        w = self.ins["w_exp_" + kind][0][e].rearrange("(k p) n -> p k n", p=P)
        src = w[:, :, half * HALF:(half + 1) * HALF] if kind == "down" else w[:, 4 * half:4 * half + 4, :]
        eng.dma_start(self.e_raw[m % 6][:, :, :], src).then_inc(self.e_in[m % 6], 16)

    def piece_hi(self, act, piece):
        j, m = piece
        act.wait_ge(self.e_in[m % 6], 16 * (j + m // 6 + 1))
        act.wait_ge(self.e_used[m % 3], 2 * j + m // 3)
        act.activation(self.e_h[m % 3][:, :, :], self.e_raw[m % 6][:, :, :], ACT.Copy).then_inc(self.e_hi[m % 3], 1)

    def piece_lo(self, dve, piece):
        j, m = piece
        dve.wait_ge(self.e_hi[m % 3], 2 * j + m // 3 + 1)
        dve.tensor_tensor(self.e_l[m % 3][:, :, :], self.e_raw[m % 6][:, :, :], self.e_h[m % 3][:, :, :].bitcast(F32),
                          ALU.subtract).then_inc(self.e_lo[m % 3], 1)

    def piece_done(self, eng, piece):
        j, m = piece
        eng.wait_ge(self.e_used[m % 3], 2 * j + m // 3 + 1)

    def piece_products(self, pe, ps, rows_h, rows_l, piece, first_piece, last_piece):
        j, m = piece
        pe.wait_ge(self.e_lo[m % 3], 2 * j + m // 3 + 1)
        w_h, w_l = self.e_h[m % 3], self.e_l[m % 3]
        for k in range(4):
            for x, w, first, last in ((rows_h, w_h, k == 0, False), (rows_h, w_l, False, False),
                                      (rows_l, w_h, False, k == 3)):
                mm = pe.matmul(ps, x[:, k, :], w[:, k, :], start=first and first_piece, stop=last and last_piece)
        mm.then_inc(self.e_used[m % 3], 1)

    def experts(self):
        nc, k_ = self.nc, self
        work = Map(nc, self.act_start, self.work_start)
        k_.e_h = [work.put(f"e_h{s}", [P, 4, HALF], F32R) for s in range(3)]
        k_.e_l = [work.put(f"e_l{s}", [P, 4, HALF], F32R) for s in range(3)]
        xg = [work.put(f"e_xg{b}", [P, D]) for b in range(2)]
        xt_h = [work.put(f"e_xth{b}", [P, KD, P], F32R) for b in range(2)]
        xt_l = [work.put(f"e_xtl{b}", [P, KD, P], F32R) for b in range(2)]
        silu = work.put("e_silu", [P, FE])
        hid = work.put("e_hid", [P, FE])
        y_sb = [work.put(f"e_y{b}", [P, D]) for b in range(2)]
        high = Map(nc, self.x2_end, self.high)
        ht_h = high.put("e_hth", [P, 4, P], F32R)
        ht_l = high.put("e_htl", [P, 4, P], F32R)
        idx = [high.put(f"e_idx{b}", [P, 1], I32) for b in range(2)]
        sem = self.sem
        idx_in, gathered, y_stored = ([sem(f"e_{n}{b}") for b in range(2)] for n in ("idx", "gathered", "stored"))
        x_mm, x_hi, x_lo, silu_out, hid_out, h_mm, h_hi, h_lo, y_out = (
            sem("e_" + n) for n in ("x_mm", "x_hi", "x_lo", "silu", "hid", "h_mm", "h_hi", "h_lo", "y_out"))
        ps_x, ps_g, ps_u = k_.ps[0], k_.ps[1][:, 0:HALF], k_.ps[1][:, HALF:2 * HALF]
        ps_h, ps_y = k_.ps[2][:, 0:HALF], k_.ps[3]
        n_over = MAXX

        def load_slots(pool, j, b):
            pool.dma_start(idx[b][:, :], k_.slots_d[bass.ds(BLK * j, BLK), :]).then_inc(idx_in[b], 16)

        def gather(pool, j, b):
            if not (type(j) is int and j < 2):
                pool.wait_ge(x_mm, j - 1)
            if not (type(j) is int and j < 1):
                pool.wait_ge(gathered[1 - b], 16 * ((j + 1) // 2))
            pool.wait_ge(idx_in[b], 16 * (j // 2 + 1))
            load_slots(pool, j + 1, 1 - b)
            pool.indirect_dma_start(out=xg[b][:, :], out_offset=None, in_=k_.xn_d,
                                    in_offset=bass.IndirectOffsetOnAxis(ap=idx[b][:, 0:1], axis=0))\
                .then_inc(gathered[b], 16)

        def turn_x(pe, j, b):
            pe.wait_ge(gathered[b], 16 * (j // 2 + 1))
            pe.wait_ge(x_lo, j)
            for k in range(KD):
                mm = pe.transpose(ps_x[:, k * P:(k + 1) * P], xg[b][:, k * P:(k + 1) * P], k_.ident[:, :])
            mm.then_inc(x_mm, 1)

        def gate(pe, j, b, half, piece):
            if half == 0:
                pe.wait_ge(x_lo, j + 1)
                pe.wait_ge(silu_out, j)
            ks = slice(4 * half, 4 * half + 4)
            k_.piece_products(pe, ps_g, xt_h[b][:, ks, :], xt_l[b][:, ks, :], piece, half == 0, half == 1)

        def up(pe, j, b, half, piece):
            if half == 0:
                pe.wait_ge(hid_out, j)
            ks = slice(4 * half, 4 * half + 4)
            k_.piece_products(pe, ps_u, xt_h[b][:, ks, :], xt_l[b][:, ks, :], piece, half == 0, half == 1)

        def turn_h(pe, j):
            pe.wait_ge(hid_out, j + 1)
            pe.wait_ge(h_lo, j)
            for k in range(4):
                mm = pe.transpose(ps_h[:, k * P:(k + 1) * P], hid[:, k * P:(k + 1) * P], k_.ident[:, :])
            mm.then_inc(h_mm, 1)

        def down(pe, j, half, piece):
            if half == 0:
                pe.wait_ge(h_lo, j + 1)
                pe.wait_ge(y_out, j)
            k_.piece_products(pe, ps_y[:, half * HALF:(half + 1) * HALF], ht_h, ht_l, piece, True, True)

        def x_high(act, j, b, used):
            act.wait_ge(x_mm, j + 1)
            if used is not None:
                k_.piece_done(act, used)
            act.activation(xt_h[b][:, :, :].rearrange("p k t -> p (k t)"), ps_x[:, :], ACT.Copy).then_inc(x_hi, 1)

        def x_low(dve, j, b):
            dve.wait_ge(x_hi, j + 1)
            dve.tensor_tensor(xt_l[b][:, :, :].rearrange("p k t -> p (k t)"), ps_x[:, :],
                              xt_h[b][:, :, :].rearrange("p k t -> p (k t)").bitcast(F32), ALU.subtract).then_inc(x_lo, 1)

        def act_silu(act, j, gate_piece):
            k_.piece_done(act, gate_piece)
            act.wait_ge(hid_out, j)
            act.activation(silu[:, :], ps_g, ACT.Silu).then_inc(silu_out, 1)

        def hidden(dve, j, up_piece):
            dve.wait_ge(silu_out, j + 1)
            k_.piece_done(dve, up_piece)
            dve.wait_ge(h_mm, j)
            dve.tensor_tensor(hid[:, :], silu[:, :], ps_u, ALU.mult).then_inc(hid_out, 1)

        def h_high(act, j, last_down):
            act.wait_ge(h_mm, j + 1)
            if last_down is not None:
                k_.piece_done(act, last_down)
            act.activation(ht_h[:, :, :].rearrange("p k t -> p (k t)"), ps_h, ACT.Copy).then_inc(h_hi, 1)

        def h_low(dve, j):
            dve.wait_ge(h_hi, j + 1)
            dve.tensor_tensor(ht_l[:, :, :].rearrange("p k t -> p (k t)"), ps_h,
                              ht_h[:, :, :].rearrange("p k t -> p (k t)").bitcast(F32), ALU.subtract).then_inc(h_lo, 1)

        def rows_out(act, j, b, down_piece):
            k_.piece_done(act, down_piece)
            act.wait_ge(y_stored[b], 16 * (j // 2))
            act.activation(y_sb[b][:, :], ps_y[:, :], ACT.Copy).then_inc(y_out, 1)
            act.wait_ge(y_out, j + 1)
            act.dma_start(k_.y_d[bass.ds(BLK * j, BLK), :], y_sb[b][:, :]).then_inc(y_stored[b], 16)

        def in_pairs(engine, body, from_pair, to_pair):
            with engine.Fori(from_pair, to_pair) as i:
                for b in range(2):
                    body(2 * i + b, b)

        def beyond(engine, body):
            n = engine.value_load(k_.blocks[0:1, n_over:n_over + 1], min_val=0, max_val=MAXX)
            with engine.Fori(0, MAXX // 2) as i:
                for b in range(2):
                    with engine.If(2 * i + b < n):
                        body(NE + 2 * i + b, b, 2 * i + b)
            return n

        listed = lambda engine, at, most: engine.value_load(k_.blocks[0:1, bass.ds(at, 1)], min_val=0, max_val=most)

        with nc.Block() as block:
            @block.sync
            def _(sp):
                def body(j, b, last=False):
                    for m, kind, half, e in ((6, "down", 0, j), (7, "down", 1, j), (8, "up", 0, j + 1), (9, "up", 1, j + 1),
                                             (10, "gate", 0, j + 2), (11, "gate", 1, j + 2)):
                        if not (last and m > 9):
                            k_.load_piece(sp, (j, m), kind, half, e)
                in_pairs(sp, body, 0, NE // 2 - 1)
                body(NE - 2, 0, True)
                for m in (4, 5):
                    k_.load_piece(sp, (NE - 1, m), "down", m - 4, NE - 1)

                def other(j, b, t):
                    e = listed(sp, t, NE - 1)
                    for m in range(6):
                        k_.load_piece(sp, (j, m), ("gate", "up", "down")[m // 2], m % 2, e)
                beyond(sp, other)

            @block.gpsimd
            def _(pool):
                load_slots(pool, 0, 0)
                gather(pool, 0, 0)
                gather(pool, 1, 1)
                in_pairs(pool, lambda j, b: gather(pool, j, b), 1, NE // 2)
                n = beyond(pool, lambda j, b, t: gather(pool, j, b))
                pool.wait_ge(y_stored[0], 16 * (NE // 2 + (n + 1) // 2))
                pool.wait_ge(y_stored[1], 16 * (NE // 2 + n // 2))
                pool.wait_ge(idx_in[0], 16 * (NE // 2 + n // 2 + 1))
                pool.wait_ge(idx_in[1], 16 * (NE // 2 + (n + 1) // 2))

            @block.tensor
            def _(pe):
                turn_x(pe, 0, 0)
                for h in range(2):
                    gate(pe, 0, 0, h, (0, h))

                def body(j, b):
                    up(pe, j, b, 0, (j, 2))
                    turn_x(pe, j + 1, 1 - b)
                    up(pe, j, b, 1, (j, 3))
                    gate(pe, j + 1, 1 - b, 0, (j, 4))
                    turn_h(pe, j)
                    gate(pe, j + 1, 1 - b, 1, (j, 5))
                    for h in range(2):
                        down(pe, j, h, (j, 6 + h))
                in_pairs(pe, body, 0, NE // 2 - 1)
                body(NE - 2, 0)
                j = NE - 1
                for h in range(2):
                    up(pe, j, 1, h, (j, 2 + h))
                turn_h(pe, j)
                for h in range(2):
                    down(pe, j, h, (j, 4 + h))

                def other(j, b, t):
                    turn_x(pe, j, b)
                    for h in range(2):
                        gate(pe, j, b, h, (j, h))
                    for h in range(2):
                        up(pe, j, b, h, (j, 2 + h))
                    turn_h(pe, j)
                    for h in range(2):
                        down(pe, j, h, (j, 4 + h))
                beyond(pe, other)

            @block.scalar
            def _(act):
                k_.piece_hi(act, (0, 0))
                x_high(act, 0, 0, None)
                for m in (1, 2, 3):
                    k_.piece_hi(act, (0, m))

                def body(j, b, first=False):
                    act_silu(act, j, (j - 1, 5) if not first else (0, 1))
                    k_.piece_hi(act, (j, 4))
                    x_high(act, j + 1, 1 - b, (j - 1, 3) if not first else None)
                    for m in (5, 6):
                        k_.piece_hi(act, (j, m))
                    h_high(act, j, (j - 1, 7) if not first else None)
                    for m in (7, 8, 9):
                        k_.piece_hi(act, (j, m))
                    rows_out(act, j, b, (j, 7))
                body(0, 0, True)
                body(1, 1)
                in_pairs(act, body, 1, NE // 2 - 1)
                body(NE - 2, 0)
                j = NE - 1
                act_silu(act, j, (j - 1, 5))
                for m in (4, 5):
                    k_.piece_hi(act, (j, m))
                h_high(act, j, (j - 1, 7))
                rows_out(act, j, 1, (j, 5))

                def other(j, b, t):
                    k_.piece_hi(act, (j, 0))
                    x_high(act, j, b, (j - 1, 3))
                    for m in (1, 2, 3):
                        k_.piece_hi(act, (j, m))
                    act_silu(act, j, (j, 1))
                    for m in (4, 5):
                        k_.piece_hi(act, (j, m))
                    h_high(act, j, (j - 1, 5))
                    rows_out(act, j, b, (j, 5))
                beyond(act, other)

            @block.vector
            def _(dve):
                k_.piece_lo(dve, (0, 0))
                x_low(dve, 0, 0)
                for m in (1, 2, 3):
                    k_.piece_lo(dve, (0, m))

                def body(j, b):
                    k_.piece_lo(dve, (j, 4))
                    x_low(dve, j + 1, 1 - b)
                    k_.piece_lo(dve, (j, 5))
                    hidden(dve, j, (j, 3))
                    k_.piece_lo(dve, (j, 6))
                    h_low(dve, j)
                    for m in (7, 8, 9):
                        k_.piece_lo(dve, (j, m))
                in_pairs(dve, body, 0, NE // 2 - 1)
                body(NE - 2, 0)
                j = NE - 1
                k_.piece_lo(dve, (j, 4))
                hidden(dve, j, (j, 3))
                k_.piece_lo(dve, (j, 5))
                h_low(dve, j)

                def other(j, b, t):
                    k_.piece_lo(dve, (j, 0))
                    x_low(dve, j, b)
                    for m in (1, 2, 3, 4):
                        k_.piece_lo(dve, (j, m))
                    hidden(dve, j, (j, 3))
                    k_.piece_lo(dve, (j, 5))
                    h_low(dve, j)
                beyond(dve, other)

    def combine(self):
        nc, k_ = self.nc, self
        work = Map(nc, self.fixed_end, self.work_start)
        RING = 4
        yg = [[work.put(f"cb_y{r}{s}", [P, D]) for s in range(2)] for r in range(RING)]
        ob = [work.put(f"cb_o{b}", [P, D]) for b in range(2)]
        g_b, square = work.put("cb_g", [P, D]), work.put("cb_square", [P, D])
        total, mean, rstd, power = (work.put(f"cb_{n}", [P, NT]) for n in ("total", "mean", "rstd", "power"))
        sem = self.sem
        got = [[sem(f"cb_got{r}{s}") for s in range(2)] for r in range(RING)]
        g_in, const, first, added, squared, averaged, powered, normed = (
            sem("cb_" + n) for n in ("g", "const", "first", "added", "squared", "averaged", "powered", "normed"))
        stored = [sem(f"cb_stored{b}") for b in range(2)]

        with nc.Block() as block:
            @block.gpsimd
            def _(pool):
                pool.memset(power[:, :], -0.5).then_inc(const, 1)
                pool.wait_ge(const, 1)

                def root(t):
                    pool.wait_ge(averaged, t + 1)
                    pool.tensor_tensor(rstd[:, t:t + 1], mean[:, t:t + 1], power[:, t:t + 1], ALU.pow).then_inc(powered, 1)
                for t in range(NT):
                    if t >= RING:
                        pool.wait_ge(added, t - RING + 1)
                    for s in range(2):
                        pool.indirect_dma_start(
                            out=yg[t % RING][s][:, :], out_offset=None, in_=k_.y_d,
                            in_offset=bass.IndirectOffsetOnAxis(ap=k_.dest[:, s, t:t + 1], axis=0))\
                            .then_inc(got[t % RING][s], 16)
                    if t >= RING - 1:
                        root(t - RING + 1)
                for t in range(NT - RING + 1, NT):
                    root(t)

            @block.sync
            def _(sp):
                sp.dma_start(g_b[:, :], k_.ins["g_final"].partition_broadcast(P)).then_inc(g_in, 16)
                for t in range(NT):
                    sp.wait_ge(normed, t + 1)
                    sp.dma_start(k_.out[t * P:(t + 1) * P, :], ob[t % 2][:, :]).then_inc(stored[t % 2], 16)
                for b in range(2):
                    sp.wait_ge(stored[b], 16 * NT // 2)

            @block.scalar
            def _(act):
                for t in range(NT):
                    act.wait_ge(added, t + 1)
                    act.activation(square[:, :], k_.x2[:, t, :], ACT.Square, accum_out=total[:, t:t + 1]).then_inc(squared, 1)
                    act.wait_ge(squared, t + 1)

            @block.vector
            def _(dve):
                def norm(t):
                    dve.wait_ge(powered, t + 1)
                    if t >= 2:
                        dve.wait_ge(stored[t % 2], 16 * (t // 2))
                    dve.scalar_tensor_tensor(out=ob[t % 2][:, :], in0=k_.x2[:, t, :], scalar=rstd[:, t:t + 1],
                                             in1=g_b[:, :], op0=ALU.mult, op1=ALU.mult).then_inc(normed, 1)
                dve.wait_ge(g_in, 16)
                for t in range(NT):
                    x2 = k_.x2[:, t, :]
                    for s in range(2):
                        dve.wait_ge(got[t % RING][s], 16 * (t // RING + 1))
                        dve.scalar_tensor_tensor(out=x2, in0=yg[t % RING][s][:, :], scalar=k_.wgt[:, s, t:t + 1], in1=x2,
                                                 op0=ALU.mult, op1=ALU.add).then_inc((first, added)[s], 1)
                        if s == 0:
                            dve.wait_ge(first, t + 1)
                    if t >= 1:
                        norm(t - 1)
                    dve.wait_ge(squared, t + 1)
                    dve.tensor_scalar(mean[:, t:t + 1], total[:, t:t + 1], 1.0 / D, EPS, ALU.mult, ALU.add)\
                        .then_inc(averaged, 1)
                norm(NT - 1)

    def write(self):
        for write, *args in ((self.norm_in,), (self.lru,), (self.qk,), (self.value,), (self.merge_gates,),
                             (self.branch_out, 0), (self.attention,), (self.branch_out, 1), (self.project,),
                             (self.route,), (self.experts,), (self.combine,)):
            self.stage(write, *args)


NAMES = ("x", "g_mix", "w_in", "conv_w", "conv_b", "w_rg_a", "b_rg_a", "w_rg_x", "b_rg_x", "lru_lambda", "b_forget",
         "w_lru_out", "w_attn_out", "w_out", "g_ffn", "w_route_group", "b_route_group", "w_route_expert",
         "b_route_expert", "w_exp_gate", "w_exp_up", "w_exp_down", "g_final")


def kernel(**inputs):
    import numpy as np
    import concourse.bacc as bacc
    from concourse.bass_utils import run_bass_kernel_spmd

    nc = bacc.Bacc("TRN2", target_bir_lowering=False, num_devices=1)
    arrays = {name: np.ascontiguousarray(inputs[name]) for name in NAMES}
    ins = {name: nc.dram_tensor(name, a.shape, mybir.dt.from_np(a.dtype), kind="ExternalInput").ap()
           for name, a in arrays.items()}
    out = nc.dram_tensor("out", (T, D), F32, kind="ExternalOutput").ap()
    Kernel(nc, ins, out).write()
    result = run_bass_kernel_spmd(nc, [arrays], core_ids=[0])
    return result.results[0]["out"].reshape(1, T, D)
```

```python
import concourse.bass as bass
from concourse import mybir

F32 = mybir.dt.float32
F32R = mybir.dt.float32r
I32 = mybir.dt.int32
U32 = mybir.dt.uint32
ALU = mybir.AluOpType
ACT = mybir.ActivationFunctionType
AX = mybir.AxisListType

P = 128
D = 1024
T = 1024
KD = D // P
NT = T // P
HALF = 512
NH = 8
HD = D // NH
WB = 256
CONV_W = 4
LRU_C = 8.0
EPS = 1e-6
NG = 4
EG = 8
NE = NG * EG
FE = 512
XR, GR, QC, KC, VC, FL, ML, MA = 0, D, 2 * D, 3 * D, 4 * D, 5 * D, 5 * D + NH, 6 * D + NH
NEG = -3.0e38
PW, PB, PBA, PBX, PS, PN, NPRM = 0, 4, 5, 6, 7, 8, 9
BLK = 128
MAXX = 2 * T // BLK
SLOTS = (NE + MAXX) * BLK


class Map:

    def __init__(self, nc, start, end):
        self.nc, self.at, self.end = nc, start, end

    def put(self, name, shape, dt=F32):
        size = 4
        for n in shape[1:]:
            size *= n
        place = self.nc.alloc_sbuf_tensor_at(name, shape, dt, offset=self.at)
        self.at += (size + 31) // 32 * 32
        assert self.at <= self.end, (name, self.at, self.end)
        return place


class Steps:

    def __init__(self, engine, sem, start=0):
        self.engine, self.sem, self.start, self.n = engine, sem, start, 0

    def did(self, instruction):
        instruction.then_inc(self.sem, 1)
        self.n += 1
        self.engine.wait_ge(self.sem, self.start + self.n)


class Kernel:
    def __init__(self, nc, ins, out):
        self.nc, self.out = nc, out
        self.x, self.g_mix, self.w_in = ins["x"][0], ins["g_mix"][0], ins["w_in"][0]
        self.ins = ins
        dram = lambda name, shape, dt=F32: nc.dram_tensor(name, shape, dt).ap()
        self.qk_d = dram("qk_d", (NH, P, 4, T))
        self.v_d = dram("v_d", (NH // 2, 2, P, NT, WB))
        self.sig_d = dram("sig_d", (2, KD, P, T))
        self.c_d = dram("c_d", (NH, 2, 4, T))
        self.o_d = dram("o_d", (NH, P, T))
        self.xn_d = dram("xn_d", (T, D))
        self.slots_d = dram("slots_d", (SLOTS + BLK, 1), I32)
        self.y_d = dram("y_d", (SLOTS, D))
        self.stage_sems = []
        low, high = (nc.SBUF_PARTITION_SIZE_BYTES - nc.sbuf_bytes_remaining + 31) // 32 * 32, nc.sbuf_usable_end
        fixed = Map(nc, low, high)
        self.ident = fixed.put("ident", [P, P])
        self.ones = fixed.put("ones", [P, P])
        self.zeros = fixed.put("zeros", [P, P])
        self.stri = fixed.put("stri", [P, P])
        self.gm = fixed.put("gm", [P, KD])
        self.prm = fixed.put("prm", [P, KD, NPRM])
        self.wgt = fixed.put("wgt", [P, 2, NT])
        self.dest = fixed.put("dest", [P, 2, NT], I32)
        self.blocks = fixed.put("blocks", [1, 32], I32)
        mixer = Map(nc, fixed.at, high)
        low = fixed.at
        self.w_raw = [mixer.put(f"w_raw{s}", [P, KD, WB]) for s in range(2)]
        self.w_h = [mixer.put(f"w_h{s}", [P, KD, WB], F32R) for s in range(2)]
        self.w_l = [Map(nc, low + s * 4 * KD * WB, high).put(f"w_l{s}", [P, KD, WB], F32R) for s in range(2)]
        self.act_start, self.high, self.fixed_end = mixer.at, high, fixed.at
        self.uh = mixer.put("uh", [P, KD, T], F32R)
        self.ul = mixer.put("ul", [P, KD, T], F32R)
        self.mix = mixer.put("mix", [P, KD, T])
        self.work_start = mixer.at
        self.w_loaded = [self.sem(f"w_loaded{s}") for s in range(2)]
        self.w_hi = [self.sem(f"w_hi{s}") for s in range(2)]
        self.w_lo = [self.sem(f"w_lo{s}") for s in range(2)]
        self.w_first = [self.sem(f"w_first{s}") for s in range(2)]
        self.w_used = [self.sem(f"w_used{s}") for s in range(2)]
        self.pairs = 0
        self.e_in = [self.sem(f"e_in{r}") for r in range(6)]
        self.e_hi, self.e_lo, self.e_used = ([self.sem(f"e_{n}{s}") for s in range(3)] for n in ("hi", "lo", "used"))
        stores = lambda name: [self.sem(f"{name}_stored{c}") for c in range(2)]
        self.qk_stored, self.v_stored, self.o_stored = stores("qk"), stores("v"), stores("o")
        self.sig_stored = [stores(f"sig{s}") for s in range(2)]
        self.rows_stored = self.sem("c_stored")
        self.qk_in, self.v_in, self.c_in = ([self.sem(f"at_{n}_in{c}") for c in range(2)] for n in ("qk", "v", "c"))
        self.ps = [nc.alloc_psum_tensor(f"ps{t}", [P, 2 * HALF], F32) for t in range(4)]

    def sem(self, name):
        self.stage_sems.append(self.nc.alloc_semaphore(name))
        return self.stage_sems[-1]

    def stage(self, write, *args):
        self.stage_sems = []
        write(*args)
        self.nc.clear_and_free_semaphores(self.stage_sems)
        self.nc.all_engine_barrier(sem_only=True)

    def work(self):
        return Map(self.nc, self.work_start, self.high)

    def load_block(self, eng, s, p, src):
        if type(p) is not int or p > 0:
            eng.wait_ge(self.w_used[s], p)
        eng.dma_start(self.w_raw[s][:, :, :], src).then_inc(self.w_loaded[s], 16)

    def split_hi(self, act, s, p):
        act.wait_ge(self.w_loaded[s], 16 * (p + 1))
        act.wait_ge(self.w_used[s], p)
        act.activation(self.w_h[s][:, :, :], self.w_raw[s][:, :, :], ACT.Copy).then_inc(self.w_hi[s], 1)

    def split_lo(self, dve, s, p):
        dve.wait_ge(self.w_hi[s], p + 1)
        dve.tensor_tensor(self.w_l[s][:, :, :], self.w_raw[s][:, :, :], self.w_h[s][:, :, :].bitcast(F32),
                          ALU.subtract).then_inc(self.w_lo[s], 1)

    def w_block(self, w, col):
        return w.rearrange("(k p) n -> p k n", p=P)[:, :, bass.ds(col, WB)]

    def product(self, pe, ps, s, c, chunks_in=None):
        wh, wl = (w[s][:, :, c * P:(c + 1) * P] for w in (self.w_h, self.w_l))
        for k in range(KD):
            if chunks_in is not None:
                pe.wait_ge(chunks_in, k + 1)
            for w, u, first, last in ((wh, self.uh, k == 0, False), (wh, self.ul, False, False),
                                      (wl, self.uh, False, k == KD - 1)):
                for h in range(2):
                    mm = pe.matmul(ps[:, h * HALF:(h + 1) * HALF], w[:, k, :], u[:, k, h * HALF:(h + 1) * HALF],
                                   start=first, stop=last)
        return mm

    def product_rows(self, pe, ps, s, tile, chunks_in=None):
        rows = slice(tile * P, (tile + 1) * P)
        for k in range(KD):
            if chunks_in is not None:
                pe.wait_ge(chunks_in, k + 1)
            for u, w, first, last in ((self.uh, self.w_h, k == 0, False), (self.uh, self.w_l, False, False),
                                      (self.ul, self.w_h, False, k == KD - 1)):
                mm = pe.matmul(ps, u[:, k, rows], w[s][:, k, :], start=first, stop=last)
        return mm

    def norm_in(self):
        nc, k_ = self.nc, self
        work = self.work()
        square = work.put("na_square", [P, D])
        total = work.put("na_total", [P, NT])
        mean = work.put("na_mean", [P, NT])
        rstd = work.put("na_rstd", [P, NT])
        power = work.put("na_power", [P, NT])
        rows = work.put("na_rows", [P, P])
        e, w1, dw, ln, eq = (work.put(f"na_{n}", [P, KD]) for n in ("e", "w1", "dw", "ln", "eq"))
        x_loaded = [self.sem(f"na_x{t}") for t in range(NT)]
        prm_loaded, prm_mm, prm_turned = self.sem("na_prm"), self.sem("na_prm_mm"), self.sem("na_prm_turned")
        consts = self.sem("na_consts")
        squared, averaged, powered, scaled = (self.sem(f"na_{n}") for n in ("squared", "averaged", "powered", "scaled"))
        turned, high, low = self.sem("na_turned"), self.sem("na_high"), self.sem("na_low")
        sp_exp, sp_one, sp_ln, own = (self.sem(f"na_{n}") for n in ("sp_exp", "sp_one", "sp_ln", "own"))
        xt = self.mix
        ins = self.ins
        vectors = [ins["conv_w"][0, j] for j in range(CONV_W)] + \
                  [ins[n][0] for n in ("conv_b", "b_rg_a", "b_rg_x", "lru_lambda", "g_mix")]
        turn = k_.ps[3][:, HALF:HALF + P]
        turn_v = turn.rearrange("p (v k) -> p k v", k=KD)

        with nc.Block() as block:
            @block.sync
            def _(sp):
                for t in range(NT):
                    sp.dma_start(xt[:, t, :], k_.x[t * P:(t + 1) * P, :]).then_inc(x_loaded[t], 16)
                for s, col in enumerate((XR, GR)):
                    k_.load_block(sp, s, 0, k_.w_block(k_.w_in, col))

            @block.scalar
            def _(act):
                act.wait_ge(consts, 3)
                for v, src in enumerate(vectors):
                    act.dma_start(rows[v * KD:(v + 1) * KD, :], src.rearrange("(k p) -> k p", p=P))\
                        .then_inc(prm_loaded, 16)
                for t in range(NT):
                    act.wait_ge(x_loaded[t], 16)
                    act.activation(square[:, :], xt[:, t, :], ACT.Square,
                                   accum_out=total[:, t:t + 1]).then_inc(squared, 1)
                    act.wait_ge(squared, t + 1)
                act.wait_ge(prm_turned, 2)
                act.activation(e[:, :], k_.prm[:, :, PS], ACT.Exp, scale=-1.0).then_inc(sp_exp, 1)
                act.wait_ge(sp_one, 1)
                act.activation(ln[:, :], w1[:, :], ACT.Ln).then_inc(sp_ln, 1)
                k_.split_hi(act, 0, 0)
                for h in range(2):
                    for k in range(KD):
                        act.wait_ge(turned, h * KD + k + 1)
                        act.activation(k_.uh[:, k, h * HALF:(h + 1) * HALF], k_.ps[k % 4][:, 0:HALF], ACT.Copy,
                                       scale=k_.gm[:, k:k + 1]).then_inc(high, 1)

            @block.gpsimd
            def _(pool):
                pool.memset(power[:, :], -0.5).then_inc(consts, 1)
                pool.memset(k_.ones[:, :], 1.0).then_inc(consts, 1)
                pool.memset(rows[:, :], 0.0).then_inc(consts, 1)
                pool.wait_ge(consts, 3)
                pool.affine_select(out=k_.ident[:, :], in_=k_.ones[:, :], compare_op=ALU.is_equal, fill=0.0,
                                   base=0, pattern=[[-1, P]], channel_multiplier=1).then_inc(consts, 1)
                pool.affine_select(out=k_.stri[:, :], in_=k_.ones[:, :], compare_op=ALU.is_gt, fill=0.0,
                                   base=0, pattern=[[1, P]], channel_multiplier=-1).then_inc(consts, 1)
                pool.wait_ge(averaged, 1)
                pool.tensor_tensor(rstd[:, :], mean[:, :], power[:, :], ALU.pow).then_inc(powered, 1)

            @block.tensor
            def _(pe):
                pe.wait_ge(consts, 5)
                pe.wait_ge(prm_loaded, 16 * len(vectors))
                pe.transpose(turn, rows[:, :], k_.ident[:, :]).then_inc(prm_mm, 1)
                for h in range(2):
                    pe.wait_ge(scaled, 4 * h + 4)
                    for k in range(KD):
                        n = h * KD + k
                        if n >= 4:
                            pe.wait_ge(low, n - 3)
                        for t in range(4):
                            mm = pe.transpose(k_.ps[k % 4][:, t * P:(t + 1) * P],
                                              xt[:, 4 * h + t, k * P:(k + 1) * P], k_.ident[:, :])
                        mm.then_inc(turned, 1)

            @block.vector
            def _(dve):
                steps = Steps(dve, own)
                dve.wait_ge(prm_mm, 1)
                dve.tensor_copy(k_.prm[:, :, 0:PN], turn_v[:, :, 0:PN]).then_inc(prm_turned, 1)
                dve.tensor_copy(k_.gm[:, :], turn[:, PN * KD:(PN + 1) * KD]).then_inc(prm_turned, 1)
                dve.wait_ge(sp_exp, 1)
                dve.tensor_scalar(w1[:, :], e[:, :], 1.0, None, ALU.add).then_inc(sp_one, 1)
                dve.wait_ge(sp_one, 1)
                steps.did(dve.tensor_scalar(dw[:, :], w1[:, :], -1.0, None, ALU.add))
                steps.did(dve.tensor_scalar(eq[:, :], dw[:, :], 0.0, None, ALU.is_equal))
                steps.did(dve.tensor_tensor(dw[:, :], dw[:, :], eq[:, :], ALU.add))
                steps.did(dve.reciprocal(dw[:, :], dw[:, :]))
                dve.wait_ge(sp_ln, 1)
                steps.did(dve.tensor_tensor(eq[:, :], eq[:, :], ln[:, :], ALU.add))
                steps.did(dve.tensor_tensor(eq[:, :], eq[:, :], dw[:, :], ALU.mult))
                steps.did(dve.tensor_tensor(eq[:, :], eq[:, :], e[:, :], ALU.mult))
                dve.tensor_scalar(k_.prm[:, :, PS], eq[:, :], LRU_C / 2, None, ALU.mult).then_inc(own, 1)
                dve.tensor_scalar(k_.prm[:, :, PN], eq[:, :], -LRU_C, None, ALU.mult).then_inc(own, 1)
                dve.wait_ge(squared, NT)
                dve.tensor_scalar(mean[:, :], total[:, :], 1.0 / D, EPS, ALU.mult, ALU.add).then_inc(averaged, 1)
                k_.split_lo(dve, 0, 0)
                dve.wait_ge(powered, 1)
                for t in range(NT):
                    dve.tensor_scalar(xt[:, t, :], xt[:, t, :], rstd[:, t:t + 1], None, ALU.mult).then_inc(scaled, 1)
                for h in range(2):
                    for k in range(KD):
                        dve.wait_ge(high, h * KD + k + 1)
                        dve.scalar_tensor_tensor(out=k_.ul[:, k, h * HALF:(h + 1) * HALF],
                                                 in0=k_.ps[k % 4][:, 0:HALF], scalar=k_.gm[:, k:k + 1],
                                                 in1=k_.uh[:, k, h * HALF:(h + 1) * HALF].bitcast(F32),
                                                 op0=ALU.mult, op1=ALU.subtract).then_inc(low, 1)

    def lru_qk(self):
        nc, k_ = self.nc, self
        turns = D // WB
        p0, self.pairs = self.pairs, self.pairs + 2 * turns
        work = self.work()
        rg_raw = work.put("rg_raw", [P, 2, 2, WB])
        rg_h = work.put("rg_h", [P, 2, 2, WB], F32R)
        rg_l = work.put("rg_l", [P, 2, 2, WB], F32R)
        cur = work.put("lru_prm", [P, 2, NPRM])
        pad = CONV_W - 1
        xr = work.put("lru_xr", [P, 2, T + 8])
        xc = work.put("lru_xc", [P, 2, T])
        xc_h = work.put("lru_xch", [P, 2, T], F32R)
        xc_l = work.put("lru_xcl", [P, 2, T], F32R)
        root_at = work.at - 2 * (2 * T * 4)
        rt_sb = Map(nc, root_at, work.at).put("lru_rt", [P, 2, T])
        a_sb = work.put("lru_a", [P, 2, T])
        i_sb = xr[:, :, pad:pad + T]
        gl = work.put("lru_gl", [P, 2, T])
        st = [work.put(f"qk_{c}", [P, 2, T], F32R) for c in range(2)]
        SCALE = (1.0, HD ** -0.5)
        sem = self.sem
        rg_loaded, rg_hi, rg_lo = (sem(f"rg_{n}") for n in ("loaded", "hi", "lo"))
        xr_out = [sem(f"lru_xr_out{c}") for c in range(2)]
        gr_out = [sem(f"lru_gr_out{c}") for c in range(2)]
        qk_hi, qk_lo = ([[sem(f"qk_{n}{g}{c}") for c in range(2)] for g in range(2)] for n in ("hi", "lo"))
        qk_stored = k_.qk_stored
        conv, xch_done, xcl_done = (sem(f"lru_{n}") for n in ("conv", "xch", "xcl"))
        gate_mm = [sem(f"lru_gate_mm{g}") for g in range(2)]
        gate_out = [sem(f"lru_gate_out{g}") for g in range(2)]
        t_done, a_done, root, mixed, own = (sem(f"lru_{n}") for n in ("t", "a", "root", "mixed", "own"))
        w_a, w_x = (self.ins[n][0].rearrange("b (c p) n -> b p c n", p=P) for n in ("w_rg_a", "w_rg_x"))
        zeroed, cleared, filled = sem("lru_zeroed"), sem("lru_cleared"), sem("lru_filled")
        zeros = self.zeros
        w_c = (k_.w_first, k_.w_used)

        with nc.Block() as block:
            @block.sync
            def _(sp):
                def gates(i):
                    sp.wait_ge(rg_lo, i)
                    for g, w in enumerate((w_a, w_x)):
                        sp.dma_start(rg_raw[:, g, :, :], w[i]).then_inc(rg_loaded, 16)

                def store(i, g, c):
                    sp.wait_ge(qk_lo[g][c], i + 1)
                    part = 2 - 2 * g
                    head = 2 * i + c if g == 0 else i + i + c
                    sp.dma_start(k_.qk_d[head][:, part:part + 2, :], st[c][:, :, :].bitcast(F32))\
                        .then_inc(qk_stored[c], 16)

                def turn(i, last):
                    for s, col in enumerate((KC, QC)):
                        k_.load_block(sp, s, p0 + 2 * i + 1, k_.w_block(k_.w_in, col + WB * i))
                    if not last:
                        gates(i + 1)
                    for s, col in enumerate((XR, GR)):
                        store(i, s, 0)
                        k_.load_block(sp, s, p0 + 2 * i + 2, k_.w_block(k_.w_in, VC + WB * s if last else col + WB + WB * i))
                        store(i, s, 1)
                gates(0)
                with sp.Fori(0, turns - 1) as i:
                    turn(i, False)
                turn(turns - 1, True)

            @block.gpsimd
            def _(pool):
                pool.memset(xr[:, :, 0:pad], 0.0).then_inc(zeroed, 1)
                pool.memset(zeros[:, :], 0.0).then_inc(cleared, 1)
                pool.wait_ge(cleared, 1)
                with pool.Fori(0, MAXX) as j:
                    pool.dma_start(k_.y_d[bass.ds(NE * BLK + BLK * j, BLK), :].rearrange("p (a n) -> p a n", n=P),
                                   zeros[:, :].unsqueeze(1).to_broadcast([P, D // P, P])).then_inc(filled, 16)
                pool.wait_ge(filled, 16 * MAXX)

            @block.tensor
            def _(pe):
                def products(i, s, pair, read, count):
                    pe.wait_ge(k_.w_lo[s], p0 + 2 * i + pair + 1)
                    for c in range(2):
                        pe.wait_ge(read[c], count)
                        k_.product(pe, k_.ps[c], s, c).then_inc(w_c[c][s], 1)

                with pe.Fori(0, turns) as i:
                    products(i, 0, 0, qk_lo[1], i)
                    products(i, 1, 0, xr_out, i + 1)
                    pe.wait_ge(rg_lo, i + 1)
                    pe.wait_ge(xcl_done, 2 * i + 2)
                    for m in range(2):
                        for g in range(2):
                            pe.wait_ge(gate_out[g], 2 * i + m)
                            for kk in range(2):
                                for w, u, first, last in ((rg_h, xc_h, kk == 0, False), (rg_h, xc_l, False, False),
                                                          (rg_l, xc_h, False, kk == 1)):
                                    for h in range(2):
                                        mm = pe.matmul(k_.ps[2 + g][:, h * HALF:(h + 1) * HALF],
                                                       w[:, g, kk, m * P:(m + 1) * P],
                                                       u[:, kk, h * HALF:(h + 1) * HALF], start=first, stop=last)
                            mm.then_inc(gate_mm[g], 1)
                    products(i, 0, 1, gr_out, i + 1)
                    products(i, 1, 1, qk_lo[0], i + 1)

            @block.scalar
            def _(act):
                def xr_copy(i, c):
                    act.wait_ge(w_c[c][0], p0 + 2 * i + 1)
                    act.activation(xr[:, c, pad:pad + T], k_.ps[c][:, :], ACT.Copy).then_inc(xr_out[c], 1)

                def conv_high(i, c):
                    act.wait_ge(conv, 2 * i + c + 1)
                    act.activation(xc_h[:, c, :], xc[:, c, :], ACT.Copy).then_inc(xch_done, 1)

                def gelu(i, c):
                    act.wait_ge(w_c[c][1], p0 + 2 * i + 1)
                    act.activation(gl[:, c, :], k_.ps[c][:, :], ACT.Gelu_apprx_tanh).then_inc(gr_out[c], 1)

                def qk_high(i, g, c):
                    act.wait_ge(w_c[c][g], p0 + 2 * i + 2)
                    act.wait_ge(qk_stored[c], 16 * (2 * i + g))
                    act.activation(st[c][:, 0, :], k_.ps[c][:, :], ACT.Copy, scale=SCALE[g]).then_inc(qk_hi[g][c], 1)

                with act.Fori(0, turns) as i:
                    k_.split_hi(act, 1, p0 + 2 * i)
                    act.wait_ge(mixed, 2 * i)
                    xr_copy(i, 0)
                    act.wait_ge(rg_loaded, 32 * (i + 1))
                    act.wait_ge(gate_mm[1], 2 * i)
                    act.activation(rg_h[:, :, :, :], rg_raw[:, :, :, :], ACT.Copy).then_inc(rg_hi, 1)
                    conv_high(i, 0)
                    xr_copy(i, 1)
                    k_.split_hi(act, 0, p0 + 2 * i + 1)
                    conv_high(i, 1)
                    for c in range(2):
                        gelu(i, c)
                    for m in range(2):
                        act.wait_ge(gate_mm[0], 2 * i + m + 1)
                        act.activation(a_sb[:, m, :], k_.ps[2][:, :], ACT.Sigmoid, bias=cur[:, m, PBA:PBA + 1])\
                            .then_inc(gate_out[0], 1)
                        act.wait_ge(gate_mm[1], 2 * i + m + 1)
                        act.activation(i_sb[:, m, :], k_.ps[3][:, :], ACT.Sigmoid, bias=cur[:, m, PBX:PBX + 1])\
                            .then_inc(gate_out[1], 1)
                    for m in range(2):
                        act.wait_ge(gate_out[0], 2 * i + m + 1)
                        act.activation(rt_sb[:, m, :], a_sb[:, m, :], ACT.Tanh, scale=cur[:, m, PS:PS + 1])\
                            .then_inc(t_done, 1)
                    for m in range(2):
                        act.wait_ge(t_done, 2 * i + m + 1)
                        act.activation(a_sb[:, m, :], a_sb[:, m, :], ACT.Exp, scale=cur[:, m, PN:PN + 1])\
                            .then_inc(a_done, 1)
                    act.activation(rt_sb[:, :, :], rt_sb[:, :, :], ACT.Sqrt).then_inc(root, 1)
                    k_.split_hi(act, 1, p0 + 2 * i + 1)
                    for c in range(2):
                        qk_high(i, 0, c)
                    k_.split_hi(act, 0, p0 + 2 * i + 2)
                    for c in range(2):
                        qk_high(i, 1, c)

            @block.vector
            def _(dve):
                PER = 15

                def qk_low(i, g, c):
                    dve.wait_ge(qk_hi[g][c], i + 1)
                    dve.scalar_tensor_tensor(out=st[c][:, 1, :], in0=k_.ps[c][:, :], scalar=SCALE[g],
                                             in1=st[c][:, 0, :].bitcast(F32), op0=ALU.mult,
                                             op1=ALU.subtract).then_inc(qk_lo[g][c], 1)

                dve.wait_ge(zeroed, 1)
                with dve.Fori(0, turns) as i:
                    steps = Steps(dve, own, i * PER)
                    dve.wait_ge(a_done, 2 * i)
                    steps.did(dve.tensor_scalar(cur[:, :, :], k_.prm[:, bass.ds(2 * i, 2), :], 1.0, None, ALU.mult))
                    k_.split_lo(dve, 1, p0 + 2 * i)
                    for c in range(2):
                        dve.wait_ge(xr_out[c], i + 1)
                        w = lambda j: cur[:, c, PW + j:PW + j + 1]
                        steps.did(dve.tensor_scalar(xc[:, c, :], xr[:, c, 0:T], w(0), cur[:, c, PB:PB + 1],
                                                    ALU.mult, ALU.add))
                        for j in range(1, CONV_W):
                            op = dve.scalar_tensor_tensor(out=xc[:, c, :], in0=xr[:, c, j:j + T], scalar=w(j),
                                                          in1=xc[:, c, :], op0=ALU.mult, op1=ALU.add)
                            if j < CONV_W - 1:
                                steps.did(op)
                        op.then_inc(conv, 1)
                        if c == 0:
                            dve.wait_ge(rg_hi, i + 1)
                            dve.tensor_tensor(rg_l[:, :, :, :], rg_raw[:, :, :, :], rg_h[:, :, :, :].bitcast(F32),
                                              ALU.subtract).then_inc(rg_lo, 1)
                        else:
                            k_.split_lo(dve, 0, p0 + 2 * i + 1)
                        dve.wait_ge(xch_done, 2 * i + c + 1)
                        dve.tensor_tensor(xc_l[:, c, :], xc[:, c, :], xc_h[:, c, :].bitcast(F32),
                                          ALU.subtract).then_inc(xcl_done, 1)
                    dve.wait_ge(a_done, 2 * i + 2)
                    dve.wait_ge(root, i + 1)
                    k_.split_lo(dve, 1, p0 + 2 * i + 1)
                    for m in range(2):
                        a = a_sb[:, m, :]
                        rt = rt_sb[:, m, :]
                        steps.did(dve.tensor_tensor(i_sb[:, m, :], i_sb[:, m, :], xc[:, m, :], ALU.mult))
                        qk_low(i, 0, m)
                        steps.did(dve.scalar_tensor_tensor(out=rt, in0=a, scalar=1.0, in1=rt, op0=ALU.add, op1=ALU.mult))
                        steps.did(dve.tensor_tensor(i_sb[:, m, :], i_sb[:, m, :], rt, ALU.mult))
                        steps.did(dve.tensor_tensor_scan(rt, a, i_sb[:, m, :], 0.0, ALU.mult, ALU.add))
                        dve.tensor_tensor(k_.mix[:, bass.ds(2 * i + m, 1), :].rearrange("p a t -> p (a t)"),
                                          rt, gl[:, m, :], ALU.mult).then_inc(mixed, 1)
                    k_.split_lo(dve, 0, p0 + 2 * i + 2)
                    for c in range(2):
                        qk_low(i, 1, c)
                    assert steps.n == PER

    def value(self):
        nc, k_ = self.nc, self
        n_pairs = D // WB // 2
        p0, self.pairs = self.pairs, self.pairs + n_pairs
        work = self.work()
        st = [[work.put(f"v_{s}{part}", [P, NT, WB], F32R) for part in range(2)] for s in range(2)]
        v_mm = [self.sem(f"v_mm{s}") for s in range(2)]
        hi, lo = ([self.sem(f"v_{n}{t}") for t in range(4)] for n in ("hi", "lo"))
        stored = k_.v_stored
        steps_of_slot = [(s, t) for s in range(2) for t in range(NT)]

        with nc.Block() as block:
            @block.sync
            def _(sp):
                def store(i, s):
                    for t in range(4):
                        sp.wait_ge(lo[t], 4 * i + 2 * s + 2)
                    for part in range(2):
                        sp.dma_start(k_.v_d[2 * i + s, part], st[s][part][:, :, :].bitcast(F32)).then_inc(stored[s], 16)
                with sp.Fori(0, n_pairs - 1) as i:
                    for s in range(2):
                        k_.load_block(sp, s, p0 + i + 1, k_.w_block(k_.w_in, VC + WB * (2 + s) + 2 * WB * i))
                        store(i, s)
                for s, col in enumerate((ML, MA)):
                    k_.load_block(sp, s, p0 + n_pairs, k_.w_block(k_.w_in, col))
                    store(n_pairs - 1, s)

            @block.tensor
            def _(pe):
                with pe.Fori(0, n_pairs) as i:
                    for s, t in steps_of_slot:
                        if t == 0:
                            pe.wait_ge(k_.w_lo[s], p0 + i + 1)
                        pe.wait_ge(lo[t % 4], 4 * i + 2 * s + t // 4)
                        mm = k_.product_rows(pe, k_.ps[t % 4][:, 0:WB], s, t)
                        mm.then_inc(k_.w_first[s] if t == 0 else k_.w_used[s] if t == NT - 1 else v_mm[s], 1)

            @block.scalar
            def _(act):
                with act.Fori(0, n_pairs) as i:
                    for s, t in steps_of_slot:
                        if t == 0:
                            act.wait_ge(stored[s], 32 * i)
                        if t in (0, NT - 1):
                            act.wait_ge((k_.w_first if t == 0 else k_.w_used)[s], p0 + i + 1)
                        else:
                            act.wait_ge(v_mm[s], (NT - 2) * i + t)
                        act.activation(st[s][0][:, t, :], k_.ps[t % 4][:, 0:WB], ACT.Copy).then_inc(hi[t % 4], 1)
                        if (s, t) == (0, 1):
                            k_.split_hi(act, 1, p0 + i)
                        if (s, t) == (0, NT - 1):
                            k_.split_hi(act, 0, p0 + i + 1)

            @block.vector
            def _(dve):
                with dve.Fori(0, n_pairs) as i:
                    for s, t in steps_of_slot:
                        dve.wait_ge(hi[t % 4], 4 * i + 2 * s + t // 4 + 1)
                        dve.tensor_tensor(st[s][1][:, t, :], k_.ps[t % 4][:, 0:WB],
                                          st[s][0][:, t, :].bitcast(F32), ALU.subtract).then_inc(lo[t % 4], 1)
                        if (s, t) == (0, 1):
                            k_.split_lo(dve, 1, p0 + i)
                        if (s, t) == (0, NT - 1):
                            k_.split_lo(dve, 0, p0 + i + 1)

    def merge_gates(self):
        nc, k_ = self.nc, self
        n_pairs = D // WB
        p0, self.pairs = self.pairs, self.pairs + n_pairs
        work = self.work()
        st = [[work.put(f"m_{s}{c}", [P, T]) for c in range(2)] for s in range(2)]
        f_raw = work.put("f_raw", [P, KD, NH])
        f_h = work.put("f_h", [P, KD, NH], F32R)
        f_l = work.put("f_l", [P, KD, NH], F32R)
        b_f = work.put("b_f", [NH, 1])
        f, e, w1, dw, eq, ones = (work.put(f"d_{n}", [NH, T]) for n in ("f", "e", "w1", "dw", "eq", "ones"))
        c_h, c_l, n_h, n_l = (work.put(f"d_{n}", [NH, T], F32R) for n in ("ch", "cl", "nh", "nl"))
        named = lambda what: [[self.sem(f"m_{what}{s}{c}") for c in range(2)] for s in range(2)]
        out, stored = named("out"), k_.sig_stored
        f_loaded, f_hi, f_lo, f_mm, sized, d_exp, one, d_ln, own, ones_set, c_hi, c_lo = (
            self.sem(f"d_{n}") for n in ("loaded", "hi", "lo", "mm", "sized", "exp", "one", "ln", "own", "ones",
                                         "c_hi", "c_lo"))
        rows_stored = k_.rows_stored
        both = [(s, c) for s in range(2) for c in range(2)]
        c_sum = dw
        PER = 10

        with nc.Block() as block:
            @block.sync
            def _(sp):
                for c in range(2):
                    sp.wait_ge(k_.v_stored[c], 16 * NH // 2)
                sp.dma_start(f_raw[:, :, :], k_.w_in.rearrange("(k p) n -> p k n", p=P)[:, :, FL:FL + NH])\
                    .then_inc(f_loaded, 16)
                sp.dma_start(b_f[:, :], k_.ins["b_forget"].rearrange("a h -> h a")).then_inc(f_loaded, 16)

                def store(i, s):
                    for c in range(2):
                        sp.wait_ge(out[s][c], i + 1)
                        sp.dma_start(k_.sig_d[s, 2 * i + c], st[s][c][:, :]).then_inc(stored[s][c], 16)
                with sp.Fori(0, n_pairs - 1) as i:
                    for s, col in enumerate((ML, MA)):
                        k_.load_block(sp, s, p0 + i + 1, k_.w_block(k_.w_in, col + WB + WB * i))
                        store(i, s)
                sp.wait_ge(ones_set, 1)
                for part, row in ((0, 0), (0, 1), (1, 2), (1, 3)):
                    sp.dma_start(k_.c_d[:, part, row, :], ones[:, :]).then_inc(rows_stored, 16)
                sp.wait_ge(c_hi, 2)
                sp.wait_ge(c_lo, 2)
                for part, row, src in ((0, 2, c_h), (0, 3, c_l), (1, 0, n_h), (1, 1, n_l)):
                    sp.dma_start(k_.c_d[:, part, row, :], src[:, :].bitcast(F32)).then_inc(rows_stored, 16)
                for s in range(2):
                    k_.load_block(sp, s, p0 + n_pairs, k_.w_block(k_.ins["w_lru_out"][0], WB * s))
                    store(n_pairs - 1, s)

            @block.gpsimd
            def _(pool):
                pool.wait_ge(f_loaded, 32)
                pool.memset(ones[:, :], 1.0).then_inc(ones_set, 1)

            @block.tensor
            def _(pe):
                def turn(i):
                    for s, c in both:
                        if c == 0:
                            pe.wait_ge(k_.w_lo[s], p0 + i + 1)
                        pe.wait_ge(out[s][c], i)
                        k_.product(pe, k_.ps[2 * s + c], s, c).then_inc((k_.w_first, k_.w_used)[c][s], 1)
                for s, c in both:
                    if c == 0:
                        pe.wait_ge(k_.w_lo[s], p0 + 1)
                    k_.product(pe, k_.ps[2 * s + c], s, c).then_inc((k_.w_first, k_.w_used)[c][s], 1)
                pe.wait_ge(f_lo, 1)
                pe.wait_ge(out[1][1], 1)
                for k in range(KD):
                    for w, u, first, last in ((f_h, k_.uh, k == 0, False), (f_h, k_.ul, False, False),
                                              (f_l, k_.uh, False, k == KD - 1)):
                        for h in range(2):
                            mm = pe.matmul(k_.ps[3][0:NH, h * HALF:(h + 1) * HALF], w[:, k, :],
                                           u[:, k, h * HALF:(h + 1) * HALF], start=first, stop=last)
                mm.then_inc(f_mm, 1)
                pe.wait_ge(sized, 2)
                with pe.Fori(1, n_pairs) as i:
                    turn(i)

            @block.scalar
            def _(act):
                k_.split_hi(act, 1, p0)
                act.wait_ge(f_loaded, 32)
                act.activation(f_h[:, :, :], f_raw[:, :, :], ACT.Copy).then_inc(f_hi, 1)

                def turn(i, last):
                    for s, c in both:
                        act.wait_ge((k_.w_first, k_.w_used)[c][s], p0 + i + 1)
                        if type(i) is not int or i > 0:
                            act.wait_ge(stored[s][c], 16 * i)
                        act.activation(st[s][c][:, :], k_.ps[2 * s + c][:, :], ACT.Sigmoid).then_inc(out[s][c], 1)
                        if c == 1 and not (last and s == 1):
                            k_.split_hi(act, s, p0 + i + 1)
                turn(0, False)
                act.wait_ge(sized, 3)
                act.activation(e[:, :], e[:, :], ACT.Exp, scale=-1.0).then_inc(d_exp, 1)
                act.wait_ge(one, 1)
                act.activation(eq[:, :], w1[:, :], ACT.Ln).then_inc(d_ln, 1)
                act.wait_ge(own, PER)
                act.activation(c_h[:, :], c_sum[:, :], ACT.Copy).then_inc(c_hi, 1)
                act.activation(n_h[:, :], c_sum[:, :], ACT.Copy, scale=-1.0).then_inc(c_hi, 1)
                with act.Fori(1, n_pairs - 1) as i:
                    turn(i, False)
                turn(n_pairs - 1, True)

            @block.vector
            def _(dve):
                steps = Steps(dve, own)
                k_.split_lo(dve, 1, p0)
                dve.wait_ge(f_hi, 1)
                dve.tensor_tensor(f_l[:, :, :], f_raw[:, :, :], f_h[:, :, :].bitcast(F32), ALU.subtract).then_inc(f_lo, 1)
                for s in range(2):
                    k_.split_lo(dve, s, p0 + 1)
                dve.wait_ge(f_mm, 1)
                dve.tensor_scalar(f[:, :], k_.ps[3][0:NH, :], b_f[:, :], None, ALU.add).then_inc(sized, 2)
                dve.wait_ge(sized, 2)
                dve.scalar_tensor_tensor(out=e[:, :], in0=f[:, :], scalar=-1.0, in1=f[:, :], op0=ALU.mult, op1=ALU.max)\
                    .then_inc(sized, 1)
                dve.wait_ge(sized, 3)
                steps.did(dve.tensor_scalar(f[:, :], f[:, :], 0.0, None, ALU.min))
                dve.wait_ge(d_exp, 1)
                dve.tensor_scalar(w1[:, :], e[:, :], 1.0, None, ALU.add).then_inc(one, 1)
                dve.wait_ge(one, 1)
                steps.did(dve.tensor_scalar(dw[:, :], w1[:, :], -1.0, None, ALU.add))
                dve.wait_ge(d_ln, 1)
                steps.did(dve.tensor_scalar(w1[:, :], dw[:, :], 0.0, None, ALU.is_equal))
                steps.did(dve.tensor_tensor(dw[:, :], dw[:, :], w1[:, :], ALU.add))
                steps.did(dve.reciprocal(dw[:, :], dw[:, :]))
                steps.did(dve.tensor_tensor(eq[:, :], eq[:, :], w1[:, :], ALU.add))
                steps.did(dve.tensor_tensor(eq[:, :], eq[:, :], dw[:, :], ALU.mult))
                steps.did(dve.tensor_tensor(eq[:, :], eq[:, :], e[:, :], ALU.mult))
                steps.did(dve.tensor_tensor(f[:, :], f[:, :], eq[:, :], ALU.subtract))
                dve.wait_ge(ones_set, 1)
                steps.did(dve.tensor_tensor_scan(c_sum[:, :], ones[:, :], f[:, :], 0.0, ALU.mult, ALU.add))
                assert steps.n == PER
                dve.wait_ge(c_hi, 2)
                dve.tensor_tensor(c_l[:, :], c_sum[:, :], c_h[:, :].bitcast(F32), ALU.subtract).then_inc(c_lo, 1)
                dve.tensor_tensor(n_l[:, :], c_h[:, :].bitcast(F32), c_sum[:, :], ALU.subtract).then_inc(c_lo, 1)
                with dve.Fori(1, n_pairs - 1) as i:
                    for s in range(2):
                        k_.split_lo(dve, s, p0 + i + 1)
                k_.split_lo(dve, 0, p0 + n_pairs)

    def branch_out(self, branch):
        nc, k_ = self.nc, self
        n_pairs = D // WB // 2
        p0, self.pairs = self.pairs, self.pairs + n_pairs
        weights = self.ins["w_lru_out" if branch == 0 else "w_attn_out"][0]
        following = self.ins["w_attn_out" if branch == 0 else "w_out"][0]
        work = self.work()
        if branch == 0:
            self.attention_inputs()
        tag = "lo" if branch == 0 else "ao"
        sg = [[work.put(f"{tag}_sg{s}{c}", [P, T]) for c in range(2)] for s in range(2)]
        stage = [work.put(f"{tag}_in{r}", [P, T]) for r in range(4)]
        named = lambda what: [[self.sem(f"{tag}_{what}{s}{c}") for c in range(2)] for s in range(2)]
        loaded, gated = named("loaded"), named("gated")
        in_loaded = [self.sem(f"{tag}_in{r}") for r in range(4)]
        in_hi, in_lo, own = (self.sem(f"{tag}_{n}") for n in ("hi", "split", "own"))
        both = [(s, c) for s in range(2) for c in range(2)]
        source = lambda k: k_.mix[:, k, :] if branch == 0 else stage[k % 4][:, :]

        with nc.Block() as block:
            @block.sync
            def _(sp):
                if branch == 0:
                    for s, c in both:
                        sp.wait_ge(k_.sig_stored[s][c], 16 * (D // WB))
                else:
                    for g in range(2):
                        sp.wait_ge(k_.o_stored[g], 16 * NH)
                    for k in range(KD):
                        if k >= 4:
                            sp.wait_ge(in_lo, k - 3)
                        sp.dma_start(stage[k % 4][:, :], k_.o_d[k]).then_inc(in_loaded[k % 4], 16)

                def gates(i):
                    for s, c in both:
                        sp.wait_ge(gated[s][c], i)
                        sp.dma_start(sg[s][c][:, :], k_.sig_d[branch, 4 * i + 2 * s + c]).then_inc(loaded[s][c], 16)
                with sp.Fori(0, n_pairs - 1) as i:
                    gates(i)
                    for s in range(2):
                        k_.load_block(sp, s, p0 + i + 1, k_.w_block(weights, WB * (2 + s) + 2 * WB * i))
                gates(n_pairs - 1)
                if branch == 0:
                    for c in range(2):
                        sp.wait_ge(k_.qk_stored[c], 16 * NH)
                        sp.wait_ge(k_.v_stored[c], 16 * NH // 2)
                    sp.wait_ge(k_.rows_stored, 16 * 8)
                    for c in range(2):
                        if c == 0:
                            k_.load_head_qk(sp, 0, c)
                        k_.load_head_v(sp, 0, c)
                for s in range(2):
                    k_.load_block(sp, s, p0 + n_pairs, k_.w_block(following, WB * s))

            @block.tensor
            def _(pe):
                with pe.Fori(0, n_pairs) as i:
                    for s, c in both:
                        if c == 0:
                            pe.wait_ge(k_.w_lo[s], p0 + i + 1)
                        pe.wait_ge(gated[s][c], i)
                        k_.product(pe, k_.ps[2 * s + c], s, c, in_lo if (s, c) == (0, 0) else None).then_inc((k_.w_first, k_.w_used)[c][s], 1)

            @block.scalar
            def _(act):
                for k in range(KD):
                    if branch == 1:
                        act.wait_ge(in_loaded[k % 4], 16 * (k // 4 + 1))
                    act.activation(k_.uh[:, k, :], source(k), ACT.Copy).then_inc(in_hi, 1)
                with act.Fori(0, n_pairs) as i:
                    k_.split_hi(act, 1, p0 + i)
                    k_.split_hi(act, 0, p0 + i + 1)

            @block.vector
            def _(dve):
                for k in range(KD):
                    dve.wait_ge(in_hi, k + 1)
                    dve.tensor_tensor(k_.ul[:, k, :], source(k), k_.uh[:, k, :].bitcast(F32),
                                      ALU.subtract).then_inc(in_lo, 1)
                with dve.Fori(0, n_pairs) as i:
                    k_.split_lo(dve, 1, p0 + i)
                    for s, c in both:
                        dve.wait_ge((k_.w_first, k_.w_used)[c][s], p0 + i + 1)
                        dve.wait_ge(loaded[s][c], 16 * (i + 1))
                        mix = k_.mix[:, bass.ds(4 * i + 2 * s + c, 1), :].rearrange("p a t -> p (a t)")
                        if branch == 0:
                            dve.tensor_tensor(mix, k_.ps[2 * s + c][:, :], sg[s][c][:, :], ALU.mult)\
                                .then_inc(gated[s][c], 1)
                        else:
                            dve.tensor_tensor(sg[s][c][:, :], k_.ps[2 * s + c][:, :], sg[s][c][:, :], ALU.mult)\
                                .then_inc(own, 1)
                            dve.wait_ge(own, 4 * i + 2 * s + c + 1)
                            dve.tensor_tensor(mix, mix, sg[s][c][:, :], ALU.add).then_inc(gated[s][c], 1)
                        if (s, c) == (0, 1):
                            k_.split_lo(dve, 0, p0 + i + 1)

    def attention_inputs(self):
        work = self.work()
        at_qk1 = work.put("at_qk1", [P, 4, T], F32R)
        self.at_qk = [work.put("at_qk0", [P, 4, T], F32R), at_qk1]
        self.at_v = [work.put(f"at_v{c}", [P, 2, NT, HD], F32R) for c in range(2)]
        self.at_rows = [work.put(f"at_rows{c}", [4, 2, T], F32R) for c in range(2)]
        self.at_work = work

    def load_head_qk(self, eng, i, c):
        eng.dma_start(self.at_qk[c][:, :, :].bitcast(F32), self.qk_d[2 * i + c]).then_inc(self.qk_in[c], 16)
        eng.dma_start(self.at_rows[c][:, :, :].bitcast(F32), self.c_d[2 * i + c].rearrange("a r t -> r a t"))\
            .then_inc(self.c_in[c], 16)

    def load_head_v(self, eng, i, c):
        for part in range(2):
            eng.dma_start(self.at_v[c][:, part, :, :].bitcast(F32),
                          self.v_d[i, part, :, :, c * HD:(c + 1) * HD]).then_inc(self.v_in[c], 16)

    def attention(self):
        nc, k_ = self.nc, self
        upper = Map(nc, self.act_start, self.work_start - 4 * KD * T)
        qk, v, rows, work = k_.at_qk, k_.at_v, k_.at_rows, k_.at_work
        o_sb = [work.put(f"at_o{g}", [P, HALF]) for g in range(2)]
        mask = work.put("at_mask", [P, T])
        pt_h = [upper.put(f"at_pth{g}", [P, 4 + 4 * g, HALF], F32R) for g in range(2)]
        pt_l = [upper.put(f"at_ptl{g}", [P, 4 + 4 * g, HALF], F32R) for g in range(2)]
        SB = 4
        sb = [upper.put(f"at_s{b}", [P, T]) for b in range(SB)]
        small = work.put("at_small", [P, 2, 4])
        sem = self.sem
        qk_in, v_in, c_in, stored = k_.qk_in, k_.v_in, k_.c_in, k_.o_stored
        names = ("mask", "s_mm", "maxed", "negated", "exped", "inverted", "scaled", "t_mm", "hi", "lo", "pv_mm", "o_out")
        masks, s_mm, maxed, negated, exped, inverted, scaled, t_mm, hi, lo, pv_mm, o_out = (sem("at_" + n) for n in names)
        turns, tiles = NH // 2, 2 * NT
        parts = [(n, kb, min(4, n % NT + 1 - kb)) for n in range(tiles) for kb in range(0, n % NT + 1, 4)]
        of_tile = [[st for st, part in enumerate(parts) if part[0] == n] for n in range(tiles)]
        turned = lambda st: k_.ps[2][:, st % 2 * HALF:st % 2 * HALF + parts[st][2] * P]

        def piece(pt, st):
            n, kb, m = parts[st]
            return pt[n % NT // 4][:, kb:kb + m, n % 4 * P:n % 4 * P + P]

        def back(i, n, by):
            if n - by >= 0:
                return (i, n - by) if n - by < tiles else None
            return None if type(i) is int and i == 0 else (i - 1, n - by + tiles)

        def steps(engine, step):
            for n in range(tiles):
                step(0, n)
            with engine.Fori(1, turns) as i:
                for n in range(tiles):
                    step(i, n)
            for n in range(tiles, tiles + 5):
                step(turns - 1, n)

        def later(engine, semaphore, count):
            if type(count) is not int or count > 0:
                engine.wait_ge(semaphore, count)

        with nc.Block() as block:
            @block.sync
            def _(sp):
                def load_qk(i, c):
                    sp.wait_ge(s_mm, tiles * i - tiles + NT * (c + 1))
                    k_.load_head_qk(sp, i, c)

                def load_v(i, c):
                    sp.wait_ge(pv_mm, 4 * i - 2 + 2 * c)
                    k_.load_head_v(sp, i, c)

                def store(i, c):
                    for g in range(2):
                        sp.wait_ge(o_out, 4 * i + 2 * c + g + 1)
                        sp.dma_start(k_.o_d[2 * i + c][:, g * HALF:(g + 1) * HALF], o_sb[g][:, :]).then_inc(stored[g], 16)
                k_.load_head_qk(sp, 0, 1)
                with sp.Fori(0, turns - 1) as i:
                    for c in range(2):
                        load_qk(i + 1, c)
                        store(i, c)
                        load_v(i + 1, c)
                for c in range(2):
                    store(turns - 1, c)

            @block.gpsimd
            def _(pool):
                pool.memset(mask[:, :], 0.0).then_inc(masks, 1)
                pool.wait_ge(masks, 1)
                pool.affine_select(out=mask[:, T - P:T], in_=mask[:, T - P:T], compare_op=ALU.is_ge, fill=NEG, base=0,
                                   pattern=[[-1, P]], channel_multiplier=1).then_inc(masks, 1)

            @block.tensor
            def _(pe):
                def scores(i, n):
                    c, qb = n // NT, n % NT
                    keys = (qb + 1) * P
                    if qb == 0:
                        pe.wait_ge(qk_in[c], 16 * (i + 1))
                        pe.wait_ge(c_in[c], 16 * (i + 1))
                    later(pe, maxed, tiles * i + n - 1)
                    queries = slice(qb * P, (qb + 1) * P)
                    q_h, q_l = (qk[c][:, part, queries] for part in range(2))
                    for at in range(0, keys, HALF):
                        end = min(at + HALF, keys)
                        for q, part, first in ((q_h, 2, True), (q_h, 3, False), (q_l, 2, False)):
                            pe.matmul(k_.ps[n % 2][:, at:end], q, qk[c][:, part, at:end], start=first, stop=False)
                        mm = pe.matmul(k_.ps[n % 2][:, at:end], rows[c][:, 0, queries], rows[c][:, 1, at:end],
                                       start=False, stop=True)
                    mm.then_inc(s_mm, 1)

                def turn(i, n):
                    pe.wait_ge(scaled, tiles * i + n + 1)
                    for st in of_tile[n]:
                        _, kb, m = parts[st]
                        later(pe, lo, len(parts) * i + st - 1)
                        for j in range(m):
                            mm = pe.transpose(turned(st)[:, j * P:(j + 1) * P],
                                              sb[n % SB][:, (kb + j) * P:(kb + j + 1) * P], k_.ident[:, :])
                        mm.then_inc(t_mm, 1)

                def values(i, group):
                    c, g = group // 2, group % 2
                    if g == 0:
                        pe.wait_ge(v_in[c], 32 * (i + 1))
                    pe.wait_ge(lo, len(parts) * i + of_tile[4 * group + 3][-1] + 1)
                    later(pe, o_out, 4 * i + group - 1)
                    blocks = 4 * g + 4
                    for kb in range(blocks):
                        q0 = max(0, kb - 4 * g) * P
                        for part, pt, first, last in ((0, pt_h, kb == 0, False), (0, pt_l, False, False),
                                                      (1, pt_h, False, kb == blocks - 1)):
                            mm = pe.matmul(k_.ps[3][:, g * HALF + q0:(g + 1) * HALF], v[c][:, part, kb, :],
                                           pt[g][:, kb, q0:HALF], start=first, stop=last)
                    mm.then_inc(pv_mm, 1)

                def step(i, n):
                    if n < tiles:
                        scores(i, n)
                    if tile := back(i, n, 2):
                        turn(*tile)
                    if (tile := back(i, n, 4)) and tile[1] % 4 == 3:
                        values(tile[0], tile[1] // 4)
                steps(pe, step)

            @block.scalar
            def _(act):
                def high(i, n):
                    for st in of_tile[n]:
                        act.wait_ge(t_mm, len(parts) * i + st + 1)
                        later(act, pv_mm, 4 * i + n // 4 - 1)
                        act.activation(piece(pt_h, st), turned(st).rearrange("p (k q) -> p k q", q=P),
                                       ACT.Copy).then_inc(hi, 1)

                def exponent(i, n):
                    keys = (n % NT + 1) * P
                    act.wait_ge(negated, tiles * i + n + 1)
                    act.activation(sb[n % SB][:, 0:keys], sb[n % SB][:, 0:keys], ACT.Exp,
                                   bias=small[:, n % 2, 1:2], accum_out=small[:, n % 2, 2:3]).then_inc(exped, 1)

                def output(i, group):
                    c, g = group // 2, group % 2
                    act.wait_ge(pv_mm, 4 * i + group + 1)
                    later(act, stored[g], 16 * (2 * i + c))
                    act.activation(o_sb[g][:, :], k_.ps[3][:, g * HALF:(g + 1) * HALF], ACT.Copy).then_inc(o_out, 1)

                def step(i, n):
                    if tile := back(i, n, 2):
                        high(*tile)
                    if n < tiles:
                        exponent(i, n)
                    if (tile := back(i, n, 5)) and tile[1] % 4 == 3:
                        output(tile[0], tile[1] // 4)
                steps(act, step)

            @block.vector
            def _(dve):
                def low(i, n):
                    for st in of_tile[n]:
                        dve.wait_ge(hi, len(parts) * i + st + 1)
                        dve.tensor_tensor(piece(pt_l, st), turned(st).rearrange("p (k q) -> p k q", q=P),
                                          piece(pt_h, st).bitcast(F32), ALU.subtract).then_inc(lo, 1)

                def step(i, n):
                    if tile := back(i, n, 3):
                        low(*tile)
                    if tile := back(i, n, 1):
                        i_, m = tile
                        b, s4, keys = m % 2, m % SB, (m % NT + 1) * P
                        dve.wait_ge(exped, tiles * i_ + m + 1)
                        dve.reciprocal(small[:, b, 3:4], small[:, b, 2:3]).then_inc(inverted, 1)
                        dve.wait_ge(inverted, tiles * i_ + m + 1)
                    if n < tiles:
                        dve.wait_ge(s_mm, tiles * i + n + 1)
                    if tile:
                        dve.tensor_scalar(sb[s4][:, 0:keys], sb[s4][:, 0:keys], small[:, b, 3:4], None, ALU.mult)\
                            .then_inc(scaled, 1)
                    if n < tiles:
                        keys = (n % NT + 1) * P
                        dve.tensor_tensor_reduce(out=sb[n % SB][:, 0:keys], in0=k_.ps[n % 2][:, 0:keys],
                                                 in1=mask[:, T - keys:T], scale=1.0, scalar=NEG, op0=ALU.add,
                                                 op1=ALU.max, accum_out=small[:, n % 2, 0:1]).then_inc(maxed, 1)
                        dve.wait_ge(maxed, tiles * i + n + 1)
                        dve.tensor_scalar(small[:, n % 2, 1:2], small[:, n % 2, 0:1], -1.0, None, ALU.mult)\
                            .then_inc(negated, 1)
                dve.wait_ge(masks, 2)
                steps(dve, step)

    def project(self):
        nc, k_ = self.nc, self
        n_pairs = D // WB // 2
        p0, self.pairs = self.pairs, self.pairs + n_pairs
        work = self.work()
        self.x2 = work.put("x2", [P, NT, D])
        self.x2_total = work.put("x2_total", [P, NT])
        self.x2_end = work.at
        square = work.put("pr_square", [P, D])
        squared = self.sem("pr_squared")
        x_in = [self.sem(f"pr_x{t}") for t in range(NT)]
        in_hi, in_lo = self.sem("pr_hi"), self.sem("pr_split")
        mm_done = [self.sem(f"pr_mm{s}") for s in range(2)]
        added = [self.sem(f"pr_add{t}") for t in range(4)]
        weights = self.ins["w_out"][0]

        with nc.Block() as block:
            @block.sync
            def _(sp):
                for t in range(NT):
                    sp.dma_start(k_.x2[:, t, :], k_.x[t * P:(t + 1) * P, :]).then_inc(x_in[t], 16)
                for s in range(2):
                    k_.load_block(sp, s, p0 + 1, k_.w_block(weights, WB * (2 + s)))

            @block.tensor
            def _(pe):
                with pe.Fori(0, n_pairs) as i:
                    for s in range(2):
                        for t in range(NT):
                            if t == 0:
                                pe.wait_ge(k_.w_lo[s], p0 + i + 1)
                            pe.wait_ge(added[t % 4], 4 * i + 2 * s + t // 4)
                            mm = k_.product_rows(pe, k_.ps[t % 4][:, 0:WB], s, t, in_lo if (s, t) == (0, 0) else None)
                            mm.then_inc(k_.w_first[s] if t == 0 else k_.w_used[s] if t == NT - 1 else mm_done[s], 1)

            @block.scalar
            def _(act):
                for k in range(KD):
                    act.activation(k_.uh[:, k, :], k_.mix[:, k, :], ACT.Copy).then_inc(in_hi, 1)
                k_.split_hi(act, 1, p0)
                for s in range(2):
                    k_.split_hi(act, s, p0 + 1)
                for t in range(NT):
                    act.wait_ge(added[t % 4], 4 * n_pairs - 1 + t // 4)
                    act.activation(square[:, :], k_.x2[:, t, :], ACT.Square, accum_out=k_.x2_total[:, t:t + 1])\
                        .then_inc(squared, 1)
                    act.wait_ge(squared, t + 1)

            @block.vector
            def _(dve):
                for k in range(KD):
                    dve.wait_ge(in_hi, k + 1)
                    dve.tensor_tensor(k_.ul[:, k, :], k_.mix[:, k, :], k_.uh[:, k, :].bitcast(F32),
                                      ALU.subtract).then_inc(in_lo, 1)
                for t in range(NT):
                    dve.wait_ge(x_in[t], 16)

                def turn(i, last):
                    for s in range(2):
                        for t in range(NT):
                            if t in (0, NT - 1):
                                dve.wait_ge((k_.w_first if t == 0 else k_.w_used)[s], p0 + i + 1)
                            else:
                                dve.wait_ge(mm_done[s], (NT - 2) * i + t)
                            part = k_.x2[:, t, bass.ds(WB * (2 * i + s), WB)]
                            dve.tensor_tensor(part, part, k_.ps[t % 4][:, 0:WB], ALU.add).then_inc(added[t % 4], 1)
                            if (s, t) == (0, 1):
                                k_.split_lo(dve, 1, p0 + i)
                        if s == 0 and not last:
                            k_.split_lo(dve, 0, p0 + i + 1)
                turn(0, False)
                turn(1, True)

    def route(self):
        nc, k_, ins = self.nc, self, self.ins
        low = Map(nc, self.fixed_end, self.work_start)
        self.e_raw = [low.put(f"e_raw{r}", [P, 4, HALF]) for r in range(6)]
        self.raw_end = low.at
        work = Map(nc, self.raw_end, self.work_start)
        put, sem = work.put, self.sem
        NL = NG + NE
        g_b, b_r, w_r = put("rt_g", [P, D]), put("rt_b", [P, NL]), put("rt_w", [P, KD, NL])
        xn = [put(f"rt_xn{b}", [P, D]) for b in range(2)]
        xt = [put(f"rt_xt{b}", [P, KD, P]) for b in range(2)]
        zeros = put("rt_zeros", [P, SLOTS // P + 1], I32)
        mean, rstd, power = (put(f"rt_{n}", [P, NT]) for n in ("mean", "rstd", "power"))
        logits = put("rt_logits", [P, NT, NL])
        i_exp, e_base = put("rt_iexp", [P, NT, NE]), put("rt_ebase", [P, NT, NE])
        i_grp, grp, g_eq = (put(f"rt_{n}", [P, NT, NG]) for n in ("igrp", "grp", "geq"))
        m_exp, eq, oh1, oh2, prod = (put(f"rt_{n}", [P, NT, NE]) for n in ("mexp", "eq", "oh1", "oh2", "prod"))
        gmax, gsum, gsel, m1, m2, sel, ex, inv, dst = (
            put(f"rt_{n}", [P, NT]) for n in ("gmax", "gsum", "gsel", "m1", "m2", "sel", "ex", "inv", "dst"))
        tok = put("rt_tok", [P, NT], I32)
        NX = MAXX
        cnt, extra, ends, shift = (put(f"rt_{n}", [P, NE]) for n in ("cnt", "extra", "ends", "shift"))
        limit, over = put("rt_limit", [P, NE, KD - 1]), put("rt_over", [P, NE, KD - 1])
        jj, before, which = put("rt_jj", [1, NX, NE]), put("rt_before", [1, NX, NE]), put("rt_which", [1, NX])

        in_sem, zeroed, filled, consts = sem("rt_in"), sem("rt_zeroed"), sem("rt_filled"), sem("rt_consts")
        averaged, powered, scaled, stored = (
            sem(f"rt_{n}") for n in ("averaged", "powered", "scaled", "stored0"))
        stored = [stored, sem("rt_stored1")]
        turned, copied, logit_mm, logit_out = (sem(f"rt_{n}") for n in ("turned", "copied", "mm", "logit"))
        own, to_exp, exped, chosen, rank_mm, dest_out, scattered = (
            sem(f"rt_{n}") for n in ("own", "to_exp", "exped", "chosen", "rank", "dest", "scattered"))
        tiles = NT // 2

        with nc.Block() as block:
            @block.sync
            def _(sp):
                sp.dma_start(g_b[:, :], ins["g_ffn"][0].partition_broadcast(P)).then_inc(in_sem, 16)
                sp.dma_start(b_r[:, 0:NG], ins["b_route_group"][0].partition_broadcast(P)).then_inc(in_sem, 16)
                sp.dma_start(b_r[:, NG:NL], ins["b_route_expert"][0].partition_broadcast(P)).then_inc(in_sem, 16)
                rows = lambda w: w[0].rearrange("(k p) n -> p k n", p=P)
                sp.dma_start(w_r[:, :, 0:NG], rows(ins["w_route_group"])).then_inc(in_sem, 16)
                sp.dma_start(w_r[:, :, NG:NL], rows(ins["w_route_expert"])).then_inc(in_sem, 16)
                sp.wait_ge(zeroed, 1)
                sp.dma_start(k_.slots_d.rearrange("(p n) a -> p (n a)", p=P), zeros[:, :]).then_inc(filled, 16)
                for m, e in ((0, 0), (1, 0), (2, 0), (3, 0), (4, 1), (5, 1)):
                    k_.load_piece(sp, (0, m), ("gate", "up", "gate")[m // 2], m % 2, e, True)
                with sp.Fori(0, tiles) as i:
                    for b in range(2):
                        sp.wait_ge(scaled, 2 * i + b + 1)
                        sp.dma_start(k_.xn_d[bass.ds((2 * i + b) * P, P), :], xn[b][:, :]).then_inc(stored[b], 16)
                for b in range(2):
                    sp.wait_ge(stored[b], 16 * tiles)

            @block.gpsimd
            def _(pool):
                pool.memset(zeros[:, :], 0).then_inc(zeroed, 1)
                pool.memset(power[:, :], -0.5).then_inc(consts, 1)
                iota = lambda out, pattern, base, step: pool.iota(
                    out, pattern, base=base, channel_multiplier=step,
                    allow_small_or_imprecise_dtypes=True).then_inc(consts, 1)
                iota(i_grp[:, :, :], [[0, NT], [1, NG]], 100, 0)
                iota(i_exp[:, :, :], [[0, NT], [1, NE]], 100, 0)
                iota(e_base[:, :, :], [[0, NT], [BLK, NE]], 0, 0)
                iota(limit[:, :, :], [[0, NE], [BLK, KD - 1]], BLK, 0)
                iota(jj[:, :, :], [[1, NX], [0, NE]], 0, 0)
                iota(tok[:, :], [[P, NT]], 0, 1)
                pool.wait_ge(averaged, 1)
                pool.wait_ge(consts, 7)
                pool.tensor_tensor(rstd[:, :], mean[:, :], power[:, :], ALU.pow).then_inc(powered, 1)
                pool.wait_ge(filled, 16)
                for s in range(2):
                    pool.wait_ge(dest_out, s + 1)
                    for t in range(NT):
                        pool.indirect_dma_start(
                            out=k_.slots_d, out_offset=bass.IndirectOffsetOnAxis(ap=k_.dest[:, s, t:t + 1], axis=0),
                            in_=tok[:, t:t + 1], in_offset=None).then_inc(scattered, 16)
                pool.wait_ge(scattered, 16 * 2 * NT)

            @block.tensor
            def _(pe):
                pe.wait_ge(in_sem, 16 * 5)

                def logits_of(i, b):
                    pe.wait_ge(copied, 2 * i + b + 1)
                    pe.wait_ge(logit_out, 2 * i)
                    for k in range(KD):
                        mm = pe.matmul(k_.ps[2 + b][:, 0:NL], xt[b][:, k, :], w_r[:, k, :],
                                       start=(k == 0), stop=(k == KD - 1))
                    mm.then_inc(logit_mm, 1)
                with pe.Fori(0, tiles) as i:
                    for b in range(2):
                        pe.wait_ge(scaled, 2 * i + b + 1)
                        pe.wait_ge(copied, 2 * i)
                        for k in range(KD):
                            mm = pe.transpose(k_.ps[b][:, k * P:(k + 1) * P], xn[b][:, k * P:(k + 1) * P], k_.ident[:, :])
                        mm.then_inc(turned, 1)
                    for b in range(2):
                        logits_of(i, b)
                pe.wait_ge(chosen, 1)
                for t in range(NT + 1):
                    for j in range(min(t + 1, NT)):
                        mm = pe.matmul(k_.ps[0][:, t * NE:(t + 1) * NE], (k_.stri if j == t else k_.ones)[:, :],
                                       prod[:, j, :], start=(j == 0), stop=(j == min(t, NT - 1)))
                mm.then_inc(rank_mm, 1)

            @block.scalar
            def _(act):
                with act.Fori(0, tiles) as i:
                    for b in range(2):
                        act.wait_ge(turned, 2 * i + b + 1)
                        act.wait_ge(logit_mm, 2 * i)
                        act.activation(xt[b][:, :, :].rearrange("p k t -> p (k t)"), k_.ps[b][:, :], ACT.Copy)\
                            .then_inc(copied, 1)
                act.wait_ge(to_exp, 1)
                act.activation(grp[:, :, :], grp[:, :, :], ACT.Exp).then_inc(exped, 1)
                act.wait_ge(to_exp, 2)
                act.activation(ex[:, :], ex[:, :], ACT.Exp).then_inc(exped, 1)

            @block.vector
            def _(dve):
                dve.tensor_scalar(mean[:, :], k_.x2_total[:, :], 1.0 / D, EPS, ALU.mult, ALU.add).then_inc(averaged, 1)
                dve.wait_ge(powered, 1)
                dve.wait_ge(in_sem, 16 * 5)
                with dve.Fori(0, tiles) as i:
                    for b in range(2):
                        t = 2 * i + b
                        dve.wait_ge(stored[b], 16 * i)
                        dve.wait_ge(turned, 2 * i)
                        dve.scalar_tensor_tensor(out=xn[b][:, :], in0=k_.x2[:, bass.ds(t, 1), :].rearrange("p a n -> p (a n)"),
                                                 scalar=rstd[:, bass.ds(t, 1)], in1=g_b[:, :], op0=ALU.mult,
                                                 op1=ALU.mult).then_inc(scaled, 1)
                    for b in range(2):
                        dve.wait_ge(logit_mm, 2 * i + b + 1)
                        dve.tensor_tensor(logits[:, bass.ds(2 * i + b, 1), :].rearrange("p a n -> p (a n)"),
                                          k_.ps[2 + b][:, 0:NL], b_r[:, :], ALU.add).then_inc(logit_out, 1)
                dve.wait_ge(logit_out, NT)
                dve.wait_ge(consts, 7)
                steps = Steps(dve, own)
                did = steps.did
                tt = lambda out, a, b, op: did(dve.tensor_tensor(out, a, b, op))
                over_last = lambda v, n: v.unsqueeze(2).to_broadcast([P, NT, n])
                gl, el = logits[:, :, 0:NG], logits[:, :, NG:NL]

                def first_match(values, top, numbers, scratch, chosen_one, n):
                    tt(scratch, values, over_last(top, n), ALU.is_equal)
                    did(dve.scalar_tensor_tensor(out=scratch, in0=scratch, scalar=-100.0, in1=numbers,
                                                 op0=ALU.mult, op1=ALU.add))
                    did(dve.tensor_reduce(sel[:, :], scratch, AX.X, ALU.min))
                    did(dve.tensor_scalar(sel[:, :], sel[:, :], 100.0, None, ALU.add))
                    tt(chosen_one, numbers, over_last(sel[:, :], n), ALU.is_equal)

                did(dve.tensor_reduce(gmax[:, :], gl, AX.X, ALU.max))
                dve.tensor_tensor(grp[:, :, :], gl, over_last(gmax[:, :], NG), ALU.subtract).then_inc(to_exp, 1)
                dve.wait_ge(exped, 1)
                did(dve.tensor_reduce(gsum[:, :], grp[:, :, :], AX.X, ALU.add))
                did(dve.reciprocal(gsum[:, :], gsum[:, :]))
                first_match(gl, gmax[:, :], i_grp[:, :, :], g_eq[:, :, :], grp[:, :, :], NG)
                in_group = grp[:, :, :].unsqueeze(3).to_broadcast([P, NT, NG, EG])
                by_group = lambda v: v.rearrange("p t (g e) -> p t g e", g=NG)
                tt(by_group(m_exp[:, :, :]), by_group(el), in_group, ALU.mult)
                did(dve.tensor_scalar(g_eq[:, :, :], grp[:, :, :], -NEG, NEG, ALU.mult, ALU.add))
                tt(by_group(m_exp[:, :, :]), by_group(m_exp[:, :, :]),
                   g_eq[:, :, :].unsqueeze(3).to_broadcast([P, NT, NG, EG]), ALU.add)
                did(dve.tensor_reduce(m1[:, :], m_exp[:, :, :], AX.X, ALU.max))
                first_match(m_exp[:, :, :], m1[:, :], i_exp[:, :, :], eq[:, :, :], oh1[:, :, :], NE)
                did(dve.scalar_tensor_tensor(out=m_exp[:, :, :], in0=oh1[:, :, :], scalar=NEG, in1=m_exp[:, :, :],
                                             op0=ALU.mult, op1=ALU.add))
                did(dve.tensor_reduce(m2[:, :], m_exp[:, :, :], AX.X, ALU.max))
                dve.tensor_tensor(ex[:, :], m2[:, :], m1[:, :], ALU.subtract).then_inc(to_exp, 1)
                first_match(m_exp[:, :, :], m2[:, :], i_exp[:, :, :], eq[:, :, :], oh2[:, :, :], NE)
                dve.tensor_tensor(prod[:, :, :], oh1[:, :, :], oh2[:, :, :], ALU.add).then_inc(chosen, 1)
                dve.wait_ge(exped, 2)
                did(dve.tensor_scalar(inv[:, :], ex[:, :], 1.0, None, ALU.add))
                did(dve.reciprocal(inv[:, :], inv[:, :]))
                tt(k_.wgt[:, 0, :], inv[:, :], gsum[:, :], ALU.mult)
                tt(k_.wgt[:, 1, :], k_.wgt[:, 0, :], ex[:, :], ALU.mult)
                dve.wait_ge(rank_mm, 1)
                did(dve.tensor_copy(cnt[:, :], k_.ps[0][:, NT * NE:(NT + 1) * NE]))
                tt(over[:, :, :], cnt[:, :].unsqueeze(2).to_broadcast([P, NE, KD - 1]), limit[:, :, :], ALU.is_gt)
                did(dve.tensor_reduce(extra[:, :], over[:, :, :], AX.X, ALU.add))
                did(dve.tensor_tensor_scan(ends[:, :], k_.ones[:, 0:NE], extra[:, :], 0.0, ALU.mult, ALU.add))
                tt(shift[:, :], ends[:, :], extra[:, :], ALU.subtract)
                did(dve.tensor_scalar(shift[:, :], shift[:, :], float(BLK), float(BLK * (NE - 1)), ALU.mult, ALU.add))
                tt(shift[:, :], shift[:, :], e_base[:, 0, :], ALU.subtract)
                rank = k_.ps[0][:, 0:NT * NE].rearrange("p (t e) -> p t e", e=NE)
                did(dve.tensor_scalar(eq[:, :, :], rank, float(BLK), None, ALU.is_ge))
                tt(eq[:, :, :], eq[:, :, :], shift[:, :].unsqueeze(1).to_broadcast([P, NT, NE]), ALU.mult)
                tt(e_base[:, :, :], e_base[:, :, :], rank, ALU.add)
                tt(e_base[:, :, :], e_base[:, :, :], eq[:, :, :], ALU.add)
                for s, oh in enumerate((oh1, oh2)):
                    tt(oh[:, :, :], oh[:, :, :], e_base[:, :, :], ALU.mult)
                    did(dve.tensor_reduce(dst[:, :], oh[:, :, :], AX.X, ALU.add))
                    dve.tensor_copy(k_.dest[:, s, :], dst[:, :]).then_inc(dest_out, 1)
                tt(before[:, :, :], ends[0:1, :].unsqueeze(1).to_broadcast([1, NX, NE]), jj[:, :, :], ALU.is_le)
                did(dve.tensor_reduce(which[:, :], before[:, :, :], AX.X, ALU.add))
                did(dve.tensor_scalar(which[:, :], which[:, :], float(NE - 1), None, ALU.min))
                did(dve.tensor_copy(k_.blocks[:, 0:NX], which[:, :]))
                did(dve.tensor_copy(k_.blocks[:, NX:NX + 1], ends[0:1, NE - 1:NE]))

    def load_piece(self, eng, piece, kind, half, e, first=False):
        j, m = piece
        if not first:
            eng.wait_ge(self.e_lo[m % 3], 2 * j + m // 3 - 1)
        w = self.ins["w_exp_" + kind][0][e].rearrange("(k p) n -> p k n", p=P)
        src = w[:, :, half * HALF:(half + 1) * HALF] if kind == "down" else w[:, 4 * half:4 * half + 4, :]
        eng.dma_start(self.e_raw[m % 6][:, :, :], src).then_inc(self.e_in[m % 6], 16)

    def piece_hi(self, act, piece):
        j, m = piece
        act.wait_ge(self.e_in[m % 6], 16 * (j + m // 6 + 1))
        act.wait_ge(self.e_used[m % 3], 2 * j + m // 3)
        act.activation(self.e_h[m % 3][:, :, :], self.e_raw[m % 6][:, :, :], ACT.Copy).then_inc(self.e_hi[m % 3], 1)

    def piece_lo(self, dve, piece):
        j, m = piece
        dve.wait_ge(self.e_hi[m % 3], 2 * j + m // 3 + 1)
        dve.tensor_tensor(self.e_l[m % 3][:, :, :], self.e_raw[m % 6][:, :, :], self.e_h[m % 3][:, :, :].bitcast(F32),
                          ALU.subtract).then_inc(self.e_lo[m % 3], 1)

    def piece_done(self, eng, piece):
        j, m = piece
        eng.wait_ge(self.e_used[m % 3], 2 * j + m // 3 + 1)

    def piece_products(self, pe, ps, rows_h, rows_l, piece, first_piece, last_piece):
        j, m = piece
        pe.wait_ge(self.e_lo[m % 3], 2 * j + m // 3 + 1)
        w_h, w_l = self.e_h[m % 3], self.e_l[m % 3]
        for k in range(4):
            for x, w, first, last in ((rows_h, w_h, k == 0, False), (rows_h, w_l, False, False),
                                      (rows_l, w_h, False, k == 3)):
                mm = pe.matmul(ps, x[:, k, :], w[:, k, :], start=first and first_piece, stop=last and last_piece)
        mm.then_inc(self.e_used[m % 3], 1)

    def experts(self):
        nc, k_ = self.nc, self
        work, high = Map(nc, self.raw_end, self.work_start), Map(nc, self.x2_end, self.high)
        k_.e_h = [work.put(f"e_h{s}", [P, 4, HALF], F32R) for s in range(3)]
        k_.e_l = [work.put(f"e_l{s}", [P, 4, HALF], F32R) for s in range(3)]
        xg = [high.put(f"e_xg{b}", [P, D]) for b in range(2)]
        xt_h = [work.put(f"e_xth{b}", [P, KD, P], F32R) for b in range(2)]
        xt_l = [work.put(f"e_xtl{b}", [P, KD, P], F32R) for b in range(2)]
        silu = work.put("e_silu", [P, FE])
        hid = work.put("e_hid", [P, FE])
        y_sb = [high.put(f"e_y{b}", [P, D]) for b in range(2)]
        ht_h = high.put("e_hth", [P, 4, P], F32R)
        ht_l = high.put("e_htl", [P, 4, P], F32R)
        idx = [high.put(f"e_idx{b}", [P, 1], I32) for b in range(2)]
        sem = self.sem
        idx_in, gathered, y_stored = ([sem(f"e_{n}{b}") for b in range(2)] for n in ("idx", "gathered", "stored"))
        x_mm, x_hi, x_lo, silu_out, hid_out, h_mm, h_hi, h_lo, y_out = (
            sem("e_" + n) for n in ("x_mm", "x_hi", "x_lo", "silu", "hid", "h_mm", "h_hi", "h_lo", "y_out"))
        ps_x, ps_g, ps_u = k_.ps[0], k_.ps[1][:, 0:HALF], k_.ps[1][:, HALF:2 * HALF]
        ps_h, ps_y = k_.ps[2][:, 0:HALF], k_.ps[3]
        n_over = MAXX

        def load_slots(pool, j, b):
            pool.dma_start(idx[b][:, :], k_.slots_d[bass.ds(BLK * j, BLK), :]).then_inc(idx_in[b], 16)

        def gather(pool, j, b):
            if not (type(j) is int and j < 2):
                pool.wait_ge(x_mm, j - 1)
            if not (type(j) is int and j < 1):
                pool.wait_ge(gathered[1 - b], 16 * ((j + 1) // 2))
            pool.wait_ge(idx_in[b], 16 * (j // 2 + 1))
            load_slots(pool, j + 1, 1 - b)
            pool.indirect_dma_start(out=xg[b][:, :], out_offset=None, in_=k_.xn_d,
                                    in_offset=bass.IndirectOffsetOnAxis(ap=idx[b][:, 0:1], axis=0))\
                .then_inc(gathered[b], 16)

        def turn_x(pe, j, b):
            pe.wait_ge(gathered[b], 16 * (j // 2 + 1))
            pe.wait_ge(x_lo, j)
            for k in range(KD):
                mm = pe.transpose(ps_x[:, k * P:(k + 1) * P], xg[b][:, k * P:(k + 1) * P], k_.ident[:, :])
            mm.then_inc(x_mm, 1)

        def gate(pe, j, b, half, piece):
            if half == 0:
                pe.wait_ge(x_lo, j + 1)
                pe.wait_ge(silu_out, j)
            ks = slice(4 * half, 4 * half + 4)
            k_.piece_products(pe, ps_g, xt_h[b][:, ks, :], xt_l[b][:, ks, :], piece, half == 0, half == 1)

        def up(pe, j, b, half, piece):
            if half == 0:
                pe.wait_ge(hid_out, j)
            ks = slice(4 * half, 4 * half + 4)
            k_.piece_products(pe, ps_u, xt_h[b][:, ks, :], xt_l[b][:, ks, :], piece, half == 0, half == 1)

        def turn_h(pe, j):
            pe.wait_ge(hid_out, j + 1)
            pe.wait_ge(h_lo, j)
            for k in range(4):
                mm = pe.transpose(ps_h[:, k * P:(k + 1) * P], hid[:, k * P:(k + 1) * P], k_.ident[:, :])
            mm.then_inc(h_mm, 1)

        def down(pe, j, half, piece):
            if half == 0:
                pe.wait_ge(h_lo, j + 1)
                pe.wait_ge(y_out, j)
            k_.piece_products(pe, ps_y[:, half * HALF:(half + 1) * HALF], ht_h, ht_l, piece, True, True)

        def x_high(act, j, b, used):
            act.wait_ge(x_mm, j + 1)
            if used is not None:
                k_.piece_done(act, used)
            act.activation(xt_h[b][:, :, :].rearrange("p k t -> p (k t)"), ps_x[:, :], ACT.Copy).then_inc(x_hi, 1)

        def x_low(dve, j, b):
            dve.wait_ge(x_hi, j + 1)
            dve.tensor_tensor(xt_l[b][:, :, :].rearrange("p k t -> p (k t)"), ps_x[:, :],
                              xt_h[b][:, :, :].rearrange("p k t -> p (k t)").bitcast(F32), ALU.subtract).then_inc(x_lo, 1)

        def act_silu(act, j, gate_piece):
            k_.piece_done(act, gate_piece)
            act.wait_ge(hid_out, j)
            act.activation(silu[:, :], ps_g, ACT.Silu).then_inc(silu_out, 1)

        def hidden(dve, j, up_piece):
            dve.wait_ge(silu_out, j + 1)
            k_.piece_done(dve, up_piece)
            dve.wait_ge(h_mm, j)
            dve.tensor_tensor(hid[:, :], silu[:, :], ps_u, ALU.mult).then_inc(hid_out, 1)

        def h_high(act, j, last_down):
            act.wait_ge(h_mm, j + 1)
            if last_down is not None:
                k_.piece_done(act, last_down)
            act.activation(ht_h[:, :, :].rearrange("p k t -> p (k t)"), ps_h, ACT.Copy).then_inc(h_hi, 1)

        def h_low(dve, j):
            dve.wait_ge(h_hi, j + 1)
            dve.tensor_tensor(ht_l[:, :, :].rearrange("p k t -> p (k t)"), ps_h,
                              ht_h[:, :, :].rearrange("p k t -> p (k t)").bitcast(F32), ALU.subtract).then_inc(h_lo, 1)

        def rows_out(act, j, b, down_piece):
            k_.piece_done(act, down_piece)
            act.wait_ge(y_stored[b], 16 * (j // 2))
            act.activation(y_sb[b][:, :], ps_y[:, :], ACT.Copy).then_inc(y_out, 1)
            act.wait_ge(y_out, j + 1)
            act.dma_start(k_.y_d[bass.ds(BLK * j, BLK), :], y_sb[b][:, :]).then_inc(y_stored[b], 16)

        def in_pairs(engine, body, from_pair, to_pair):
            with engine.Fori(from_pair, to_pair) as i:
                for b in range(2):
                    body(2 * i + b, b)

        def beyond(engine, body):
            n = engine.value_load(k_.blocks[0:1, n_over:n_over + 1], min_val=0, max_val=MAXX)
            with engine.Fori(0, MAXX // 2) as i:
                for b in range(2):
                    with engine.If(2 * i + b < n):
                        body(NE + 2 * i + b, b, 2 * i + b)
            return n

        listed = lambda engine, at, most: engine.value_load(k_.blocks[0:1, bass.ds(at, 1)], min_val=0, max_val=most)

        with nc.Block() as block:
            @block.sync
            def _(sp):
                def body(j, b, last=False):
                    for m, kind, half, e in ((6, "down", 0, j), (7, "down", 1, j), (8, "up", 0, j + 1), (9, "up", 1, j + 1),
                                             (10, "gate", 0, j + 2), (11, "gate", 1, j + 2)):
                        if not (last and m > 9):
                            k_.load_piece(sp, (j, m), kind, half, e)
                in_pairs(sp, body, 0, NE // 2 - 1)
                body(NE - 2, 0, True)
                for m in (4, 5):
                    k_.load_piece(sp, (NE - 1, m), "down", m - 4, NE - 1)

                def other(j, b, t):
                    e = listed(sp, t, NE - 1)
                    for m in range(6):
                        k_.load_piece(sp, (j, m), ("gate", "up", "down")[m // 2], m % 2, e)
                beyond(sp, other)

            @block.gpsimd
            def _(pool):
                load_slots(pool, 0, 0)
                gather(pool, 0, 0)
                gather(pool, 1, 1)
                in_pairs(pool, lambda j, b: gather(pool, j, b), 1, NE // 2)
                n = beyond(pool, lambda j, b, t: gather(pool, j, b))
                pool.wait_ge(y_stored[0], 16 * (NE // 2 + (n + 1) // 2))
                pool.wait_ge(y_stored[1], 16 * (NE // 2 + n // 2))
                pool.wait_ge(idx_in[0], 16 * (NE // 2 + n // 2 + 1))
                pool.wait_ge(idx_in[1], 16 * (NE // 2 + (n + 1) // 2))

            @block.tensor
            def _(pe):
                turn_x(pe, 0, 0)
                for h in range(2):
                    gate(pe, 0, 0, h, (0, h))

                def body(j, b):
                    up(pe, j, b, 0, (j, 2))
                    turn_x(pe, j + 1, 1 - b)
                    up(pe, j, b, 1, (j, 3))
                    gate(pe, j + 1, 1 - b, 0, (j, 4))
                    turn_h(pe, j)
                    gate(pe, j + 1, 1 - b, 1, (j, 5))
                    for h in range(2):
                        down(pe, j, h, (j, 6 + h))
                in_pairs(pe, body, 0, NE // 2 - 1)
                body(NE - 2, 0)
                j = NE - 1
                for h in range(2):
                    up(pe, j, 1, h, (j, 2 + h))
                turn_h(pe, j)
                for h in range(2):
                    down(pe, j, h, (j, 4 + h))

                def other(j, b, t):
                    turn_x(pe, j, b)
                    for h in range(2):
                        gate(pe, j, b, h, (j, h))
                    for h in range(2):
                        up(pe, j, b, h, (j, 2 + h))
                    turn_h(pe, j)
                    for h in range(2):
                        down(pe, j, h, (j, 4 + h))
                beyond(pe, other)

            @block.scalar
            def _(act):
                k_.piece_hi(act, (0, 0))
                x_high(act, 0, 0, None)
                for m in (1, 2, 3):
                    k_.piece_hi(act, (0, m))

                def body(j, b, first=False):
                    act_silu(act, j, (j - 1, 5) if not first else (0, 1))
                    k_.piece_hi(act, (j, 4))
                    x_high(act, j + 1, 1 - b, (j - 1, 3) if not first else None)
                    for m in (5, 6):
                        k_.piece_hi(act, (j, m))
                    h_high(act, j, (j - 1, 7) if not first else None)
                    for m in (7, 8, 9):
                        k_.piece_hi(act, (j, m))
                    rows_out(act, j, b, (j, 7))
                body(0, 0, True)
                body(1, 1)
                in_pairs(act, body, 1, NE // 2 - 1)
                body(NE - 2, 0)
                j = NE - 1
                act_silu(act, j, (j - 1, 5))
                for m in (4, 5):
                    k_.piece_hi(act, (j, m))
                h_high(act, j, (j - 1, 7))
                rows_out(act, j, 1, (j, 5))

                def other(j, b, t):
                    k_.piece_hi(act, (j, 0))
                    x_high(act, j, b, (j - 1, 3))
                    for m in (1, 2, 3):
                        k_.piece_hi(act, (j, m))
                    act_silu(act, j, (j, 1))
                    for m in (4, 5):
                        k_.piece_hi(act, (j, m))
                    h_high(act, j, (j - 1, 5))
                    rows_out(act, j, b, (j, 5))
                beyond(act, other)

            @block.vector
            def _(dve):
                k_.piece_lo(dve, (0, 0))
                x_low(dve, 0, 0)
                for m in (1, 2, 3):
                    k_.piece_lo(dve, (0, m))

                def body(j, b):
                    k_.piece_lo(dve, (j, 4))
                    x_low(dve, j + 1, 1 - b)
                    k_.piece_lo(dve, (j, 5))
                    hidden(dve, j, (j, 3))
                    k_.piece_lo(dve, (j, 6))
                    h_low(dve, j)
                    for m in (7, 8, 9):
                        k_.piece_lo(dve, (j, m))
                in_pairs(dve, body, 0, NE // 2 - 1)
                body(NE - 2, 0)
                j = NE - 1
                k_.piece_lo(dve, (j, 4))
                hidden(dve, j, (j, 3))
                k_.piece_lo(dve, (j, 5))
                h_low(dve, j)

                def other(j, b, t):
                    k_.piece_lo(dve, (j, 0))
                    x_low(dve, j, b)
                    for m in (1, 2, 3, 4):
                        k_.piece_lo(dve, (j, m))
                    hidden(dve, j, (j, 3))
                    k_.piece_lo(dve, (j, 5))
                    h_low(dve, j)
                beyond(dve, other)

    def combine(self):
        nc, k_ = self.nc, self
        work = Map(nc, self.fixed_end, self.work_start)
        RING = 4
        yg = [[work.put(f"cb_y{r}{s}", [P, D]) for s in range(2)] for r in range(RING)]
        ob = [work.put(f"cb_o{b}", [P, D]) for b in range(2)]
        g_b, square = work.put("cb_g", [P, D]), work.put("cb_square", [P, D])
        total, mean, rstd, power = (work.put(f"cb_{n}", [P, NT]) for n in ("total", "mean", "rstd", "power"))
        sem = self.sem
        got = [[sem(f"cb_got{r}{s}") for s in range(2)] for r in range(RING)]
        g_in, const, first, added, squared, averaged, powered, normed = (
            sem("cb_" + n) for n in ("g", "const", "first", "added", "squared", "averaged", "powered", "normed"))
        stored = [sem(f"cb_stored{b}") for b in range(2)]

        with nc.Block() as block:
            @block.gpsimd
            def _(pool):
                pool.memset(power[:, :], -0.5).then_inc(const, 1)
                pool.wait_ge(const, 1)

                def root(t):
                    pool.wait_ge(averaged, t + 1)
                    pool.tensor_tensor(rstd[:, t:t + 1], mean[:, t:t + 1], power[:, t:t + 1], ALU.pow).then_inc(powered, 1)
                for t in range(NT):
                    if t >= RING:
                        pool.wait_ge(added, t - RING + 1)
                    for s in range(2):
                        pool.indirect_dma_start(
                            out=yg[t % RING][s][:, :], out_offset=None, in_=k_.y_d,
                            in_offset=bass.IndirectOffsetOnAxis(ap=k_.dest[:, s, t:t + 1], axis=0))\
                            .then_inc(got[t % RING][s], 16)
                    if t >= RING - 1:
                        root(t - RING + 1)
                for t in range(NT - RING + 1, NT):
                    root(t)

            @block.sync
            def _(sp):
                sp.dma_start(g_b[:, :], k_.ins["g_final"].partition_broadcast(P)).then_inc(g_in, 16)
                for t in range(NT):
                    sp.wait_ge(normed, t + 1)
                    sp.dma_start(k_.out[t * P:(t + 1) * P, :], ob[t % 2][:, :]).then_inc(stored[t % 2], 16)
                for b in range(2):
                    sp.wait_ge(stored[b], 16 * NT // 2)

            @block.scalar
            def _(act):
                for t in range(NT):
                    act.wait_ge(added, t + 1)
                    act.activation(square[:, :], k_.x2[:, t, :], ACT.Square, accum_out=total[:, t:t + 1]).then_inc(squared, 1)
                    act.wait_ge(squared, t + 1)

            @block.vector
            def _(dve):
                def norm(t):
                    dve.wait_ge(powered, t + 1)
                    if t >= 2:
                        dve.wait_ge(stored[t % 2], 16 * (t // 2))
                    dve.scalar_tensor_tensor(out=ob[t % 2][:, :], in0=k_.x2[:, t, :], scalar=rstd[:, t:t + 1],
                                             in1=g_b[:, :], op0=ALU.mult, op1=ALU.mult).then_inc(normed, 1)
                dve.wait_ge(g_in, 16)
                for t in range(NT):
                    x2 = k_.x2[:, t, :]
                    for s in range(2):
                        dve.wait_ge(got[t % RING][s], 16 * (t // RING + 1))
                        dve.scalar_tensor_tensor(out=x2, in0=yg[t % RING][s][:, :], scalar=k_.wgt[:, s, t:t + 1], in1=x2,
                                                 op0=ALU.mult, op1=ALU.add).then_inc((first, added)[s], 1)
                        if s == 0:
                            dve.wait_ge(first, t + 1)
                    if t >= 1:
                        norm(t - 1)
                    dve.wait_ge(squared, t + 1)
                    dve.tensor_scalar(mean[:, t:t + 1], total[:, t:t + 1], 1.0 / D, EPS, ALU.mult, ALU.add)\
                        .then_inc(averaged, 1)
                norm(NT - 1)

    def write(self):
        for write, *args in ((self.norm_in,), (self.lru_qk,), (self.value,), (self.merge_gates,),
                             (self.branch_out, 0), (self.attention,), (self.branch_out, 1), (self.project,),
                             (self.route,), (self.experts,), (self.combine,)):
            self.stage(write, *args)


NAMES = ("x", "g_mix", "w_in", "conv_w", "conv_b", "w_rg_a", "b_rg_a", "w_rg_x", "b_rg_x", "lru_lambda", "b_forget",
         "w_lru_out", "w_attn_out", "w_out", "g_ffn", "w_route_group", "b_route_group", "w_route_expert",
         "b_route_expert", "w_exp_gate", "w_exp_up", "w_exp_down", "g_final")


def kernel(**inputs):
    import numpy as np
    import concourse.bacc as bacc
    from concourse.bass_utils import run_bass_kernel_spmd

    nc = bacc.Bacc("TRN2", target_bir_lowering=False, num_devices=1)
    arrays = {name: np.ascontiguousarray(inputs[name]) for name in NAMES}
    ins = {name: nc.dram_tensor(name, a.shape, mybir.dt.from_np(a.dtype), kind="ExternalInput").ap()
           for name, a in arrays.items()}
    out = nc.dram_tensor("out", (T, D), F32, kind="ExternalOutput").ap()
    Kernel(nc, ins, out).write()
    result = run_bass_kernel_spmd(nc, [arrays], core_ids=[0])
    return result.results[0]["out"].reshape(1, T, D)
```

```python
import concourse.bass as bass
from concourse import mybir

F32 = mybir.dt.float32
F32R = mybir.dt.float32r
I32 = mybir.dt.int32
ALU = mybir.AluOpType
ACT = mybir.ActivationFunctionType
AX = mybir.AxisListType

P = 128
D = 1024
T = 1024
KD = D // P
NT = T // P
HALF = 512
NH = 8
HD = D // NH
WB = 256
CONV_W = 4
LRU_C = 8.0
EPS = 1e-6
NG = 4
EG = 8
NE = NG * EG
FE = 512
XR, GR, QC, KC, VC, FL, ML, MA = 0, D, 2 * D, 3 * D, 4 * D, 5 * D, 5 * D + NH, 6 * D + NH
NEG = -3.0e38
PW, PB, PBA, PBX, PS, PN, NPRM = 0, 4, 5, 6, 7, 8, 9
BLK = 96
MOST = -(-T // BLK)
MAXX = 2 * T // BLK + 2 * T // BLK % 2
RAW, SPLIT = 12, 3
SLOTS = (NE + MAXX) * BLK


class Map:

    def __init__(self, nc, start, end):
        self.nc, self.at, self.end = nc, start, end

    def put(self, name, shape, dt=F32):
        size = 4
        for n in shape[1:]:
            size *= n
        place = self.nc.alloc_sbuf_tensor_at(name, shape, dt, offset=self.at)
        self.at += (size + 31) // 32 * 32
        assert self.at <= self.end, (name, self.at, self.end)
        return place


class Steps:

    def __init__(self, engine, sem, start=0):
        self.engine, self.sem, self.start, self.n = engine, sem, start, 0

    def did(self, instruction):
        instruction.then_inc(self.sem, 1)
        self.n += 1
        self.engine.wait_ge(self.sem, self.start + self.n)


class Kernel:
    def __init__(self, nc, ins, out):
        self.nc, self.out = nc, out
        self.x, self.g_mix, self.w_in = ins["x"][0], ins["g_mix"][0], ins["w_in"][0]
        self.ins = ins
        dram = lambda name, shape, dt=F32: nc.dram_tensor(name, shape, dt).ap()
        self.qk_d = dram("qk_d", (NH, P, 4, T))
        self.v_d = dram("v_d", (NH // 2, 2, P, NT, WB))
        self.sig_d = dram("sig_d", (2, KD, P, T))
        self.c_d = dram("c_d", (NH, 2, 4, T))
        self.o_d = dram("o_d", (NH, P, T))
        self.xn_d = dram("xn_d", (T, D))
        self.slots_d = dram("slots_d", (SLOTS + BLK, 1), I32)
        self.y_d = dram("y_d", (SLOTS, D))
        self.stage_sems = []
        low, high = (nc.SBUF_PARTITION_SIZE_BYTES - nc.sbuf_bytes_remaining + 31) // 32 * 32, nc.sbuf_usable_end
        fixed = Map(nc, low, high)
        self.ident = fixed.put("ident", [P, P])
        self.ones = fixed.put("ones", [P, P])
        self.zeros = fixed.put("zeros", [P, P])
        self.stri = fixed.put("stri", [P, P])
        self.gm = fixed.put("gm", [P, KD])
        self.prm = fixed.put("prm", [P, KD, NPRM])
        self.wgt = fixed.put("wgt", [P, 2, NT])
        self.dest = fixed.put("dest", [P, 2, NT], I32)
        self.slots_i = fixed.put("slots_i", [P, NE], I32)
        self.blocks = fixed.put("blocks", [1, 32], I32)
        mixer = Map(nc, fixed.at, high)
        low = fixed.at
        self.w_raw = [mixer.put(f"w_raw{s}", [P, KD, WB]) for s in range(2)]
        self.w_h = [mixer.put(f"w_h{s}", [P, KD, WB], F32R) for s in range(2)]
        self.w_l = [Map(nc, low + s * 4 * KD * WB, high).put(f"w_l{s}", [P, KD, WB], F32R) for s in range(2)]
        self.act_start, self.high, self.fixed_end = mixer.at, high, fixed.at
        self.uh = mixer.put("uh", [P, KD, T], F32R)
        self.ul = mixer.put("ul", [P, KD, T], F32R)
        self.mix = mixer.put("mix", [P, KD, T])
        self.work_start = mixer.at
        self.w_loaded = [self.sem(f"w_loaded{s}") for s in range(2)]
        self.w_hi = [self.sem(f"w_hi{s}") for s in range(2)]
        self.w_lo = [self.sem(f"w_lo{s}") for s in range(2)]
        self.w_first = [self.sem(f"w_first{s}") for s in range(2)]
        self.w_used = [self.sem(f"w_used{s}") for s in range(2)]
        self.pairs = 0
        self.e_in = [self.sem(f"e_in{r}") for r in range(RAW)]
        self.e_hi, self.e_lo, self.e_used = ([self.sem(f"e_{n}{s}") for s in range(SPLIT)] for n in ("hi", "lo", "used"))
        stores = lambda name: [self.sem(f"{name}_stored{c}") for c in range(2)]
        self.qk_stored, self.v_stored, self.o_stored = stores("qk"), stores("v"), stores("o")
        self.sig_stored = [stores(f"sig{s}") for s in range(2)]
        self.rows_stored = self.sem("c_stored")
        self.qk_in, self.v_in, self.c_in = ([self.sem(f"at_{n}_in{c}") for c in range(2)] for n in ("qk", "v", "c"))
        self.ps = [nc.alloc_psum_tensor(f"ps{t}", [P, 2 * HALF], F32) for t in range(4)]

    def sem(self, name):
        self.stage_sems.append(self.nc.alloc_semaphore(name))
        return self.stage_sems[-1]

    def stage(self, write, *args):
        self.stage_sems = []
        write(*args)
        self.nc.clear_and_free_semaphores(self.stage_sems)
        self.nc.all_engine_barrier(sem_only=True)

    def work(self):
        return Map(self.nc, self.work_start, self.high)

    def load_block(self, eng, s, p, src):
        if type(p) is not int or p > 0:
            eng.wait_ge(self.w_used[s], p)
        eng.dma_start(self.w_raw[s][:, :, :], src).then_inc(self.w_loaded[s], 16)

    def split_hi(self, act, s, p):
        act.wait_ge(self.w_loaded[s], 16 * (p + 1))
        act.wait_ge(self.w_used[s], p)
        act.activation(self.w_h[s][:, :, :], self.w_raw[s][:, :, :], ACT.Copy).then_inc(self.w_hi[s], 1)

    def split_lo(self, dve, s, p):
        dve.wait_ge(self.w_hi[s], p + 1)
        dve.tensor_tensor(self.w_l[s][:, :, :], self.w_raw[s][:, :, :], self.w_h[s][:, :, :].bitcast(F32),
                          ALU.subtract).then_inc(self.w_lo[s], 1)

    def w_block(self, w, col):
        return w.rearrange("(k p) n -> p k n", p=P)[:, :, bass.ds(col, WB)]

    def product(self, pe, ps, s, c, chunks_in=None):
        wh, wl = (w[s][:, :, c * P:(c + 1) * P] for w in (self.w_h, self.w_l))
        for k in range(KD):
            if chunks_in is not None:
                pe.wait_ge(chunks_in, k + 1)
            for w, u, first, last in ((wh, self.uh, k == 0, False), (wh, self.ul, False, False),
                                      (wl, self.uh, False, k == KD - 1)):
                for h in range(2):
                    mm = pe.matmul(ps[:, h * HALF:(h + 1) * HALF], w[:, k, :], u[:, k, h * HALF:(h + 1) * HALF],
                                   start=first, stop=last)
        return mm

    def product_rows(self, pe, ps, s, tile, chunks_in=None):
        rows = slice(tile * P, (tile + 1) * P)
        for k in range(KD):
            if chunks_in is not None:
                pe.wait_ge(chunks_in, k + 1)
            for u, w, first, last in ((self.uh, self.w_h, k == 0, False), (self.uh, self.w_l, False, False),
                                      (self.ul, self.w_h, False, k == KD - 1)):
                mm = pe.matmul(ps, u[:, k, rows], w[s][:, k, :], start=first, stop=last)
        return mm

    def norm_in(self):
        nc, k_ = self.nc, self
        work = self.work()
        square = work.put("na_square", [P, D])
        total = work.put("na_total", [P, NT])
        mean = work.put("na_mean", [P, NT])
        rstd = work.put("na_rstd", [P, NT])
        power = work.put("na_power", [P, NT])
        n_rows = (CONV_W + 5) * KD
        rows = work.put("na_rows", [n_rows, P])
        e, w1, dw, ln, eq = (work.put(f"na_{n}", [P, KD]) for n in ("e", "w1", "dw", "ln", "eq"))
        x_loaded = [self.sem(f"na_x{t}") for t in range(NT)]
        prm_loaded, prm_mm, prm_turned = self.sem("na_prm"), self.sem("na_prm_mm"), self.sem("na_prm_turned")
        consts = self.sem("na_consts")
        squared, averaged, powered, scaled = (self.sem(f"na_{n}") for n in ("squared", "averaged", "powered", "scaled"))
        turned, high, low = self.sem("na_turned"), self.sem("na_high"), self.sem("na_low")
        sp_exp, sp_one, sp_ln, own = (self.sem(f"na_{n}") for n in ("sp_exp", "sp_one", "sp_ln", "own"))
        xt = self.mix
        ins = self.ins
        vectors = [ins["conv_w"]] + [ins[n] for n in ("conv_b", "b_rg_a", "b_rg_x", "lru_lambda", "g_mix")]
        turn = k_.ps[3][:, HALF:HALF + n_rows]
        turn_v = turn.rearrange("p (v k) -> p k v", k=KD)

        with nc.Block() as block:
            @block.sync
            def _(sp):
                for t in range(NT):
                    sp.dma_start(xt[:, t, :], k_.x[t * P:(t + 1) * P, :]).then_inc(x_loaded[t], 16)
                for s, col in enumerate((XR, GR)):
                    k_.load_block(sp, s, 0, k_.w_block(k_.w_in, col))

            @block.scalar
            def _(act):
                row = 0
                for src in vectors:
                    if src is vectors[0]:
                        n, flat = CONV_W * KD, src.rearrange("a j (k p) -> (a j k) p", p=P)
                    else:
                        n, flat = KD, src.rearrange("a (k p) -> (a k) p", p=P)
                    act.dma_start(rows[row:row + n, :], flat).then_inc(prm_loaded, 16)
                    row += n
                for t in range(NT):
                    if t == NT // 2:
                        act.wait_ge(prm_turned, 2)
                        act.activation(e[:, :], k_.prm[:, :, PS], ACT.Exp, scale=-1.0).then_inc(sp_exp, 1)
                        act.wait_ge(sp_one, 1)
                        act.activation(ln[:, :], w1[:, :], ACT.Ln).then_inc(sp_ln, 1)
                    act.wait_ge(x_loaded[t], 16)
                    act.activation(square[:, :], xt[:, t, :], ACT.Square,
                                   accum_out=total[:, t:t + 1]).then_inc(squared, 1)
                    act.wait_ge(squared, t + 1)
                k_.split_hi(act, 0, 0)
                for h in range(2):
                    for k in range(KD):
                        act.wait_ge(turned, h * KD + k + 1)
                        act.activation(k_.uh[:, k, h * HALF:(h + 1) * HALF], k_.ps[k % 4][:, 0:HALF], ACT.Copy,
                                       scale=k_.gm[:, k:k + 1]).then_inc(high, 1)

            @block.gpsimd
            def _(pool):
                pool.memset(power[:, :], -0.5).then_inc(consts, 1)
                pool.memset(k_.ones[:, :], 1.0).then_inc(consts, 1)
                pool.wait_ge(consts, 2)
                pool.affine_select(out=k_.ident[:, :], in_=k_.ones[:, :], compare_op=ALU.is_equal, fill=0.0,
                                   base=0, pattern=[[-1, P]], channel_multiplier=1).then_inc(consts, 1)
                pool.affine_select(out=k_.stri[:, :], in_=k_.ones[:, :], compare_op=ALU.is_gt, fill=0.0,
                                   base=0, pattern=[[1, P]], channel_multiplier=-1).then_inc(consts, 1)
                pool.wait_ge(averaged, 1)
                pool.tensor_tensor(rstd[:, :], mean[:, :], power[:, :], ALU.pow).then_inc(powered, 1)

            @block.tensor
            def _(pe):
                pe.wait_ge(consts, 4)
                pe.wait_ge(prm_loaded, 16 * len(vectors))
                pe.transpose(turn, rows[:, :], k_.ident[0:n_rows, 0:n_rows]).then_inc(prm_mm, 1)
                for h in range(2):
                    pe.wait_ge(scaled, 4 * h + 4)
                    for k in range(KD):
                        n = h * KD + k
                        if n >= 4:
                            pe.wait_ge(low, n - 3)
                        for t in range(4):
                            mm = pe.transpose(k_.ps[k % 4][:, t * P:(t + 1) * P],
                                              xt[:, 4 * h + t, k * P:(k + 1) * P], k_.ident[:, :])
                        mm.then_inc(turned, 1)

            @block.vector
            def _(dve):
                steps = Steps(dve, own)
                dve.wait_ge(prm_mm, 1)
                dve.tensor_copy(k_.prm[:, :, 0:PN], turn_v[:, :, 0:PN]).then_inc(prm_turned, 1)
                dve.tensor_copy(k_.gm[:, :], turn[:, PN * KD:(PN + 1) * KD]).then_inc(prm_turned, 1)
                dve.wait_ge(sp_exp, 1)
                dve.tensor_scalar(w1[:, :], e[:, :], 1.0, None, ALU.add).then_inc(sp_one, 1)
                dve.wait_ge(sp_one, 1)
                steps.did(dve.tensor_scalar(dw[:, :], w1[:, :], -1.0, None, ALU.add))
                steps.did(dve.tensor_scalar(eq[:, :], dw[:, :], 0.0, None, ALU.is_equal))
                steps.did(dve.tensor_tensor(dw[:, :], dw[:, :], eq[:, :], ALU.add))
                steps.did(dve.reciprocal(dw[:, :], dw[:, :]))
                dve.wait_ge(sp_ln, 1)
                steps.did(dve.tensor_tensor(eq[:, :], eq[:, :], ln[:, :], ALU.add))
                steps.did(dve.tensor_tensor(eq[:, :], eq[:, :], dw[:, :], ALU.mult))
                steps.did(dve.tensor_tensor(eq[:, :], eq[:, :], e[:, :], ALU.mult))
                dve.tensor_scalar(k_.prm[:, :, PS], eq[:, :], LRU_C / 2, None, ALU.mult).then_inc(own, 1)
                dve.tensor_scalar(k_.prm[:, :, PN], eq[:, :], -LRU_C, None, ALU.mult).then_inc(own, 1)
                dve.wait_ge(squared, NT)
                dve.tensor_scalar(mean[:, :], total[:, :], 1.0 / D, EPS, ALU.mult, ALU.add).then_inc(averaged, 1)
                dve.wait_ge(powered, 1)
                for t in range(NT):
                    dve.tensor_scalar(xt[:, t, :], xt[:, t, :], rstd[:, t:t + 1], None, ALU.mult).then_inc(scaled, 1)
                k_.split_lo(dve, 0, 0)
                for h in range(2):
                    for k in range(KD):
                        dve.wait_ge(high, h * KD + k + 1)
                        dve.scalar_tensor_tensor(out=k_.ul[:, k, h * HALF:(h + 1) * HALF],
                                                 in0=k_.ps[k % 4][:, 0:HALF], scalar=k_.gm[:, k:k + 1],
                                                 in1=k_.uh[:, k, h * HALF:(h + 1) * HALF].bitcast(F32),
                                                 op0=ALU.mult, op1=ALU.subtract).then_inc(low, 1)

    def lru_qk(self):
        nc, k_ = self.nc, self
        turns = D // WB
        p0, self.pairs = self.pairs, self.pairs + 2 * turns
        work = self.work()
        rg_raw = work.put("rg_raw", [P, 2, 2, WB])
        rg_h = work.put("rg_h", [P, 2, 2, WB], F32R)
        rg_l = work.put("rg_l", [P, 2, 2, WB], F32R)
        cur = work.put("lru_prm", [P, 2, NPRM])
        pad = CONV_W - 1
        xr = work.put("lru_xr", [P, 2, T + 8])
        xc = work.put("lru_xc", [P, 2, T])
        xc_h = work.put("lru_xch", [P, 2, T], F32R)
        xc_l = work.put("lru_xcl", [P, 2, T], F32R)
        root_at = work.at - 2 * (2 * T * 4)
        rt_sb = Map(nc, root_at, work.at).put("lru_rt", [P, 2, T])
        a_sb = work.put("lru_a", [P, 2, T])
        i_sb = xr[:, :, pad:pad + T]
        gl = work.put("lru_gl", [P, 2, T])
        st = [work.put(f"qk_{c}", [P, 2, T], F32R) for c in range(2)]
        SCALE = (1.0, HD ** -0.5)
        sem = self.sem
        rg_loaded, rg_hi, rg_lo = (sem(f"rg_{n}") for n in ("loaded", "hi", "lo"))
        xr_out = [sem(f"lru_xr_out{c}") for c in range(2)]
        gr_out = [sem(f"lru_gr_out{c}") for c in range(2)]
        qk_hi, qk_lo = ([[sem(f"qk_{n}{g}{c}") for c in range(2)] for g in range(2)] for n in ("hi", "lo"))
        qk_stored = k_.qk_stored
        conv, xch_done, xcl_done = (sem(f"lru_{n}") for n in ("conv", "xch", "xcl"))
        gate_mm = [sem(f"lru_gate_mm{g}") for g in range(2)]
        gate_out = [sem(f"lru_gate_out{g}") for g in range(2)]
        t_done, a_done, root, mixed, own = (sem(f"lru_{n}") for n in ("t", "a", "root", "mixed", "own"))
        w_a, w_x = (self.ins[n][0].rearrange("b (c p) n -> b p c n", p=P) for n in ("w_rg_a", "w_rg_x"))
        zeroed, cleared, filled = sem("lru_zeroed"), sem("lru_cleared"), sem("lru_filled")
        zeros = self.zeros
        w_c = (k_.w_first, k_.w_used)

        with nc.Block() as block:
            @block.sync
            def _(sp):
                def gates(i):
                    sp.wait_ge(rg_lo, i)
                    for g, w in enumerate((w_a, w_x)):
                        sp.dma_start(rg_raw[:, g, :, :], w[i]).then_inc(rg_loaded, 16)

                def store(i, g, c):
                    sp.wait_ge(qk_lo[g][c], i + 1)
                    part = 2 - 2 * g
                    head = 2 * i + c if g == 0 else i + i + c
                    sp.dma_start(k_.qk_d[head][:, part:part + 2, :], st[c][:, :, :].bitcast(F32))\
                        .then_inc(qk_stored[c], 16)

                def turn(i, last):
                    for s, col in enumerate((KC, QC)):
                        k_.load_block(sp, s, p0 + 2 * i + 1, k_.w_block(k_.w_in, col + WB * i))
                    if not last:
                        gates(i + 1)
                    for s, col in enumerate((XR, GR)):
                        store(i, s, 0)
                        k_.load_block(sp, s, p0 + 2 * i + 2, k_.w_block(k_.w_in, VC + WB * s if last else col + WB + WB * i))
                        store(i, s, 1)
                gates(0)
                with sp.Fori(0, turns - 1) as i:
                    turn(i, False)
                turn(turns - 1, True)

            @block.gpsimd
            def _(pool):
                pool.memset(xr[:, :, 0:pad], 0.0).then_inc(zeroed, 1)
                pool.memset(zeros[:, :], 0.0).then_inc(cleared, 1)
                pool.wait_ge(cleared, 1)
                with pool.Fori(0, MAXX) as j:
                    pool.dma_start(k_.y_d[bass.ds(NE * BLK + BLK * j, BLK), :].rearrange("p (a n) -> p a n", n=P),
                                   zeros[0:BLK, :].unsqueeze(1).to_broadcast([BLK, D // P, P])).then_inc(filled, 16)
                pool.wait_ge(filled, 16 * MAXX)

            @block.tensor
            def _(pe):
                def products(i, s, pair, read, count):
                    pe.wait_ge(k_.w_lo[s], p0 + 2 * i + pair + 1)
                    for c in range(2):
                        pe.wait_ge(read[c], count)
                        k_.product(pe, k_.ps[c], s, c).then_inc(w_c[c][s], 1)

                with pe.Fori(0, turns) as i:
                    products(i, 0, 0, qk_lo[1], i)
                    products(i, 1, 0, xr_out, i + 1)
                    pe.wait_ge(rg_lo, i + 1)
                    pe.wait_ge(xcl_done, 2 * i + 2)
                    for m in range(2):
                        for g in range(2):
                            pe.wait_ge(gate_out[g], 2 * i + m)
                            for kk in range(2):
                                for w, u, first, last in ((rg_h, xc_h, kk == 0, False), (rg_h, xc_l, False, False),
                                                          (rg_l, xc_h, False, kk == 1)):
                                    for h in range(2):
                                        mm = pe.matmul(k_.ps[2 + g][:, h * HALF:(h + 1) * HALF],
                                                       w[:, g, kk, m * P:(m + 1) * P],
                                                       u[:, kk, h * HALF:(h + 1) * HALF], start=first, stop=last)
                            mm.then_inc(gate_mm[g], 1)
                    products(i, 0, 1, gr_out, i + 1)
                    products(i, 1, 1, qk_lo[0], i + 1)

            @block.scalar
            def _(act):
                def xr_copy(i, c):
                    act.wait_ge(w_c[c][0], p0 + 2 * i + 1)
                    act.activation(xr[:, c, pad:pad + T], k_.ps[c][:, :], ACT.Copy).then_inc(xr_out[c], 1)

                def conv_high(i, c):
                    act.wait_ge(conv, 2 * i + c + 1)
                    act.activation(xc_h[:, c, :], xc[:, c, :], ACT.Copy).then_inc(xch_done, 1)

                def gelu(i, c):
                    act.wait_ge(w_c[c][1], p0 + 2 * i + 1)
                    act.activation(gl[:, c, :], k_.ps[c][:, :], ACT.Gelu_apprx_tanh).then_inc(gr_out[c], 1)

                def qk_high(i, g, c):
                    act.wait_ge(w_c[c][g], p0 + 2 * i + 2)
                    act.wait_ge(qk_stored[c], 16 * (2 * i + g))
                    act.activation(st[c][:, 0, :], k_.ps[c][:, :], ACT.Copy, scale=SCALE[g]).then_inc(qk_hi[g][c], 1)

                with act.Fori(0, turns) as i:
                    k_.split_hi(act, 1, p0 + 2 * i)
                    act.wait_ge(mixed, 2 * i)
                    xr_copy(i, 0)
                    act.wait_ge(rg_loaded, 32 * (i + 1))
                    act.wait_ge(gate_mm[1], 2 * i)
                    act.activation(rg_h[:, :, :, :], rg_raw[:, :, :, :], ACT.Copy).then_inc(rg_hi, 1)
                    conv_high(i, 0)
                    xr_copy(i, 1)
                    k_.split_hi(act, 0, p0 + 2 * i + 1)
                    conv_high(i, 1)
                    for c in range(2):
                        gelu(i, c)
                    for m in range(2):
                        act.wait_ge(gate_mm[0], 2 * i + m + 1)
                        act.activation(a_sb[:, m, :], k_.ps[2][:, :], ACT.Sigmoid, bias=cur[:, m, PBA:PBA + 1])\
                            .then_inc(gate_out[0], 1)
                        act.wait_ge(gate_mm[1], 2 * i + m + 1)
                        act.activation(i_sb[:, m, :], k_.ps[3][:, :], ACT.Sigmoid, bias=cur[:, m, PBX:PBX + 1])\
                            .then_inc(gate_out[1], 1)
                    for m in range(2):
                        act.wait_ge(gate_out[0], 2 * i + m + 1)
                        act.activation(rt_sb[:, m, :], a_sb[:, m, :], ACT.Tanh, scale=cur[:, m, PS:PS + 1])\
                            .then_inc(t_done, 1)
                    for m in range(2):
                        act.wait_ge(t_done, 2 * i + m + 1)
                        act.activation(a_sb[:, m, :], a_sb[:, m, :], ACT.Exp, scale=cur[:, m, PN:PN + 1])\
                            .then_inc(a_done, 1)
                    act.activation(rt_sb[:, :, :], rt_sb[:, :, :], ACT.Sqrt).then_inc(root, 1)
                    k_.split_hi(act, 1, p0 + 2 * i + 1)
                    for c in range(2):
                        qk_high(i, 0, c)
                    k_.split_hi(act, 0, p0 + 2 * i + 2)
                    for c in range(2):
                        qk_high(i, 1, c)

            @block.vector
            def _(dve):
                PER = 15

                def qk_low(i, g, c):
                    dve.wait_ge(qk_hi[g][c], i + 1)
                    dve.scalar_tensor_tensor(out=st[c][:, 1, :], in0=k_.ps[c][:, :], scalar=SCALE[g],
                                             in1=st[c][:, 0, :].bitcast(F32), op0=ALU.mult,
                                             op1=ALU.subtract).then_inc(qk_lo[g][c], 1)

                dve.wait_ge(zeroed, 1)
                with dve.Fori(0, turns) as i:
                    steps = Steps(dve, own, i * PER)
                    dve.wait_ge(a_done, 2 * i)
                    steps.did(dve.tensor_scalar(cur[:, :, :], k_.prm[:, bass.ds(2 * i, 2), :], 1.0, None, ALU.mult))
                    k_.split_lo(dve, 1, p0 + 2 * i)
                    for c in range(2):
                        dve.wait_ge(xr_out[c], i + 1)
                        w = lambda j: cur[:, c, PW + j:PW + j + 1]
                        steps.did(dve.tensor_scalar(xc[:, c, :], xr[:, c, 0:T], w(0), cur[:, c, PB:PB + 1],
                                                    ALU.mult, ALU.add))
                        for j in range(1, CONV_W):
                            op = dve.scalar_tensor_tensor(out=xc[:, c, :], in0=xr[:, c, j:j + T], scalar=w(j),
                                                          in1=xc[:, c, :], op0=ALU.mult, op1=ALU.add)
                            if j < CONV_W - 1:
                                steps.did(op)
                        op.then_inc(conv, 1)
                        if c == 0:
                            dve.wait_ge(rg_hi, i + 1)
                            dve.tensor_tensor(rg_l[:, :, :, :], rg_raw[:, :, :, :], rg_h[:, :, :, :].bitcast(F32),
                                              ALU.subtract).then_inc(rg_lo, 1)
                        else:
                            k_.split_lo(dve, 0, p0 + 2 * i + 1)
                        dve.wait_ge(xch_done, 2 * i + c + 1)
                        dve.tensor_tensor(xc_l[:, c, :], xc[:, c, :], xc_h[:, c, :].bitcast(F32),
                                          ALU.subtract).then_inc(xcl_done, 1)
                    dve.wait_ge(a_done, 2 * i + 2)
                    dve.wait_ge(root, i + 1)
                    k_.split_lo(dve, 1, p0 + 2 * i + 1)
                    for m in range(2):
                        a = a_sb[:, m, :]
                        rt = rt_sb[:, m, :]
                        steps.did(dve.tensor_tensor(i_sb[:, m, :], i_sb[:, m, :], xc[:, m, :], ALU.mult))
                        qk_low(i, 0, m)
                        steps.did(dve.scalar_tensor_tensor(out=rt, in0=a, scalar=1.0, in1=rt, op0=ALU.add, op1=ALU.mult))
                        steps.did(dve.tensor_tensor(i_sb[:, m, :], i_sb[:, m, :], rt, ALU.mult))
                        steps.did(dve.tensor_tensor_scan(rt, a, i_sb[:, m, :], 0.0, ALU.mult, ALU.add))
                        dve.tensor_tensor(k_.mix[:, bass.ds(2 * i + m, 1), :].rearrange("p a t -> p (a t)"),
                                          rt, gl[:, m, :], ALU.mult).then_inc(mixed, 1)
                    k_.split_lo(dve, 0, p0 + 2 * i + 2)
                    for c in range(2):
                        qk_low(i, 1, c)
                    assert steps.n == PER

    def value(self):
        nc, k_ = self.nc, self
        n_pairs = D // WB // 2
        p0, self.pairs = self.pairs, self.pairs + n_pairs
        work = self.work()
        st = [[work.put(f"v_{s}{part}", [P, NT, WB], F32R) for part in range(2)] for s in range(2)]
        v_mm = [self.sem(f"v_mm{s}") for s in range(2)]
        hi, lo = ([self.sem(f"v_{n}{t}") for t in range(4)] for n in ("hi", "lo"))
        stored = k_.v_stored
        steps_of_slot = [(s, t) for s in range(2) for t in range(NT)]

        with nc.Block() as block:
            @block.sync
            def _(sp):
                def store(i, s):
                    for t in range(4):
                        sp.wait_ge(lo[t], 4 * i + 2 * s + 2)
                    for part in range(2):
                        sp.dma_start(k_.v_d[2 * i + s, part], st[s][part][:, :, :].bitcast(F32)).then_inc(stored[s], 16)
                with sp.Fori(0, n_pairs - 1) as i:
                    for s in range(2):
                        k_.load_block(sp, s, p0 + i + 1, k_.w_block(k_.w_in, VC + WB * (2 + s) + 2 * WB * i))
                        store(i, s)
                for s, col in enumerate((ML, MA)):
                    k_.load_block(sp, s, p0 + n_pairs, k_.w_block(k_.w_in, col))
                    store(n_pairs - 1, s)

            @block.tensor
            def _(pe):
                with pe.Fori(0, n_pairs) as i:
                    for s, t in steps_of_slot:
                        if t == 0:
                            pe.wait_ge(k_.w_lo[s], p0 + i + 1)
                        pe.wait_ge(lo[t % 4], 4 * i + 2 * s + t // 4)
                        mm = k_.product_rows(pe, k_.ps[t % 4][:, 0:WB], s, t)
                        mm.then_inc(k_.w_first[s] if t == 0 else k_.w_used[s] if t == NT - 1 else v_mm[s], 1)

            @block.scalar
            def _(act):
                with act.Fori(0, n_pairs) as i:
                    for s, t in steps_of_slot:
                        if t == 0:
                            act.wait_ge(stored[s], 32 * i)
                        if t in (0, NT - 1):
                            act.wait_ge((k_.w_first if t == 0 else k_.w_used)[s], p0 + i + 1)
                        else:
                            act.wait_ge(v_mm[s], (NT - 2) * i + t)
                        act.activation(st[s][0][:, t, :], k_.ps[t % 4][:, 0:WB], ACT.Copy).then_inc(hi[t % 4], 1)
                        if (s, t) == (0, 1):
                            k_.split_hi(act, 1, p0 + i)
                        if (s, t) == (0, NT - 1):
                            k_.split_hi(act, 0, p0 + i + 1)

            @block.vector
            def _(dve):
                with dve.Fori(0, n_pairs) as i:
                    for s, t in steps_of_slot:
                        dve.wait_ge(hi[t % 4], 4 * i + 2 * s + t // 4 + 1)
                        dve.tensor_tensor(st[s][1][:, t, :], k_.ps[t % 4][:, 0:WB],
                                          st[s][0][:, t, :].bitcast(F32), ALU.subtract).then_inc(lo[t % 4], 1)
                        if (s, t) == (0, 1):
                            k_.split_lo(dve, 1, p0 + i)
                        if (s, t) == (0, NT - 1):
                            k_.split_lo(dve, 0, p0 + i + 1)

    def merge_gates(self):
        nc, k_ = self.nc, self
        n_pairs = D // WB
        p0, self.pairs = self.pairs, self.pairs + n_pairs
        work = self.work()
        st = [[work.put(f"m_{s}{c}", [P, T]) for c in range(2)] for s in range(2)]
        f_raw = work.put("f_raw", [P, KD, NH])
        f_h = work.put("f_h", [P, KD, NH], F32R)
        f_l = work.put("f_l", [P, KD, NH], F32R)
        b_f = work.put("b_f", [NH, 1])
        f, e, w1, dw, eq, ones = (work.put(f"d_{n}", [NH, T]) for n in ("f", "e", "w1", "dw", "eq", "ones"))
        c_h, c_l, n_h, n_l = (work.put(f"d_{n}", [NH, T], F32R) for n in ("ch", "cl", "nh", "nl"))
        named = lambda what: [[self.sem(f"m_{what}{s}{c}") for c in range(2)] for s in range(2)]
        out, stored = named("out"), k_.sig_stored
        f_loaded, f_hi, f_lo, f_mm, sized, d_exp, one, d_ln, own, ones_set, c_hi, c_lo = (
            self.sem(f"d_{n}") for n in ("loaded", "hi", "lo", "mm", "sized", "exp", "one", "ln", "own", "ones",
                                         "c_hi", "c_lo"))
        rows_stored = k_.rows_stored
        both = [(s, c) for s in range(2) for c in range(2)]
        c_sum = dw
        PER = 10

        with nc.Block() as block:
            @block.sync
            def _(sp):
                for c in range(2):
                    sp.wait_ge(k_.v_stored[c], 16 * NH // 2)
                sp.dma_start(f_raw[:, :, :], k_.w_in.rearrange("(k p) n -> p k n", p=P)[:, :, FL:FL + NH])\
                    .then_inc(f_loaded, 16)
                sp.dma_start(b_f[:, :], k_.ins["b_forget"].rearrange("a h -> h a")).then_inc(f_loaded, 16)

                def store(i, s):
                    for c in range(2):
                        sp.wait_ge(out[s][c], i + 1)
                        sp.dma_start(k_.sig_d[s, 2 * i + c], st[s][c][:, :]).then_inc(stored[s][c], 16)
                with sp.Fori(0, n_pairs - 1) as i:
                    for s, col in enumerate((ML, MA)):
                        k_.load_block(sp, s, p0 + i + 1, k_.w_block(k_.w_in, col + WB + WB * i))
                        store(i, s)
                sp.wait_ge(ones_set, 1)
                for part, row in ((0, 0), (0, 1), (1, 2), (1, 3)):
                    sp.dma_start(k_.c_d[:, part, row, :], ones[:, :]).then_inc(rows_stored, 16)
                sp.wait_ge(c_hi, 2)
                sp.wait_ge(c_lo, 2)
                for part, row, src in ((0, 2, c_h), (0, 3, c_l), (1, 0, n_h), (1, 1, n_l)):
                    sp.dma_start(k_.c_d[:, part, row, :], src[:, :].bitcast(F32)).then_inc(rows_stored, 16)
                for s in range(2):
                    k_.load_block(sp, s, p0 + n_pairs, k_.w_block(k_.ins["w_lru_out"][0], WB * s))
                    store(n_pairs - 1, s)

            @block.gpsimd
            def _(pool):
                pool.wait_ge(f_loaded, 32)
                pool.memset(ones[:, :], 1.0).then_inc(ones_set, 1)

            @block.tensor
            def _(pe):
                def turn(i):
                    for s, c in both:
                        if c == 0:
                            pe.wait_ge(k_.w_lo[s], p0 + i + 1)
                        pe.wait_ge(out[s][c], i)
                        k_.product(pe, k_.ps[2 * s + c], s, c).then_inc((k_.w_first, k_.w_used)[c][s], 1)
                for s, c in both:
                    if c == 0:
                        pe.wait_ge(k_.w_lo[s], p0 + 1)
                    k_.product(pe, k_.ps[2 * s + c], s, c).then_inc((k_.w_first, k_.w_used)[c][s], 1)
                pe.wait_ge(f_lo, 1)
                pe.wait_ge(out[1][1], 1)
                for k in range(KD):
                    for w, u, first, last in ((f_h, k_.uh, k == 0, False), (f_h, k_.ul, False, False),
                                              (f_l, k_.uh, False, k == KD - 1)):
                        for h in range(2):
                            mm = pe.matmul(k_.ps[3][0:NH, h * HALF:(h + 1) * HALF], w[:, k, :],
                                           u[:, k, h * HALF:(h + 1) * HALF], start=first, stop=last)
                mm.then_inc(f_mm, 1)
                pe.wait_ge(sized, 2)
                with pe.Fori(1, n_pairs) as i:
                    turn(i)

            @block.scalar
            def _(act):
                k_.split_hi(act, 1, p0)
                act.wait_ge(f_loaded, 32)
                act.activation(f_h[:, :, :], f_raw[:, :, :], ACT.Copy).then_inc(f_hi, 1)

                def turn(i, last):
                    for s, c in both:
                        act.wait_ge((k_.w_first, k_.w_used)[c][s], p0 + i + 1)
                        if type(i) is not int or i > 0:
                            act.wait_ge(stored[s][c], 16 * i)
                        act.activation(st[s][c][:, :], k_.ps[2 * s + c][:, :], ACT.Sigmoid).then_inc(out[s][c], 1)
                        if c == 1 and not (last and s == 1):
                            k_.split_hi(act, s, p0 + i + 1)
                turn(0, False)
                act.wait_ge(sized, 3)
                act.activation(e[:, :], e[:, :], ACT.Exp, scale=-1.0).then_inc(d_exp, 1)
                act.wait_ge(one, 1)
                act.activation(eq[:, :], w1[:, :], ACT.Ln).then_inc(d_ln, 1)
                act.wait_ge(own, PER)
                act.activation(c_h[:, :], c_sum[:, :], ACT.Copy).then_inc(c_hi, 1)
                act.activation(n_h[:, :], c_sum[:, :], ACT.Copy, scale=-1.0).then_inc(c_hi, 1)
                with act.Fori(1, n_pairs - 1) as i:
                    turn(i, False)
                turn(n_pairs - 1, True)

            @block.vector
            def _(dve):
                steps = Steps(dve, own)
                k_.split_lo(dve, 1, p0)
                dve.wait_ge(f_hi, 1)
                dve.tensor_tensor(f_l[:, :, :], f_raw[:, :, :], f_h[:, :, :].bitcast(F32), ALU.subtract).then_inc(f_lo, 1)
                for s in range(2):
                    k_.split_lo(dve, s, p0 + 1)
                dve.wait_ge(f_mm, 1)
                dve.tensor_scalar(f[:, :], k_.ps[3][0:NH, :], b_f[:, :], None, ALU.add).then_inc(sized, 2)
                dve.wait_ge(sized, 2)
                dve.scalar_tensor_tensor(out=e[:, :], in0=f[:, :], scalar=-1.0, in1=f[:, :], op0=ALU.mult, op1=ALU.max)\
                    .then_inc(sized, 1)
                dve.wait_ge(sized, 3)
                steps.did(dve.tensor_scalar(f[:, :], f[:, :], 0.0, None, ALU.min))
                dve.wait_ge(d_exp, 1)
                dve.tensor_scalar(w1[:, :], e[:, :], 1.0, None, ALU.add).then_inc(one, 1)
                dve.wait_ge(one, 1)
                steps.did(dve.tensor_scalar(dw[:, :], w1[:, :], -1.0, None, ALU.add))
                dve.wait_ge(d_ln, 1)
                steps.did(dve.tensor_scalar(w1[:, :], dw[:, :], 0.0, None, ALU.is_equal))
                steps.did(dve.tensor_tensor(dw[:, :], dw[:, :], w1[:, :], ALU.add))
                steps.did(dve.reciprocal(dw[:, :], dw[:, :]))
                steps.did(dve.tensor_tensor(eq[:, :], eq[:, :], w1[:, :], ALU.add))
                steps.did(dve.tensor_tensor(eq[:, :], eq[:, :], dw[:, :], ALU.mult))
                steps.did(dve.tensor_tensor(eq[:, :], eq[:, :], e[:, :], ALU.mult))
                steps.did(dve.tensor_tensor(f[:, :], f[:, :], eq[:, :], ALU.subtract))
                dve.wait_ge(ones_set, 1)
                steps.did(dve.tensor_tensor_scan(c_sum[:, :], ones[:, :], f[:, :], 0.0, ALU.mult, ALU.add))
                assert steps.n == PER
                dve.wait_ge(c_hi, 2)
                dve.tensor_tensor(c_l[:, :], c_sum[:, :], c_h[:, :].bitcast(F32), ALU.subtract).then_inc(c_lo, 1)
                dve.tensor_tensor(n_l[:, :], c_h[:, :].bitcast(F32), c_sum[:, :], ALU.subtract).then_inc(c_lo, 1)
                with dve.Fori(1, n_pairs - 1) as i:
                    for s in range(2):
                        k_.split_lo(dve, s, p0 + i + 1)
                k_.split_lo(dve, 0, p0 + n_pairs)

    def branch_out(self, branch):
        nc, k_ = self.nc, self
        n_pairs = D // WB // 2
        p0, self.pairs = self.pairs, self.pairs + n_pairs
        weights = self.ins["w_lru_out" if branch == 0 else "w_attn_out"][0]
        following = self.ins["w_attn_out" if branch == 0 else "w_out"][0]
        work = self.work()
        if branch == 0:
            self.attention_inputs()
        tag = "lo" if branch == 0 else "ao"
        sg = [[work.put(f"{tag}_sg{s}{c}", [P, T]) for c in range(2)] for s in range(2)]
        stage = [work.put(f"{tag}_in{r}", [P, T]) for r in range(4)]
        named = lambda what: [[self.sem(f"{tag}_{what}{s}{c}") for c in range(2)] for s in range(2)]
        loaded, gated = named("loaded"), named("gated")
        in_loaded = [self.sem(f"{tag}_in{r}") for r in range(4)]
        in_hi, in_lo, own = (self.sem(f"{tag}_{n}") for n in ("hi", "split", "own"))
        both = [(s, c) for s in range(2) for c in range(2)]
        source = lambda k: k_.mix[:, k, :] if branch == 0 else stage[k % 4][:, :]

        with nc.Block() as block:
            @block.sync
            def _(sp):
                if branch == 0:
                    for s, c in both:
                        sp.wait_ge(k_.sig_stored[s][c], 16 * (D // WB))
                else:
                    for k in range(KD):
                        for g in range(2):
                            sp.wait_ge(k_.o_stored[g], 16 * (k + 1))
                        if k >= 4:
                            sp.wait_ge(in_lo, k - 3)
                        sp.dma_start(stage[k % 4][:, :], k_.o_d[k]).then_inc(in_loaded[k % 4], 16)

                def gates(i):
                    for s, c in both:
                        sp.wait_ge(gated[s][c], i)
                        sp.dma_start(sg[s][c][:, :], k_.sig_d[branch, 4 * i + 2 * s + c]).then_inc(loaded[s][c], 16)
                with sp.Fori(0, n_pairs - 1) as i:
                    gates(i)
                    for s in range(2):
                        k_.load_block(sp, s, p0 + i + 1, k_.w_block(weights, WB * (2 + s) + 2 * WB * i))
                gates(n_pairs - 1)
                if branch == 0:
                    for c in range(2):
                        sp.wait_ge(k_.qk_stored[c], 16 * NH)
                        sp.wait_ge(k_.v_stored[c], 16 * NH // 2)
                    sp.wait_ge(k_.rows_stored, 16 * 8)
                    for c in range(2):
                        if c == 0:
                            k_.load_head_qk(sp, 0, c)
                        k_.load_head_v(sp, 0, c)
                for s in range(2):
                    k_.load_block(sp, s, p0 + n_pairs, k_.w_block(following, WB * s))

            @block.tensor
            def _(pe):
                with pe.Fori(0, n_pairs) as i:
                    for s, c in both:
                        if c == 0:
                            pe.wait_ge(k_.w_lo[s], p0 + i + 1)
                        pe.wait_ge(gated[s][c], i)
                        k_.product(pe, k_.ps[2 * s + c], s, c, in_lo if (s, c) == (0, 0) else None).then_inc((k_.w_first, k_.w_used)[c][s], 1)

            @block.scalar
            def _(act):
                for k in range(KD):
                    if branch == 1:
                        act.wait_ge(in_loaded[k % 4], 16 * (k // 4 + 1))
                    act.activation(k_.uh[:, k, :], source(k), ACT.Copy).then_inc(in_hi, 1)
                with act.Fori(0, n_pairs) as i:
                    k_.split_hi(act, 1, p0 + i)
                    k_.split_hi(act, 0, p0 + i + 1)

            @block.vector
            def _(dve):
                for k in range(KD):
                    dve.wait_ge(in_hi, k + 1)
                    dve.tensor_tensor(k_.ul[:, k, :], source(k), k_.uh[:, k, :].bitcast(F32),
                                      ALU.subtract).then_inc(in_lo, 1)
                with dve.Fori(0, n_pairs) as i:
                    k_.split_lo(dve, 1, p0 + i)
                    for s, c in both:
                        dve.wait_ge((k_.w_first, k_.w_used)[c][s], p0 + i + 1)
                        dve.wait_ge(loaded[s][c], 16 * (i + 1))
                        mix = k_.mix[:, bass.ds(4 * i + 2 * s + c, 1), :].rearrange("p a t -> p (a t)")
                        if branch == 0:
                            dve.tensor_tensor(mix, k_.ps[2 * s + c][:, :], sg[s][c][:, :], ALU.mult)\
                                .then_inc(gated[s][c], 1)
                        else:
                            dve.tensor_tensor(sg[s][c][:, :], k_.ps[2 * s + c][:, :], sg[s][c][:, :], ALU.mult)\
                                .then_inc(own, 1)
                            dve.wait_ge(own, 4 * i + 2 * s + c + 1)
                            dve.tensor_tensor(mix, mix, sg[s][c][:, :], ALU.add).then_inc(gated[s][c], 1)
                        if (s, c) == (0, 1):
                            k_.split_lo(dve, 0, p0 + i + 1)

    def attention_inputs(self):
        work = self.work()
        at_qk1 = work.put("at_qk1", [P, 4, T], F32R)
        self.at_qk = [work.put("at_qk0", [P, 4, T], F32R), at_qk1]
        self.at_v = [work.put(f"at_v{c}", [P, 2, NT, HD], F32R) for c in range(2)]
        self.at_rows = [work.put(f"at_rows{c}", [4, 2, T], F32R) for c in range(2)]
        self.at_work = work

    def load_head_qk(self, eng, i, c):
        eng.dma_start(self.at_qk[c][:, :, :].bitcast(F32), self.qk_d[2 * i + c]).then_inc(self.qk_in[c], 16)
        eng.dma_start(self.at_rows[c][:, :, :].bitcast(F32), self.c_d[2 * i + c].rearrange("a r t -> r a t"))\
            .then_inc(self.c_in[c], 16)

    def load_head_v(self, eng, i, c):
        for part in range(2):
            eng.dma_start(self.at_v[c][:, part, :, :].bitcast(F32),
                          self.v_d[i, part, :, :, c * HD:(c + 1) * HD]).then_inc(self.v_in[c], 16)

    def attention(self):
        nc, k_ = self.nc, self
        upper = Map(nc, self.act_start, self.work_start - 4 * KD * T)
        qk, v, rows, work = k_.at_qk, k_.at_v, k_.at_rows, k_.at_work
        o_sb = [work.put(f"at_o{g}", [P, HALF]) for g in range(2)]
        mask = work.put("at_mask", [P, T])
        pt_h = [upper.put(f"at_pth{g}", [P, 4 + 4 * g, HALF], F32R) for g in range(2)]
        pt_l = [upper.put(f"at_ptl{g}", [P, 4 + 4 * g, HALF], F32R) for g in range(2)]
        SB = 4
        sb = [upper.put(f"at_s{b}", [P, T]) for b in range(SB)]
        small = work.put("at_small", [P, 2, 4])
        sem = self.sem
        qk_in, v_in, c_in, stored = k_.qk_in, k_.v_in, k_.c_in, k_.o_stored
        names = ("mask", "s_mm", "maxed", "negated", "exped", "inverted", "scaled", "t_mm", "hi", "lo", "pv_mm", "o_out")
        masks, s_mm, maxed, negated, exped, inverted, scaled, t_mm, hi, lo, pv_mm, o_out = (sem("at_" + n) for n in names)
        turns, tiles = NH // 2, 2 * NT
        parts = [(n, kb, min(4, n % NT + 1 - kb)) for n in range(tiles) for kb in range(0, n % NT + 1, 4)]
        of_tile = [[st for st, part in enumerate(parts) if part[0] == n] for n in range(tiles)]
        turned = lambda st: k_.ps[2][:, st % 2 * HALF:st % 2 * HALF + parts[st][2] * P]

        def piece(pt, st):
            n, kb, m = parts[st]
            return pt[n % NT // 4][:, kb:kb + m, n % 4 * P:n % 4 * P + P]

        def back(i, n, by):
            if n - by >= 0:
                return (i, n - by) if n - by < tiles else None
            return None if type(i) is int and i == 0 else (i - 1, n - by + tiles)

        def steps(engine, step):
            for n in range(tiles):
                step(0, n)
            with engine.Fori(1, turns) as i:
                for n in range(tiles):
                    step(i, n)
            for n in range(tiles, tiles + 5):
                step(turns - 1, n)

        def later(engine, semaphore, count):
            if type(count) is not int or count > 0:
                engine.wait_ge(semaphore, count)

        with nc.Block() as block:
            @block.sync
            def _(sp):
                def load_qk(i, c):
                    sp.wait_ge(s_mm, tiles * i - tiles + NT * (c + 1))
                    k_.load_head_qk(sp, i, c)

                def load_v(i, c):
                    sp.wait_ge(pv_mm, 4 * i - 2 + 2 * c)
                    k_.load_head_v(sp, i, c)

                def store(i, c):
                    for g in range(2):
                        sp.wait_ge(o_out, 4 * i + 2 * c + g + 1)
                        sp.dma_start(k_.o_d[2 * i + c][:, g * HALF:(g + 1) * HALF], o_sb[g][:, :]).then_inc(stored[g], 16)
                k_.load_head_qk(sp, 0, 1)
                with sp.Fori(0, turns - 1) as i:
                    for c in range(2):
                        load_qk(i + 1, c)
                        store(i, c)
                        load_v(i + 1, c)
                for c in range(2):
                    store(turns - 1, c)

            @block.gpsimd
            def _(pool):
                pool.memset(mask[:, :], 0.0).then_inc(masks, 1)
                pool.wait_ge(masks, 1)
                pool.affine_select(out=mask[:, T - P:T], in_=mask[:, T - P:T], compare_op=ALU.is_ge, fill=NEG, base=0,
                                   pattern=[[-1, P]], channel_multiplier=1).then_inc(masks, 1)

            @block.tensor
            def _(pe):
                def scores(i, n):
                    c, qb = n // NT, n % NT
                    keys = (qb + 1) * P
                    if qb == 0:
                        pe.wait_ge(qk_in[c], 16 * (i + 1))
                        pe.wait_ge(c_in[c], 16 * (i + 1))
                    later(pe, maxed, tiles * i + n - 1)
                    queries = slice(qb * P, (qb + 1) * P)
                    q_h, q_l = (qk[c][:, part, queries] for part in range(2))
                    for at in range(0, keys, HALF):
                        end = min(at + HALF, keys)
                        for q, part, first in ((q_h, 2, True), (q_h, 3, False), (q_l, 2, False)):
                            pe.matmul(k_.ps[n % 2][:, at:end], q, qk[c][:, part, at:end], start=first, stop=False)
                        mm = pe.matmul(k_.ps[n % 2][:, at:end], rows[c][:, 0, queries], rows[c][:, 1, at:end],
                                       start=False, stop=True)
                    mm.then_inc(s_mm, 1)

                def turn(i, n):
                    pe.wait_ge(scaled, tiles * i + n + 1)
                    for st in of_tile[n]:
                        _, kb, m = parts[st]
                        later(pe, lo, len(parts) * i + st - 1)
                        for j in range(m):
                            mm = pe.transpose(turned(st)[:, j * P:(j + 1) * P],
                                              sb[n % SB][:, (kb + j) * P:(kb + j + 1) * P], k_.ident[:, :])
                        mm.then_inc(t_mm, 1)

                def values(i, group):
                    c, g = group // 2, group % 2
                    if g == 0:
                        pe.wait_ge(v_in[c], 32 * (i + 1))
                    pe.wait_ge(lo, len(parts) * i + of_tile[4 * group + 3][-1] + 1)
                    later(pe, o_out, 4 * i + group - 1)
                    blocks = 4 * g + 4
                    for kb in range(blocks):
                        q0 = max(0, kb - 4 * g) * P
                        for part, pt, first, last in ((0, pt_h, kb == 0, False), (0, pt_l, False, False),
                                                      (1, pt_h, False, kb == blocks - 1)):
                            mm = pe.matmul(k_.ps[3][:, g * HALF + q0:(g + 1) * HALF], v[c][:, part, kb, :],
                                           pt[g][:, kb, q0:HALF], start=first, stop=last)
                    mm.then_inc(pv_mm, 1)

                def step(i, n):
                    if n < tiles:
                        scores(i, n)
                    if tile := back(i, n, 3):
                        turn(*tile)
                    if (tile := back(i, n, 5)) and tile[1] % 4 == 3:
                        values(tile[0], tile[1] // 4)
                steps(pe, step)

            @block.scalar
            def _(act):
                def high(i, n):
                    for st in of_tile[n]:
                        act.wait_ge(t_mm, len(parts) * i + st + 1)
                        later(act, pv_mm, 4 * i + n // 4 - 1)
                        act.activation(piece(pt_h, st), turned(st).rearrange("p (k q) -> p k q", q=P),
                                       ACT.Copy).then_inc(hi, 1)

                def exponent(i, n):
                    keys = (n % NT + 1) * P
                    act.wait_ge(negated, tiles * i + n + 1)
                    act.activation(sb[n % SB][:, 0:keys], sb[n % SB][:, 0:keys], ACT.Exp,
                                   bias=small[:, n % 2, 1:2], accum_out=small[:, n % 2, 2:3]).then_inc(exped, 1)

                def output(i, group):
                    c, g = group // 2, group % 2
                    act.wait_ge(pv_mm, 4 * i + group + 1)
                    later(act, stored[g], 16 * (2 * i + c))
                    act.activation(o_sb[g][:, :], k_.ps[3][:, g * HALF:(g + 1) * HALF], ACT.Copy).then_inc(o_out, 1)

                def step(i, n):
                    if tile := back(i, n, 2):
                        high(*tile)
                    if n < tiles:
                        exponent(i, n)
                    if (tile := back(i, n, 5)) and tile[1] % 4 == 3:
                        output(tile[0], tile[1] // 4)
                steps(act, step)

            @block.vector
            def _(dve):
                def scored(i, n):
                    if n < tiles:
                        dve.wait_ge(s_mm, tiles * i + n + 1)

                def low(i, n, step_):
                    for st in of_tile[n]:
                        dve.wait_ge(hi, len(parts) * i + st + 1)
                        if st == of_tile[n][-1]:
                            scored(*step_)
                        dve.tensor_tensor(piece(pt_l, st), turned(st).rearrange("p (k q) -> p k q", q=P),
                                          piece(pt_h, st).bitcast(F32), ALU.subtract).then_inc(lo, 1)

                def step(i, n):
                    if tile := back(i, n, 3):
                        low(*tile, (i, n))
                    else:
                        scored(i, n)
                    if n < tiles:
                        keys = (n % NT + 1) * P
                        dve.tensor_tensor_reduce(out=sb[n % SB][:, 0:keys], in0=k_.ps[n % 2][:, 0:keys],
                                                 in1=mask[:, T - keys:T], scale=1.0, scalar=NEG, op0=ALU.add,
                                                 op1=ALU.max, accum_out=small[:, n % 2, 0:1]).then_inc(maxed, 1)
                        dve.wait_ge(maxed, tiles * i + n + 1)
                        dve.tensor_scalar(small[:, n % 2, 1:2], small[:, n % 2, 0:1], -1.0, None, ALU.mult)\
                            .then_inc(negated, 1)
                    if tile := back(i, n, 1):
                        i_, m = tile
                        b, keys = m % 2, (m % NT + 1) * P
                        dve.wait_ge(exped, tiles * i_ + m + 1)
                        dve.reciprocal(small[:, b, 3:4], small[:, b, 2:3]).then_inc(inverted, 1)
                        dve.wait_ge(inverted, tiles * i_ + m + 1)
                        dve.tensor_scalar(sb[m % SB][:, 0:keys], sb[m % SB][:, 0:keys], small[:, b, 3:4], None,
                                          ALU.mult).then_inc(scaled, 1)
                dve.wait_ge(masks, 2)
                steps(dve, step)

    def project(self):
        nc, k_ = self.nc, self
        n_pairs = D // WB // 2
        p0, self.pairs = self.pairs, self.pairs + n_pairs
        work = self.work()
        self.x2 = work.put("x2", [P, NT, D])
        self.x2_total = work.put("x2_total", [P, NT])
        self.x2_end = work.at
        square = work.put("pr_square", [P, D])
        squared = self.sem("pr_squared")
        x_in = [self.sem(f"pr_x{t}") for t in range(NT)]
        in_hi, in_lo = self.sem("pr_hi"), self.sem("pr_split")
        mm_done = [self.sem(f"pr_mm{s}") for s in range(2)]
        added = [self.sem(f"pr_add{t}") for t in range(4)]
        weights = self.ins["w_out"][0]

        with nc.Block() as block:
            @block.sync
            def _(sp):
                for t in range(NT):
                    sp.dma_start(k_.x2[:, t, :], k_.x[t * P:(t + 1) * P, :]).then_inc(x_in[t], 16)
                for s in range(2):
                    k_.load_block(sp, s, p0 + 1, k_.w_block(weights, WB * (2 + s)))

            @block.tensor
            def _(pe):
                with pe.Fori(0, n_pairs) as i:
                    for s in range(2):
                        for t in range(NT):
                            if t == 0:
                                pe.wait_ge(k_.w_lo[s], p0 + i + 1)
                            pe.wait_ge(added[t % 4], 4 * i + 2 * s + t // 4)
                            mm = k_.product_rows(pe, k_.ps[t % 4][:, 0:WB], s, t, in_lo if (s, t) == (0, 0) else None)
                            mm.then_inc(k_.w_first[s] if t == 0 else k_.w_used[s] if t == NT - 1 else mm_done[s], 1)

            @block.scalar
            def _(act):
                for k in range(KD):
                    act.activation(k_.uh[:, k, :], k_.mix[:, k, :], ACT.Copy).then_inc(in_hi, 1)
                k_.split_hi(act, 1, p0)
                for s in range(2):
                    k_.split_hi(act, s, p0 + 1)
                for t in range(NT):
                    act.wait_ge(added[t % 4], 4 * n_pairs - 1 + t // 4)
                    act.activation(square[:, :], k_.x2[:, t, :], ACT.Square, accum_out=k_.x2_total[:, t:t + 1])\
                        .then_inc(squared, 1)
                    act.wait_ge(squared, t + 1)

            @block.vector
            def _(dve):
                for k in range(KD):
                    dve.wait_ge(in_hi, k + 1)
                    dve.tensor_tensor(k_.ul[:, k, :], k_.mix[:, k, :], k_.uh[:, k, :].bitcast(F32),
                                      ALU.subtract).then_inc(in_lo, 1)
                for t in range(NT):
                    dve.wait_ge(x_in[t], 16)

                def turn(i, last):
                    for s in range(2):
                        for t in range(NT):
                            if t in (0, NT - 1):
                                dve.wait_ge((k_.w_first if t == 0 else k_.w_used)[s], p0 + i + 1)
                            else:
                                dve.wait_ge(mm_done[s], (NT - 2) * i + t)
                            part = k_.x2[:, t, bass.ds(WB * (2 * i + s), WB)]
                            dve.tensor_tensor(part, part, k_.ps[t % 4][:, 0:WB], ALU.add).then_inc(added[t % 4], 1)
                            if (s, t) == (0, 1):
                                k_.split_lo(dve, 1, p0 + i)
                        if s == 0 and not last:
                            k_.split_lo(dve, 0, p0 + i + 1)
                turn(0, False)
                turn(1, True)

    def route(self):
        nc, k_, ins = self.nc, self, self.ins
        low = Map(nc, self.fixed_end, self.work_start)
        self.e_raw = [low.put(f"e_raw{r}", [P, 4, HALF]) for r in range(RAW)]
        self.e_l = [Map(nc, self.fixed_end + r * 16 * HALF, self.high).put(f"e_l{r}", [P, 4, HALF], F32R)
                    for r in range(RAW)]
        high = Map(nc, self.x2_end, self.high)
        self.e_h = [high.put(f"e_h{r}", [P, 4, HALF], F32R) for r in range(SPLIT)]
        self.split_end = high.at
        self.raw_end = low.at
        work = Map(nc, self.raw_end, self.work_start)
        put, sem = work.put, self.sem
        NL = NG + NE
        g_b, b_r, w_r = put("rt_g", [P, D]), put("rt_b", [P, NL]), put("rt_w", [P, KD, NL])
        xn = [high.put(f"rt_xn{b}", [P, D]) for b in range(2)]
        over_xt = Map(nc, high.at, self.high)
        xt = high.put("rt_xt", [P, KD, 2 * P])
        number, slot_no = put("rt_number", [P, NT]), put("rt_slot_no", [P, BLK])
        at_expert = [put(f"rt_ate{s}", [P, NT, NE]) for s in range(2)]
        at_rank = [over_xt.put(f"rt_atr{s}", [P, NT, BLK]) for s in range(2)]
        ranked, slots_mm, listed = sem("rt_ranked"), sem("rt_slots"), sem("rt_listed")
        by_expert = put("rt_by_expert", [NL, T])
        zeros = put("rt_zeros", [BLK, NE + MAXX + 1], I32)
        mean, rstd, power = (put(f"rt_{n}", [P, NT]) for n in ("mean", "rstd", "power"))
        logits = put("rt_logits", [P, NT, NL])
        i_exp, e_base = put("rt_iexp", [P, NT, NE]), put("rt_ebase", [P, NT, NE])
        i_grp, grp, g_eq = (put(f"rt_{n}", [P, NT, NG]) for n in ("igrp", "grp", "geq"))
        m_exp, eq, oh1, oh2, prod = (put(f"rt_{n}", [P, NT, NE]) for n in ("mexp", "eq", "oh1", "oh2", "prod"))
        gmax, gsum, m1, m2, sel, ex, inv, dst = (
            put(f"rt_{n}", [P, NT]) for n in ("gmax", "gsum", "m1", "m2", "sel", "ex", "inv", "dst"))
        tok = put("rt_tok", [P, NT], I32)
        NX = MAXX
        cnt, extra, ends, shift = (put(f"rt_{n}", [P, NE]) for n in ("cnt", "extra", "ends", "shift"))
        limit, over = put("rt_limit", [P, NE, MOST - 1]), put("rt_over", [P, NE, MOST - 1])
        before_t = put("rt_before_t", [P, NT + 1, NE])
        jj, before, which = put("rt_jj", [1, NX, NE]), put("rt_before", [1, NX, NE]), put("rt_which", [1, NX])

        in_sem, zeroed, filled, consts = sem("rt_in"), sem("rt_zeroed"), sem("rt_filled"), sem("rt_consts")
        averaged, powered, scaled, stored = (
            sem(f"rt_{n}") for n in ("averaged", "powered", "scaled", "stored0"))
        stored = [stored, sem("rt_stored1")]
        turned, copied, logit_mm, logit_copied, logit_turned, logit_out = (
            sem(f"rt_{n}") for n in ("turned", "copied", "mm", "mm_copied", "mm_turned", "logit"))
        own, to_exp, exped, chosen, rank_mm, dest_out, scattered = (
            sem(f"rt_{n}") for n in ("own", "to_exp", "exped", "chosen", "rank", "dest", "scattered"))
        tiles = NT // 2

        with nc.Block() as block:
            @block.sync
            def _(sp):
                sp.dma_start(g_b[:, :], ins["g_ffn"][0].partition_broadcast(P)).then_inc(in_sem, 16)
                sp.dma_start(b_r[:, 0:NG], ins["b_route_group"][0].partition_broadcast(P)).then_inc(in_sem, 16)
                sp.dma_start(b_r[:, NG:NL], ins["b_route_expert"][0].partition_broadcast(P)).then_inc(in_sem, 16)
                rows = lambda w: w[0].rearrange("(k p) n -> p k n", p=P)
                sp.dma_start(w_r[:, :, 0:NG], rows(ins["w_route_group"])).then_inc(in_sem, 16)
                sp.dma_start(w_r[:, :, NG:NL], rows(ins["w_route_expert"])).then_inc(in_sem, 16)
                sp.wait_ge(zeroed, 1)
                sp.dma_start(k_.slots_d.rearrange("(p n) a -> p (n a)", p=BLK), zeros[:, :]).then_inc(filled, 16)
                def first_pieces(ms):
                    for m in ms:
                        k_.load_piece(sp, (0, 0, m), ("gate", "up", "gate")[m // 2], m % 2, m // 4, True)
                first_pieces(range(2))
                with sp.Fori(0, tiles) as i:
                    for b in range(2):
                        sp.wait_ge(scaled, 2 * i + b + 1)
                        sp.dma_start(k_.xn_d[bass.ds((2 * i + b) * P, P), :], xn[b][:, :]).then_inc(stored[b], 16)
                first_pieces(range(2, 6))
                for m, kind, half, e in k_.loads_of(0):
                    k_.load_piece(sp, (0, 0, m), kind, half, e, True)
                for b in range(2):
                    sp.wait_ge(stored[b], 16 * tiles)

            @block.gpsimd
            def _(pool):
                pool.memset(power[:, :], -0.5).then_inc(consts, 1)
                pool.wait_ge(averaged, 1)
                pool.wait_ge(consts, 1)
                pool.tensor_tensor(rstd[:, :], mean[:, :], power[:, :], ALU.pow).then_inc(powered, 1)
                pool.memset(zeros[:, :], 0).then_inc(zeroed, 1)
                iota = lambda out, pattern, base, step: pool.iota(
                    out, pattern, base=base, channel_multiplier=step,
                    allow_small_or_imprecise_dtypes=True).then_inc(consts, 1)
                iota(i_grp[:, :, :], [[0, NT], [1, NG]], 100, 0)
                iota(i_exp[:, :, :], [[0, NT], [1, NE]], 100, 0)
                iota(e_base[:, :, :], [[0, NT], [BLK, NE]], 0, 0)
                iota(limit[:, :, :], [[0, NE], [BLK, MOST - 1]], BLK, 0)
                iota(jj[:, :, :], [[1, NX], [0, NE]], 0, 0)
                iota(tok[:, :], [[P, NT]], 0, 1)
                pool.memset(before_t[:, 0, :], 0.0).then_inc(consts, 1)
                iota(number[:, :], [[P, NT]], 0, 1)
                iota(slot_no[:, :], [[1, BLK]], 0, 0)
                pool.wait_ge(consts, 10)
                pool.wait_ge(filled, 16)
                pool.wait_ge(dest_out, 2)
                pool.wait_ge(listed, 1)
                n = pool.value_load(k_.blocks[0:1, MAXX:MAXX + 1], min_val=0, max_val=MAXX)
                with pool.If(0 < n):
                    for s in range(2):
                        for t in range(NT):
                            pool.indirect_dma_start(
                                out=k_.slots_d, out_offset=bass.IndirectOffsetOnAxis(ap=k_.dest[:, s, t:t + 1], axis=0),
                                in_=tok[:, t:t + 1], in_offset=None).then_inc(scattered, 16)
                    pool.wait_ge(scattered, 16 * 2 * NT)

            @block.tensor
            def _(pe):
                pe.wait_ge(in_sem, 16 * 5)

                with pe.Fori(0, tiles) as i:
                    for b in range(2):
                        pe.wait_ge(scaled, 2 * i + b + 1)
                        pe.wait_ge(copied, 2 * i)
                        for k in range(KD):
                            mm = pe.transpose(k_.ps[b][:, k * P:(k + 1) * P], xn[b][:, k * P:(k + 1) * P], k_.ident[:, :])
                        mm.then_inc(turned, 1)
                    pe.wait_ge(copied, 2 * i + 2)
                    for k in range(KD):
                        mm = pe.matmul(k_.ps[2][0:NL, bass.ds(2 * P * i, 2 * P)], w_r[:, k, :], xt[:, k, :],
                                       start=(k == 0), stop=(k == KD - 1))
                    mm.then_inc(logit_mm, 1)
                pe.wait_ge(logit_copied, 1)
                for t in range(NT):
                    mm = pe.transpose(k_.ps[3][:, t * NL:(t + 1) * NL], by_expert[:, t * P:(t + 1) * P],
                                      k_.ident[0:NL, 0:NL])
                mm.then_inc(logit_turned, 1)
                pe.wait_ge(chosen, 1)
                pe.matmul(k_.ps[0][:, 0:NT * NE], k_.stri[:, :], prod[:, :, :].rearrange("p t e -> p (t e)"),
                          start=True, stop=False)
                pe.matmul(k_.ps[0][:, 0:NT * NE], k_.ones[:, :], before_t[:, 0:NT, :].rearrange("p t e -> p (t e)"),
                          start=False, stop=True)
                mm = pe.matmul(k_.ps[0][:, NT * NE:(NT + 1) * NE], k_.ones[:, :], before_t[:, NT, :],
                               start=True, stop=True)
                mm.then_inc(rank_mm, 1)
                for s in range(2):
                    pe.wait_ge(ranked, s + 1)
                    for t in range(NT):
                        mm = pe.matmul(k_.ps[1][0:BLK, 0:NE], at_rank[s][:, t, :], at_expert[s][:, t, :],
                                       start=(s, t) == (0, 0), stop=(s, t) == (1, NT - 1))
                mm.then_inc(slots_mm, 1)

            @block.scalar
            def _(act):
                with act.Fori(0, tiles) as i:
                    for b in range(2):
                        act.wait_ge(turned, 2 * i + b + 1)
                        act.wait_ge(logit_mm, i)
                        act.activation(xt[:, :, b * P:(b + 1) * P], k_.ps[b][:, :].rearrange("p (k t) -> p k t", t=P),
                                       ACT.Copy).then_inc(copied, 1)
                act.wait_ge(logit_mm, tiles)
                act.activation(by_expert[:, :], k_.ps[2][0:NL, :], ACT.Copy).then_inc(logit_copied, 1)
                act.wait_ge(to_exp, 1)
                act.activation(grp[:, :, :], grp[:, :, :], ACT.Exp).then_inc(exped, 1)
                act.wait_ge(to_exp, 2)
                act.activation(ex[:, :], ex[:, :], ACT.Exp).then_inc(exped, 1)
                for m in range(SPLIT):
                    k_.piece_hi(act, (0, 0, m))

            @block.vector
            def _(dve):
                dve.tensor_scalar(mean[:, :], k_.x2_total[:, :], 1.0 / D, EPS, ALU.mult, ALU.add).then_inc(averaged, 1)
                dve.wait_ge(powered, 1)
                dve.wait_ge(in_sem, 16 * 5)
                with dve.Fori(0, tiles) as i:
                    for b in range(2):
                        t = 2 * i + b
                        dve.wait_ge(stored[b], 16 * i)
                        dve.wait_ge(turned, 2 * i)
                        dve.scalar_tensor_tensor(out=xn[b][:, :], in0=k_.x2[:, bass.ds(t, 1), :].rearrange("p a n -> p (a n)"),
                                                 scalar=rstd[:, bass.ds(t, 1)], in1=g_b[:, :], op0=ALU.mult,
                                                 op1=ALU.mult).then_inc(scaled, 1)
                dve.wait_ge(logit_turned, 1)
                dve.tensor_tensor(logits[:, :, :], k_.ps[3][:, 0:NT * NL].rearrange("p (t n) -> p t n", n=NL),
                                  b_r[:, :].unsqueeze(1).to_broadcast([P, NT, NL]), ALU.add).then_inc(logit_out, 1)
                dve.wait_ge(logit_out, 1)
                dve.wait_ge(consts, 10)
                steps = Steps(dve, own)
                did = steps.did
                tt = lambda out, a, b, op: did(dve.tensor_tensor(out, a, b, op))
                over_last = lambda v, n: v.unsqueeze(2).to_broadcast([P, NT, n])
                gl, el = logits[:, :, 0:NG], logits[:, :, NG:NL]

                def first_match(values, top, numbers, scratch, chosen_one, n):
                    tt(scratch, values, over_last(top, n), ALU.is_equal)
                    did(dve.scalar_tensor_tensor(out=scratch, in0=scratch, scalar=-100.0, in1=numbers,
                                                 op0=ALU.mult, op1=ALU.add))
                    did(dve.tensor_reduce(sel[:, :], scratch, AX.X, ALU.min))
                    did(dve.tensor_scalar(sel[:, :], sel[:, :], 100.0, None, ALU.add))
                    tt(chosen_one, numbers, over_last(sel[:, :], n), ALU.is_equal)

                did(dve.tensor_reduce(gmax[:, :], gl, AX.X, ALU.max))
                dve.tensor_tensor(grp[:, :, :], gl, over_last(gmax[:, :], NG), ALU.subtract).then_inc(to_exp, 1)
                dve.wait_ge(exped, 1)
                did(dve.tensor_reduce(gsum[:, :], grp[:, :, :], AX.X, ALU.add))
                did(dve.reciprocal(gsum[:, :], gsum[:, :]))
                first_match(gl, gmax[:, :], i_grp[:, :, :], g_eq[:, :, :], grp[:, :, :], NG)
                in_group = grp[:, :, :].unsqueeze(3).to_broadcast([P, NT, NG, EG])
                by_group = lambda v: v.rearrange("p t (g e) -> p t g e", g=NG)
                tt(by_group(m_exp[:, :, :]), by_group(el), in_group, ALU.mult)
                did(dve.tensor_scalar(g_eq[:, :, :], grp[:, :, :], -NEG, NEG, ALU.mult, ALU.add))
                tt(by_group(m_exp[:, :, :]), by_group(m_exp[:, :, :]),
                   g_eq[:, :, :].unsqueeze(3).to_broadcast([P, NT, NG, EG]), ALU.add)
                did(dve.tensor_reduce(m1[:, :], m_exp[:, :, :], AX.X, ALU.max))
                first_match(m_exp[:, :, :], m1[:, :], i_exp[:, :, :], eq[:, :, :], oh1[:, :, :], NE)
                did(dve.scalar_tensor_tensor(out=m_exp[:, :, :], in0=oh1[:, :, :], scalar=NEG, in1=m_exp[:, :, :],
                                             op0=ALU.mult, op1=ALU.add))
                did(dve.tensor_reduce(m2[:, :], m_exp[:, :, :], AX.X, ALU.max))
                dve.tensor_tensor(ex[:, :], m2[:, :], m1[:, :], ALU.subtract).then_inc(to_exp, 1)
                first_match(m_exp[:, :, :], m2[:, :], i_exp[:, :, :], eq[:, :, :], oh2[:, :, :], NE)
                tt(prod[:, :, :], oh1[:, :, :], oh2[:, :, :], ALU.add)
                for t in range(NT):
                    op = dve.tensor_tensor(before_t[:, t + 1, :], before_t[:, t, :], prod[:, t, :], ALU.add)
                    if t < NT - 1:
                        did(op)
                op.then_inc(chosen, 1)
                for s, oh in enumerate((oh1, oh2)):
                    tt(at_expert[s][:, :, :], oh[:, :, :], over_last(number[:, :], NE), ALU.mult)
                dve.wait_ge(exped, 2)
                did(dve.tensor_scalar(inv[:, :], ex[:, :], 1.0, None, ALU.add))
                did(dve.reciprocal(inv[:, :], inv[:, :]))
                tt(k_.wgt[:, 0, :], inv[:, :], gsum[:, :], ALU.mult)
                tt(k_.wgt[:, 1, :], k_.wgt[:, 0, :], ex[:, :], ALU.mult)
                dve.wait_ge(rank_mm, 1)
                rank = k_.ps[0][:, 0:NT * NE].rearrange("p (t e) -> p t e", e=NE)
                for s, oh in enumerate((oh1, oh2)):
                    tt(eq[:, :, :], oh[:, :, :], rank, ALU.mult)
                    did(dve.tensor_reduce(dst[:, :], eq[:, :, :], AX.X, ALU.add))
                    dve.tensor_tensor(at_rank[s][:, :, :], slot_no[:, :].unsqueeze(1).to_broadcast([P, NT, BLK]),
                                      over_last(dst[:, :], BLK), ALU.is_equal).then_inc(ranked, 1)
                dve.wait_ge(ranked, 2)
                did(dve.tensor_copy(cnt[:, :], k_.ps[0][:, NT * NE:(NT + 1) * NE]))
                tt(over[:, :, :], cnt[:, :].unsqueeze(2).to_broadcast([P, NE, MOST - 1]), limit[:, :, :], ALU.is_gt)
                did(dve.tensor_reduce(extra[:, :], over[:, :, :], AX.X, ALU.add))
                did(dve.tensor_tensor_scan(ends[:, :], k_.ones[:, 0:NE], extra[:, :], 0.0, ALU.mult, ALU.add))
                tt(shift[:, :], ends[:, :], extra[:, :], ALU.subtract)
                did(dve.tensor_scalar(shift[:, :], shift[:, :], float(BLK), float(BLK * (NE - 1)), ALU.mult, ALU.add))
                tt(shift[:, :], shift[:, :], e_base[:, 0, :], ALU.subtract)
                did(dve.tensor_scalar(eq[:, :, :], rank, float(BLK), None, ALU.is_ge))
                tt(eq[:, :, :], eq[:, :, :], shift[:, :].unsqueeze(1).to_broadcast([P, NT, NE]), ALU.mult)
                tt(e_base[:, :, :], e_base[:, :, :], rank, ALU.add)
                tt(e_base[:, :, :], e_base[:, :, :], eq[:, :, :], ALU.add)
                for s, oh in enumerate((oh1, oh2)):
                    tt(oh[:, :, :], oh[:, :, :], e_base[:, :, :], ALU.mult)
                    did(dve.tensor_reduce(dst[:, :], oh[:, :, :], AX.X, ALU.add))
                    dve.tensor_copy(k_.dest[:, s, :], dst[:, :]).then_inc(dest_out, 1)
                tt(before[:, :, :], ends[0:1, :].unsqueeze(1).to_broadcast([1, NX, NE]), jj[:, :, :], ALU.is_le)
                did(dve.tensor_reduce(which[:, :], before[:, :, :], AX.X, ALU.add))
                did(dve.tensor_scalar(which[:, :], which[:, :], float(NE - 1), None, ALU.min))
                did(dve.tensor_copy(k_.blocks[:, 0:NX], which[:, :]))
                dve.tensor_copy(k_.blocks[:, NX:NX + 1], ends[0:1, NE - 1:NE]).then_inc(listed, 1)
                dve.wait_ge(slots_mm, 1)
                did(dve.tensor_copy(k_.slots_i[0:BLK, :], k_.ps[1][0:BLK, 0:NE]))

    def raw_slot(self, piece):
        j, b, m = piece
        return (6 * b + m) % RAW, j // 2 + (6 * b + m) // RAW

    def loads_of(self, j):
        rest = ((6, "down", 0, j), (7, "down", 1, j), (8, "up", 0, j + 1), (9, "up", 1, j + 1),
                (10, "gate", 0, j + 2), (11, "gate", 1, j + 2))
        return rest if type(j) is not int or j < NE - 2 else rest[:4]

    def load_piece(self, eng, piece, kind, half, e, first=False):
        j, b, m = piece
        if not first:
            eng.wait_ge(self.e_used[m % SPLIT], 2 * j + m // SPLIT + 1 - RAW // SPLIT)
        w = self.ins["w_exp_" + kind][0][e].rearrange("(k p) n -> p k n", p=P)
        src = w[:, :, half * HALF:(half + 1) * HALF] if kind == "down" else w[:, 4 * half:4 * half + 4, :]
        slot, _ = self.raw_slot(piece)
        eng.dma_start(self.e_raw[slot][:, :, :], src).then_inc(self.e_in[slot], 16)

    def piece_hi(self, act, piece):
        j, b, m = piece
        slot, before = self.raw_slot(piece)
        act.wait_ge(self.e_in[slot], 16 * (before + 1))
        used = 2 * j + m // SPLIT
        if type(used) is not int or used > 0:
            act.wait_ge(self.e_used[m % SPLIT], used)
        act.activation(self.e_h[m % SPLIT][:, :, :], self.e_raw[slot][:, :, :], ACT.Copy).then_inc(self.e_hi[m % SPLIT], 1)

    def piece_lo(self, dve, piece):
        j, b, m = piece
        slot, _ = self.raw_slot(piece)
        dve.wait_ge(self.e_hi[m % SPLIT], 2 * j + m // SPLIT + 1)
        dve.tensor_tensor(self.e_l[slot][:, :, :], self.e_raw[slot][:, :, :],
                          self.e_h[m % SPLIT][:, :, :].bitcast(F32), ALU.subtract).then_inc(self.e_lo[m % SPLIT], 1)

    def piece_done(self, eng, piece):
        j, b, m = piece
        eng.wait_ge(self.e_used[m % SPLIT], 2 * j + m // SPLIT + 1)

    def piece_products(self, pe, ps, rows_h, rows_l, piece, first_piece, last_piece):
        j, b, m = piece
        slot, _ = self.raw_slot(piece)
        pe.wait_ge(self.e_lo[m % SPLIT], 2 * j + m // SPLIT + 1)
        w_h, w_l = self.e_h[m % SPLIT], self.e_l[slot]
        for k in range(4):
            for x, w, first, last in ((rows_h, w_h, k == 0, False), (rows_h, w_l, False, False),
                                      (rows_l, w_h, False, k == 3)):
                mm = pe.matmul(ps, x[:, k, :], w[:, k, :], start=first and first_piece, stop=last and last_piece)
        mm.then_inc(self.e_used[m % SPLIT], 1)

    def experts(self):
        nc, k_ = self.nc, self
        work, high = Map(nc, self.raw_end, self.work_start), Map(nc, self.split_end, self.high)
        xg = [high.put(f"e_xg{b}", [BLK, D]) for b in range(2)]
        xt_h = [work.put(f"e_xth{b}", [P, KD, BLK], F32R) for b in range(2)]
        xt_l = [work.put(f"e_xtl{b}", [P, KD, BLK], F32R) for b in range(2)]
        silu = work.put("e_silu", [BLK, FE])
        hid = work.put("e_hid", [BLK, FE])
        y_sb = [high.put(f"e_y{b}", [BLK, D]) for b in range(2)]
        ht_h = high.put("e_hth", [P, 4, BLK], F32R)
        ht_l = high.put("e_htl", [P, 4, BLK], F32R)
        idx = [high.put(f"e_idx{b}", [BLK, 1], I32) for b in range(2)]
        sem = self.sem
        idx_in, gathered, y_stored = ([sem(f"e_{n}{b}") for b in range(2)] for n in ("idx", "gathered", "stored"))
        x_mm, x_hi, x_lo, silu_out, hid_out, h_mm, h_hi, h_lo, y_out = (
            sem("e_" + n) for n in ("x_mm", "x_hi", "x_lo", "silu", "hid", "h_mm", "h_hi", "h_lo", "y_out"))
        by_chunk = lambda ps: ps.rearrange("p (k t) -> p k t", t=P)[:, :, 0:BLK]
        ps_x, ps_h = by_chunk(k_.ps[0][:, :]), by_chunk(k_.ps[2][:, 0:HALF])
        ps_g, ps_u, ps_y = k_.ps[1][0:BLK, 0:HALF], k_.ps[1][0:BLK, HALF:2 * HALF], k_.ps[3][0:BLK, :]
        ident = k_.ident[0:BLK, 0:BLK]
        n_over = MAXX

        def gather(pool, j, b, slots, t=None):
            if type(j) is not int or j >= 2:
                pool.wait_ge(x_mm, j - 1)
            if t is not None:
                pool.wait_ge(gathered[1 - b], 16 * ((j + 1) // 2))
                pool.wait_ge(idx_in[b], 16 * (t // 2 + 1))
                load_slots(pool, j + 1, 1 - b)
                slots = idx[b][:, 0:1]
            pool.indirect_dma_start(out=xg[b][:, :], out_offset=None, in_=k_.xn_d,
                                    in_offset=bass.IndirectOffsetOnAxis(ap=slots, axis=0)).then_inc(gathered[b], 16)

        def load_slots(pool, j, b):
            pool.dma_start(idx[b][:, :], k_.slots_d[bass.ds(BLK * j, BLK), :]).then_inc(idx_in[b], 16)

        def turn_x(pe, j, b):
            pe.wait_ge(gathered[b], 16 * (j // 2 + 1))
            pe.wait_ge(x_lo, j)
            for k in range(KD):
                mm = pe.transpose(ps_x[:, k, :], xg[b][:, k * P:(k + 1) * P], ident)
            mm.then_inc(x_mm, 1)

        def gate(pe, j, b, half, piece):
            if half == 0:
                pe.wait_ge(x_lo, j + 1)
                pe.wait_ge(silu_out, j)
            ks = slice(4 * half, 4 * half + 4)
            k_.piece_products(pe, ps_g, xt_h[b][:, ks, :], xt_l[b][:, ks, :], piece, half == 0, half == 1)

        def up(pe, j, b, half, piece):
            if half == 0:
                pe.wait_ge(hid_out, j)
            ks = slice(4 * half, 4 * half + 4)
            k_.piece_products(pe, ps_u, xt_h[b][:, ks, :], xt_l[b][:, ks, :], piece, half == 0, half == 1)

        def turn_h(pe, j):
            pe.wait_ge(hid_out, j + 1)
            pe.wait_ge(h_lo, j)
            for k in range(4):
                mm = pe.transpose(ps_h[:, k, :], hid[:, k * P:(k + 1) * P], ident)
            mm.then_inc(h_mm, 1)

        def down(pe, j, half, piece):
            if half == 0:
                pe.wait_ge(h_lo, j + 1)
                pe.wait_ge(y_out, j)
            k_.piece_products(pe, ps_y[:, half * HALF:(half + 1) * HALF], ht_h, ht_l, piece, True, True)

        def x_high(act, j, b, used):
            act.wait_ge(x_mm, j + 1)
            if used is not None:
                k_.piece_done(act, used)
            act.activation(xt_h[b][:, :, :], ps_x, ACT.Copy).then_inc(x_hi, 1)

        def x_low(dve, j, b):
            dve.wait_ge(x_hi, j + 1)
            dve.tensor_tensor(xt_l[b][:, :, :], ps_x, xt_h[b][:, :, :].bitcast(F32), ALU.subtract).then_inc(x_lo, 1)

        def act_silu(act, j, gate_piece):
            k_.piece_done(act, gate_piece)
            act.wait_ge(hid_out, j)
            act.activation(silu[:, :], ps_g, ACT.Silu).then_inc(silu_out, 1)

        def hidden(dve, j, up_piece):
            dve.wait_ge(silu_out, j + 1)
            k_.piece_done(dve, up_piece)
            dve.wait_ge(h_mm, j)
            dve.tensor_tensor(hid[:, :], silu[:, :], ps_u, ALU.mult).then_inc(hid_out, 1)

        def h_high(act, j, last_down):
            act.wait_ge(h_mm, j + 1)
            if last_down is not None:
                k_.piece_done(act, last_down)
            act.activation(ht_h[:, :, :], ps_h, ACT.Copy).then_inc(h_hi, 1)

        def h_low(dve, j):
            dve.wait_ge(h_hi, j + 1)
            dve.tensor_tensor(ht_l[:, :, :], ps_h, ht_h[:, :, :].bitcast(F32), ALU.subtract).then_inc(h_lo, 1)

        def rows_out(act, j, b, down_piece):
            k_.piece_done(act, down_piece)
            act.wait_ge(y_stored[b], 16 * (j // 2))
            act.activation(y_sb[b][:, :], ps_y[:, :], ACT.Copy).then_inc(y_out, 1)
            act.wait_ge(y_out, j + 1)
            act.dma_start(k_.y_d[bass.ds(BLK * j, BLK), :], y_sb[b][:, :]).then_inc(y_stored[b], 16)

        def in_pairs(engine, body, from_pair, to_pair):
            with engine.Fori(from_pair, to_pair) as i:
                for b in range(2):
                    body(2 * i + b, b)

        def beyond(engine, body):
            n = engine.value_load(k_.blocks[0:1, n_over:n_over + 1], min_val=0, max_val=MAXX)
            with engine.If(0 < n):
                with engine.Fori(0, MAXX // 2) as i:
                    for b in range(2):
                        with engine.If(2 * i + b < n):
                            body(NE + 2 * i + b, b, 2 * i + b)
            return n

        listed = lambda engine, at, most: engine.value_load(k_.blocks[0:1, bass.ds(at, 1)], min_val=0, max_val=most)

        with nc.Block() as block:
            @block.sync
            def _(sp):
                def body(j, b):
                    for m, kind, half, e in k_.loads_of(j):
                        k_.load_piece(sp, (j, b, m), kind, half, e)
                body(1, 1)
                in_pairs(sp, body, 1, NE // 2 - 1)
                body(NE - 2, 0)
                for m in (4, 5):
                    k_.load_piece(sp, (NE - 1, 1, m), "down", m - 4, NE - 1)

                def other(j, b, t):
                    e = listed(sp, t, NE - 1)
                    for m in range(6):
                        k_.load_piece(sp, (j, b, m), ("gate", "up", "down")[m // 2], m % 2, e)
                beyond(sp, other)

            @block.gpsimd
            def _(pool):
                for j in range(NE):
                    gather(pool, j, j % 2, k_.slots_i[0:BLK, j:j + 1])
                load_slots(pool, NE, 0)
                n = beyond(pool, lambda j, b, t: gather(pool, j, b, None, t))
                pool.wait_ge(y_stored[0], 16 * (NE // 2 + (n + 1) // 2))
                pool.wait_ge(y_stored[1], 16 * (NE // 2 + n // 2))
                pool.wait_ge(idx_in[0], 16 * (n // 2 + 1))
                pool.wait_ge(idx_in[1], 16 * ((n + 1) // 2))

            @block.tensor
            def _(pe):
                turn_x(pe, 0, 0)
                for h in range(2):
                    gate(pe, 0, 0, h, (0, 0, h))

                def body(j, b):
                    turn_x(pe, j + 1, 1 - b)
                    up(pe, j, b, 0, (j, b, 2))
                    up(pe, j, b, 1, (j, b, 3))
                    gate(pe, j + 1, 1 - b, 0, (j, b, 4))
                    turn_h(pe, j)
                    gate(pe, j + 1, 1 - b, 1, (j, b, 5))
                    for h in range(2):
                        down(pe, j, h, (j, b, 6 + h))
                in_pairs(pe, body, 0, NE // 2 - 1)
                body(NE - 2, 0)
                j, b = NE - 1, 1
                for h in range(2):
                    up(pe, j, 1, h, (j, b, 2 + h))
                turn_h(pe, j)
                for h in range(2):
                    down(pe, j, h, (j, b, 4 + h))

                def other(j, b, t):
                    turn_x(pe, j, b)
                    for h in range(2):
                        gate(pe, j, b, h, (j, b, h))
                    for h in range(2):
                        up(pe, j, b, h, (j, b, 2 + h))
                    turn_h(pe, j)
                    for h in range(2):
                        down(pe, j, h, (j, b, 4 + h))
                beyond(pe, other)

            @block.scalar
            def _(act):
                x_high(act, 0, 0, None)
                k_.piece_hi(act, (0, 0, SPLIT))

                def body(j, b, first=False):
                    k_.piece_hi(act, (j, b, 4))
                    act_silu(act, j, (j, b, -1) if not first else (0, 0, 1))
                    x_high(act, j + 1, 1 - b, (j, b, -3) if not first else None)
                    for m in (5, 6):
                        k_.piece_hi(act, (j, b, m))
                    h_high(act, j, (j, b, 1) if not first else None)
                    for m in (7, 8, 9):
                        k_.piece_hi(act, (j, b, m))
                    rows_out(act, j, b, (j, b, 7))
                body(0, 0, True)
                body(1, 1)
                in_pairs(act, body, 1, NE // 2 - 1)
                body(NE - 2, 0)
                j, b = NE - 1, 1
                act_silu(act, j, (j, b, -1))
                for m in (4, 5):
                    k_.piece_hi(act, (j, b, m))
                h_high(act, j, (j, b, 1))
                rows_out(act, j, 1, (j, b, 5))

                def other(j, b, t):
                    k_.piece_hi(act, (j, b, 0))
                    x_high(act, j, b, (j, b, -3))
                    for m in (1, 2, 3):
                        k_.piece_hi(act, (j, b, m))
                    act_silu(act, j, (j, b, 1))
                    for m in (4, 5):
                        k_.piece_hi(act, (j, b, m))
                    h_high(act, j, (j, b, -1))
                    rows_out(act, j, b, (j, b, 5))
                beyond(act, other)

            @block.vector
            def _(dve):
                for m in range(2):
                    k_.piece_lo(dve, (0, 0, m))
                x_low(dve, 0, 0)
                for m in (2, 3):
                    k_.piece_lo(dve, (0, 0, m))

                def body(j, b):
                    k_.piece_lo(dve, (j, b, 4))
                    x_low(dve, j + 1, 1 - b)
                    k_.piece_lo(dve, (j, b, 5))
                    hidden(dve, j, (j, b, 3))
                    k_.piece_lo(dve, (j, b, 6))
                    h_low(dve, j)
                    for m in (7, 8, 9):
                        k_.piece_lo(dve, (j, b, m))
                in_pairs(dve, body, 0, NE // 2 - 1)
                body(NE - 2, 0)
                j, b = NE - 1, 1
                k_.piece_lo(dve, (j, b, 4))
                hidden(dve, j, (j, b, 3))
                k_.piece_lo(dve, (j, b, 5))
                h_low(dve, j)

                def other(j, b, t):
                    k_.piece_lo(dve, (j, b, 0))
                    x_low(dve, j, b)
                    for m in (1, 2, 3, 4):
                        k_.piece_lo(dve, (j, b, m))
                    hidden(dve, j, (j, b, 3))
                    k_.piece_lo(dve, (j, b, 5))
                    h_low(dve, j)
                beyond(dve, other)

    def combine(self):
        nc, k_ = self.nc, self
        work = Map(nc, self.fixed_end, self.work_start)
        RING = 4
        yg = [[work.put(f"cb_y{r}{s}", [P, D]) for s in range(2)] for r in range(RING)]
        ob = [work.put(f"cb_o{b}", [P, D]) for b in range(2)]
        g_b, square = work.put("cb_g", [P, D]), work.put("cb_square", [P, D])
        total, mean, rstd, power = (work.put(f"cb_{n}", [P, NT]) for n in ("total", "mean", "rstd", "power"))
        sem = self.sem
        got = [[sem(f"cb_got{r}{s}") for s in range(2)] for r in range(RING)]
        g_in, const, first, added, squared, averaged, powered, normed = (
            sem("cb_" + n) for n in ("g", "const", "first", "added", "squared", "averaged", "powered", "normed"))
        stored = [sem(f"cb_stored{b}") for b in range(2)]

        with nc.Block() as block:
            @block.gpsimd
            def _(pool):
                pool.memset(power[:, :], -0.5).then_inc(const, 1)
                pool.wait_ge(const, 1)

                def root(t):
                    pool.wait_ge(averaged, t + 1)
                    pool.tensor_tensor(rstd[:, t:t + 1], mean[:, t:t + 1], power[:, t:t + 1], ALU.pow).then_inc(powered, 1)
                for t in range(NT):
                    if t >= RING:
                        pool.wait_ge(added, t - RING + 1)
                    for s in range(2):
                        pool.indirect_dma_start(
                            out=yg[t % RING][s][:, :], out_offset=None, in_=k_.y_d,
                            in_offset=bass.IndirectOffsetOnAxis(ap=k_.dest[:, s, t:t + 1], axis=0))\
                            .then_inc(got[t % RING][s], 16)
                    if t >= RING - 1:
                        root(t - RING + 1)
                for t in range(NT - RING + 1, NT):
                    root(t)

            @block.sync
            def _(sp):
                sp.dma_start(g_b[:, :], k_.ins["g_final"].partition_broadcast(P)).then_inc(g_in, 16)
                for t in range(NT):
                    sp.wait_ge(normed, t + 1)
                    sp.dma_start(k_.out[t * P:(t + 1) * P, :], ob[t % 2][:, :]).then_inc(stored[t % 2], 16)
                for b in range(2):
                    sp.wait_ge(stored[b], 16 * NT // 2)

            @block.scalar
            def _(act):
                for t in range(NT):
                    act.wait_ge(added, t + 1)
                    act.activation(square[:, :], k_.x2[:, t, :], ACT.Square, accum_out=total[:, t:t + 1]).then_inc(squared, 1)
                    act.wait_ge(squared, t + 1)

            @block.vector
            def _(dve):
                def averages(t):
                    dve.wait_ge(squared, t + 1)
                    dve.tensor_scalar(mean[:, t:t + 1], total[:, t:t + 1], 1.0 / D, EPS, ALU.mult, ALU.add)\
                        .then_inc(averaged, 1)

                def norm(t):
                    dve.wait_ge(powered, t + 1)
                    if t >= 2:
                        dve.wait_ge(stored[t % 2], 16 * (t // 2))
                    dve.scalar_tensor_tensor(out=ob[t % 2][:, :], in0=k_.x2[:, t, :], scalar=rstd[:, t:t + 1],
                                             in1=g_b[:, :], op0=ALU.mult, op1=ALU.mult).then_inc(normed, 1)
                dve.wait_ge(g_in, 16)
                for t in range(NT):
                    x2 = k_.x2[:, t, :]
                    for s in range(2):
                        dve.wait_ge(got[t % RING][s], 16 * (t // RING + 1))
                        dve.scalar_tensor_tensor(out=x2, in0=yg[t % RING][s][:, :], scalar=k_.wgt[:, s, t:t + 1], in1=x2,
                                                 op0=ALU.mult, op1=ALU.add).then_inc((first, added)[s], 1)
                        if s == 0:
                            dve.wait_ge(first, t + 1)
                    if t >= 1:
                        averages(t - 1)
                    if t >= 2:
                        norm(t - 2)
                averages(NT - 1)
                for t in (NT - 2, NT - 1):
                    norm(t)

    def write(self):
        for write, *args in ((self.norm_in,), (self.lru_qk,), (self.value,), (self.merge_gates,),
                             (self.branch_out, 0), (self.attention,), (self.branch_out, 1), (self.project,),
                             (self.route,), (self.experts,), (self.combine,)):
            self.stage(write, *args)


NAMES = ("x", "g_mix", "w_in", "conv_w", "conv_b", "w_rg_a", "b_rg_a", "w_rg_x", "b_rg_x", "lru_lambda", "b_forget",
         "w_lru_out", "w_attn_out", "w_out", "g_ffn", "w_route_group", "b_route_group", "w_route_expert",
         "b_route_expert", "w_exp_gate", "w_exp_up", "w_exp_down", "g_final")


def kernel(**inputs):
    import numpy as np
    import concourse.bacc as bacc
    from concourse.bass_utils import run_bass_kernel_spmd

    nc = bacc.Bacc("TRN2", target_bir_lowering=False, num_devices=1)
    arrays = {name: np.ascontiguousarray(inputs[name]) for name in NAMES}
    ins = {name: nc.dram_tensor(name, a.shape, mybir.dt.from_np(a.dtype), kind="ExternalInput").ap()
           for name, a in arrays.items()}
    out = nc.dram_tensor("out", (T, D), F32, kind="ExternalOutput").ap()
    Kernel(nc, ins, out).write()
    result = run_bass_kernel_spmd(nc, [arrays], core_ids=[0])
    return result.results[0]["out"].reshape(1, T, D)
```
